# Optimizing a Trainium2 kernel written in Bass

```python
import math
import jax, jax.numpy as jnp
from jax import lax
import numpy as np

D_MODEL = 1024
BATCH = 1
SEQ = 512
DEPTH = 1

CHUNK = 64
Q_BLOCK = 128
HEAD_DIM = 64
H_FOX = 8
H_CHK = 8
W_FOX = H_FOX * HEAD_DIM
W_CHK = H_CHK * HEAD_DIM
LEFT_CHUNKS = 8
MAX_REL = 128
N_REL = 2 * MAX_REL + 1
N_BRANCH = 2
D_FF = 4 * D_MODEL
EPS = 1e-6
NEG = -1e30
N_IN = 3 * W_FOX + H_FOX + 3 * W_CHK + N_BRANCH * D_MODEL
SPLITS = tuple(np.cumsum([W_FOX, W_FOX, W_FOX, H_FOX, W_CHK, W_CHK, W_CHK]).tolist())


def rms_norm(x, g):
    xf = x.astype(jnp.float32)
    y = xf * lax.rsqrt(jnp.mean(xf * xf, axis=-1, keepdims=True) + EPS)
    return (y * g.astype(jnp.float32)).astype(x.dtype)

def to_heads(t, h):
    b, s, _ = t.shape
    return t.reshape(b, s, h, HEAD_DIM).transpose(0, 2, 1, 3)

def from_heads(t):
    b, h, s, d = t.shape
    return t.transpose(0, 2, 1, 3).reshape(b, s, h * d)

def forgetting_attention(q, k, v, log_f):
    b, h, s, d = q.shape
    nblk = s // Q_BLOCK
    scale = 1.0 / math.sqrt(d)
    c = jnp.cumsum(log_f, axis=-1)
    qb = q.reshape(b, h, nblk, Q_BLOCK, d).transpose(2, 0, 1, 3, 4)
    cb = c.reshape(b, h, nblk, Q_BLOCK).transpose(2, 0, 1, 3)
    key_pos = jnp.arange(s, dtype=jnp.int32)

    def block(args):
        qi, ci, i = args
        sc = jnp.einsum('bhqd,bhkd->bhqk', qi, k, preferred_element_type=jnp.float32)
        sc = sc * scale + ci[..., None] - c[:, :, None, :]
        tq = i * Q_BLOCK + jnp.arange(Q_BLOCK, dtype=jnp.int32)
        mask = key_pos[None, :] <= tq[:, None]
        sc = jnp.where(mask, sc, NEG)
        p = jax.nn.softmax(sc, axis=-1).astype(v.dtype)
        return jnp.einsum('bhqk,bhkd->bhqd', p, v)

    out = lax.map(block, (qb, cb, jnp.arange(nblk, dtype=jnp.int32)))
    return out.transpose(1, 2, 0, 3, 4).reshape(b, h, s, d)

def chunk_band_attention(q, k, v, rel_bias):
    b, h, s, d = q.shape
    nblk = s // Q_BLOCK
    scale = 1.0 / math.sqrt(d)
    pad = LEFT_CHUNKS * CHUNK
    band = pad + Q_BLOCK
    kp = jnp.pad(k, ((0, 0), (0, 0), (pad, 0), (0, 0)))
    vp = jnp.pad(v, ((0, 0), (0, 0), (pad, 0), (0, 0)))
    qb = q.reshape(b, h, nblk, Q_BLOCK, d).transpose(2, 0, 1, 3, 4)

    def block(args):
        qi, i = args
        p0 = i * Q_BLOCK
        kb = lax.dynamic_slice_in_dim(kp, p0, band, axis=2)
        vb = lax.dynamic_slice_in_dim(vp, p0, band, axis=2)
        tq = p0 + jnp.arange(Q_BLOCK, dtype=jnp.int32)
        sk = p0 - pad + jnp.arange(band, dtype=jnp.int32)
        cq = tq // CHUNK
        ck = sk // CHUNK
        valid = (sk[None, :] >= 0) & (ck[None, :] <= cq[:, None]) & (ck[None, :] >= cq[:, None] - LEFT_CHUNKS)
        rel = jnp.clip(tq[:, None] - sk[None, :], -MAX_REL, MAX_REL) + MAX_REL
        bias = rel_bias[:, rel].astype(jnp.float32)
        sc = jnp.einsum('bhqd,bhkd->bhqk', qi, kb, preferred_element_type=jnp.float32)
        sc = jnp.where(valid, sc * scale + bias[None], NEG)
        p = jax.nn.softmax(sc, axis=-1).astype(vb.dtype)
        return jnp.einsum('bhqk,bhkd->bhqd', p, vb)

    out = lax.map(block, (qb, jnp.arange(nblk, dtype=jnp.int32)))
    return out.transpose(1, 2, 0, 3, 4).reshape(b, h, s, d)

def first_inputs(seed: int = 0) -> dict:
    key = jax.random.key(seed)
    ks = jax.random.split(key, 14)
    nrm = lambda k, shape, fan_in: jax.random.normal(k, shape, jnp.float32) * (fan_in ** -0.5)
    x = jax.random.normal(ks[0], (BATCH, SEQ, D_MODEL), jnp.float32)
    norm1 = 1.0 + 0.02 * jax.random.normal(ks[1], (DEPTH, D_MODEL), jnp.float32)
    w_in = nrm(ks[2], (DEPTH, D_MODEL, N_IN), D_MODEL)
    forget_bias = jnp.linspace(1.0, 6.0, H_FOX, dtype=jnp.float32)[None, :] + 0.1 * jax.random.normal(ks[3], (DEPTH, H_FOX), jnp.float32)
    rel_bias = 0.5 * jax.random.normal(ks[4], (DEPTH, H_CHK, N_REL), jnp.float32)
    w_branch_a = nrm(ks[5], (DEPTH, W_FOX, D_MODEL), W_FOX)
    w_branch_b = nrm(ks[6], (DEPTH, W_CHK, D_MODEL), W_CHK)
    w_out = nrm(ks[7], (DEPTH, D_MODEL, D_MODEL), D_MODEL)
    norm2 = 1.0 + 0.02 * jax.random.normal(ks[8], (DEPTH, D_MODEL), jnp.float32)
    w_up = nrm(ks[9], (DEPTH, D_MODEL, D_FF), D_MODEL)
    w_down = nrm(ks[10], (DEPTH, D_FF, D_MODEL), D_FF)
    final_norm = 1.0 + 0.02 * jax.random.normal(ks[11], (D_MODEL,), jnp.float32)
    return {"x": x, "norm1": norm1, "w_in": w_in, "forget_bias": forget_bias,
            "rel_bias": rel_bias, "w_branch_a": w_branch_a, "w_branch_b": w_branch_b,
            "w_out": w_out, "norm2": norm2, "w_up": w_up, "w_down": w_down,
            "final_norm": final_norm}

def first_block(x, norm1, w_in, forget_bias, rel_bias, w_branch_a, w_branch_b,
              w_out, norm2, w_up, w_down, final_norm):
    for l in range(DEPTH):
        h = rms_norm(x, norm1[l])
        proj = h @ w_in[l]
        qa, ka, va, fa, qc, kc, vc, gates = jnp.split(proj, SPLITS, axis=-1)
        log_f = jax.nn.log_sigmoid((fa + forget_bias[l]).astype(jnp.float32))
        log_f = log_f.transpose(0, 2, 1)
        o_a = from_heads(forgetting_attention(to_heads(qa, H_FOX), to_heads(ka, H_FOX),
                                              to_heads(va, H_FOX), log_f))
        o_b = from_heads(chunk_band_attention(to_heads(qc, H_CHK), to_heads(kc, H_CHK),
                                              to_heads(vc, H_CHK), rel_bias[l]))
        g_a, g_b = jnp.split(jax.nn.sigmoid(gates), N_BRANCH, axis=-1)
        merged = g_a * (o_a @ w_branch_a[l]) + g_b * (o_b @ w_branch_b[l])
        x = x + merged @ w_out[l]
        h2 = rms_norm(x, norm2[l])
        x = x + jnp.square(jax.nn.relu(h2 @ w_up[l])) @ w_down[l]
    return rms_norm(x, final_norm)


DEPTH_2 = 2

N_EVEN = (DEPTH_2 + 1) // 2
N_ODD = DEPTH_2 // 2
DN_ALPHA = (2.0 * DEPTH_2) ** 0.25
DN_BETA = (8.0 * DEPTH_2) ** -0.25
LN_EPS = 1e-5
RMS_EPS = 1e-6

GLA_HEADS = 4
GLA_DK = 64
GLA_DV = 128
GLA_GATE_RANK = 16
GLA_TAU = 16.0
GLA_QK = GLA_HEADS * GLA_DK
GLA_V = GLA_HEADS * GLA_DV
GLA_SPLITS = (GLA_QK, GLA_QK, GLA_V, GLA_V, GLA_GATE_RANK)
GLA_IN = sum(GLA_SPLITS)
GLA_OFFSETS = tuple(int(o) for o in np.cumsum(GLA_SPLITS)[:-1])

RW_HEADS = 8
RW_N = 64
RW_W = RW_HEADS * RW_N
RW_DECAY_RANK = 64
RW_A_RANK = 64
RW_GATE_RANK = 160
RW_GN_EPS = 64e-5
RW_SPLITS = (RW_W, RW_W, RW_W, RW_DECAY_RANK, RW_A_RANK, RW_GATE_RANK)
RW_IN = sum(RW_SPLITS)
RW_OFFSETS = tuple(int(o) for o in np.cumsum(RW_SPLITS)[:-1])

EVEN_IN = GLA_IN + RW_IN
EVEN_MIX = GLA_V + RW_W

MLA_HEADS = 16
MLA_NOPE = 64
MLA_ROPE = 32
MLA_V = 64
MLA_Q_RANK = 768
MLA_KV_RANK = 256
ODD_IN = MLA_Q_RANK + MLA_KV_RANK + MLA_ROPE
MLA_MIX = MLA_HEADS * MLA_V
ROPE_THETA = 10000.0

FFN_HIDDEN = math.ceil(8 * D_MODEL / 3 / 256) * 256


def layer_norm(x, g, b):
    xf = x.astype(jnp.float32)
    mu = xf.mean(-1, keepdims=True)
    var = jnp.square(xf - mu).mean(-1, keepdims=True)
    return ((xf - mu) * lax.rsqrt(var + LN_EPS) * g + b).astype(x.dtype)

def rms_norm_2(x, g):
    xf = x.astype(jnp.float32)
    return (xf * lax.rsqrt(jnp.mean(xf * xf, -1, keepdims=True) + RMS_EPS) * g).astype(x.dtype)

def token_shift(t):
    return jnp.pad(t[:, :-1], ((0, 0), (1, 0), (0, 0)))

def gla_chunked(q, k, v, log_a):
    B, S, H, DK = q.shape
    DV = v.shape[-1]
    n = S // CHUNK

    def to_chunks(t):
        return t.astype(jnp.float32).reshape(B, n, CHUNK, H, t.shape[-1]).transpose(1, 0, 3, 2, 4)

    qc, kc, vc, gc = to_chunks(q), to_chunks(k), to_chunks(v), to_chunks(log_a)
    causal = jnp.tril(jnp.ones((CHUNK, CHUNK), bool))[None, None, :, :, None]

    def step(state, inp):
        qi, ki, vi, gi = inp
        b = jnp.cumsum(gi, axis=2)
        o_inter = jnp.einsum('bhck,bhkv->bhcv', qi * jnp.exp(b), state)
        rel = jnp.where(causal, b[:, :, :, None, :] - b[:, :, None, :, :], -jnp.inf)
        attn = jnp.einsum('bhik,bhjk,bhijk->bhij', qi, ki, jnp.exp(rel))
        o_intra = jnp.einsum('bhij,bhjv->bhiv', attn, vi)
        b_last = b[:, :, -1:, :]
        new_state = (jnp.exp(b_last[:, :, 0, :])[..., None] * state
                     + jnp.einsum('bhck,bhcv->bhkv', ki * jnp.exp(b_last - b), vi))
        return new_state, o_inter + o_intra

    s0 = jnp.zeros((B, H, DK, DV), jnp.float32)
    _, o = lax.scan(step, s0, (qc, kc, vc, gc))
    return o.transpose(1, 0, 3, 2, 4).reshape(B, S, H, DV)

def rwkv7_scan(r, w, k, v, a_vec, b_vec):
    B, S, H, N = r.shape

    def tm(t):
        return t.astype(jnp.float32).transpose(1, 0, 2, 3)

    def step(state, inp):
        rt, wt, kt, vt, at, bt = inp
        sa = jnp.einsum('bhvk,bhk->bhv', state, at)
        state = state * wt[:, :, None, :] + sa[..., None] * bt[:, :, None, :] + vt[..., None] * kt[:, :, None, :]
        return state, jnp.einsum('bhvk,bhk->bhv', state, rt)

    s0 = jnp.zeros((B, H, N, N), jnp.float32)
    _, y = lax.scan(step, s0, (tm(r), tm(w), tm(k), tm(v), tm(a_vec), tm(b_vec)))
    return y.transpose(1, 0, 2, 3)

def even_mixer(x, w_in, gla_gate_w2, gla_gate_b, gla_norm_g, rw_mu, rw_w0, rw_w2, rw_a0, rw_a2,
               rw_g2, rw_k_k, rw_k_a, rw_r_k, rw_ln_g, rw_ln_b, w_out):
    B, S, _ = x.shape
    p = x @ w_in
    p_gla, p_rw = p[..., :GLA_IN], p[..., GLA_IN:]

    def heads(t, d):
        return t.reshape(B, S, -1, d)

    gq, gk, gv, gg, glr = jnp.split(p_gla, GLA_OFFSETS, axis=-1)
    log_a = jax.nn.log_sigmoid((glr @ gla_gate_w2 + gla_gate_b).astype(jnp.float32)) / GLA_TAU
    o_a = gla_chunked(heads(gq, GLA_DK) * GLA_DK ** -0.5, heads(gk, GLA_DK),
                      heads(gv, GLA_DV), heads(log_a, GLA_DK))
    o_a = (rms_norm_2(o_a, gla_norm_g) * jax.nn.silu(heads(gg, GLA_DV).astype(jnp.float32)))
    o_a = o_a.reshape(B, S, GLA_V).astype(x.dtype)

    p_rw = p_rw + rw_mu * (token_shift(p_rw) - p_rw)
    r, k, v, wl, al, gl = jnp.split(p_rw, RW_OFFSETS, axis=-1)
    w = -jax.nn.softplus(-(rw_w0 + jnp.tanh(wl) @ rw_w2)) - 0.5
    decay = jnp.exp(-jnp.exp(w.astype(jnp.float32)))
    a = jax.nn.sigmoid(rw_a0 + al @ rw_a2)
    g = jax.nn.sigmoid(gl) @ rw_g2
    kk = heads(k * rw_k_k, RW_N).astype(jnp.float32)
    kk = kk * lax.rsqrt(jnp.maximum(jnp.sum(kk * kk, -1, keepdims=True), 1e-24))
    k = k * (1 + (a - 1) * rw_k_a)
    r_h, k_h, v_h, a_h = heads(r, RW_N), heads(k, RW_N), heads(v, RW_N), heads(a, RW_N)
    y = rwkv7_scan(r_h, heads(decay, RW_N), k_h, v_h, -kk, kk * a_h)
    mu = y.mean(-1, keepdims=True)
    var = jnp.square(y - mu).mean(-1, keepdims=True)
    y = ((y - mu) * lax.rsqrt(var + RW_GN_EPS)).reshape(B, S, RW_W) * rw_ln_g + rw_ln_b
    bonus = jnp.sum(r_h * k_h * rw_r_k, -1, keepdims=True) * v_h
    o_b = ((heads(y, RW_N) + bonus).reshape(B, S, RW_W) * g).astype(x.dtype)

    return jnp.concatenate([o_a, o_b], axis=-1) @ w_out

def apply_rope(t, cos, sin):
    t2 = t.astype(jnp.float32).reshape(t.shape[:-1] + (-1, 2))
    x1, x2 = t2[..., 0], t2[..., 1]
    out = jnp.stack([x1 * cos - x2 * sin, x1 * sin + x2 * cos], axis=-1)
    return out.reshape(t.shape).astype(t.dtype)

def block_causal_mla_attention(q_nope, q_pe, k_nope, k_pe, v):
    B, S, H, _ = q_nope.shape
    scale = (MLA_NOPE + MLA_ROPE) ** -0.5
    key_chunk = jnp.arange(S) // CHUNK

    def block(i):
        start = i * Q_BLOCK
        qn = lax.dynamic_slice_in_dim(q_nope, start, Q_BLOCK, axis=1)
        qp = lax.dynamic_slice_in_dim(q_pe, start, Q_BLOCK, axis=1)
        s = (jnp.einsum('bqhd,bkhd->bhqk', qn, k_nope)
             + jnp.einsum('bqhr,bkr->bhqk', qp, k_pe)).astype(jnp.float32) * scale
        q_chunk = (start + jnp.arange(Q_BLOCK)) // CHUNK
        s = jnp.where(key_chunk[None, :] <= q_chunk[:, None], s, -jnp.inf)
        pr = jax.nn.softmax(s, axis=-1).astype(v.dtype)
        return jnp.einsum('bhqk,bkhd->bqhd', pr, v)

    o = lax.map(block, jnp.arange(S // Q_BLOCK))
    return o.transpose(1, 0, 2, 3, 4).reshape(B, S, H, MLA_V)

def odd_mixer(x, positions, w_in, q_norm_g, w_q_b, kv_norm_g, w_kv_b, w_out):
    B, S, _ = x.shape
    p = x @ w_in
    cq = p[..., :MLA_Q_RANK]
    ckv = p[..., MLA_Q_RANK:MLA_Q_RANK + MLA_KV_RANK]
    k_pe = p[..., MLA_Q_RANK + MLA_KV_RANK:]
    q = (rms_norm_2(cq, q_norm_g) @ w_q_b).reshape(B, S, MLA_HEADS, MLA_NOPE + MLA_ROPE)
    kv = (rms_norm_2(ckv, kv_norm_g) @ w_kv_b).reshape(B, S, MLA_HEADS, MLA_NOPE + MLA_V)
    q_nope, q_pe = q[..., :MLA_NOPE], q[..., MLA_NOPE:]
    k_nope, v = kv[..., :MLA_NOPE], kv[..., MLA_NOPE:]
    inv_freq = ROPE_THETA ** (-jnp.arange(0, MLA_ROPE, 2, dtype=jnp.float32) / MLA_ROPE)
    ang = positions.astype(jnp.float32)[..., None] * inv_freq
    cos, sin = jnp.cos(ang), jnp.sin(ang)
    q_pe = apply_rope(q_pe, cos[:, :, None, :], sin[:, :, None, :])
    k_pe = apply_rope(k_pe, cos, sin)
    o = block_causal_mla_attention(q_nope, q_pe, k_nope, k_pe, v)
    return o.reshape(B, S, MLA_MIX) @ w_out

def swiglu_ffn(x, w_gate_up, w_down):
    gu = x @ w_gate_up
    gate, up = gu[..., :FFN_HIDDEN], gu[..., FFN_HIDDEN:]
    return (jax.nn.silu(gate) * up) @ w_down

def second_inputs(seed: int = 0) -> dict:
    key = jax.random.key(seed)
    ks = iter(jax.random.split(key, 64))

    def dense(lead, fan_in, fan_out, scale=1.0):
        return jax.random.normal(next(ks), lead + (fan_in, fan_out), jnp.float32) * (scale * fan_in ** -0.5)

    def vec(shape, base, noise):
        return base + noise * jax.random.normal(next(ks), shape, jnp.float32)

    E, O = (N_EVEN,), (N_ODD,)
    x = jax.random.normal(next(ks), (BATCH, SEQ, D_MODEL), jnp.float32)
    positions = (jax.random.randint(next(ks), (BATCH, 1), 0, 4096, jnp.int32)
                 + jnp.arange(SEQ, dtype=jnp.int32)[None, :])

    even_scales = (1.0, 1.0, DN_BETA, 1.0, 1.0) + (1.0, 1.0, DN_BETA, 1.0, 1.0, 1.0)
    even_w_in = jnp.concatenate([dense(E, D_MODEL, c, s) for c, s in zip(GLA_SPLITS + RW_SPLITS, even_scales)], -1)

    mla_w_kv_b = jnp.concatenate([
        dense(O, MLA_KV_RANK, MLA_NOPE, 1.0).reshape(O + (MLA_KV_RANK, 1, MLA_NOPE)) * jnp.ones((1, MLA_HEADS, 1)),
        dense(O, MLA_KV_RANK, MLA_HEADS * MLA_V, DN_BETA).reshape(O + (MLA_KV_RANK, MLA_HEADS, MLA_V)),
    ], -1)
    mla_w_kv_b = mla_w_kv_b + 0.3 * dense(O, MLA_KV_RANK, MLA_HEADS * (MLA_NOPE + MLA_V)).reshape(mla_w_kv_b.shape) * jnp.concatenate([jnp.ones((MLA_NOPE,)), jnp.zeros((MLA_V,))])

    return {
        "x": x,
        "positions": positions,
        "even_w_in": even_w_in,
        "gla_gate_w2": dense(E, GLA_GATE_RANK, GLA_QK),
        "gla_gate_b": vec(E + (GLA_QK,), 0.0, 0.1),
        "gla_norm_g": vec(E + (GLA_DV,), 1.0, 0.02),
        "rwkv_mu": jax.random.uniform(next(ks), E + (RW_IN,), jnp.float32),
        "rwkv_w0": vec(E + (RW_W,), 0.0, 0.5),
        "rwkv_w2": dense(E, RW_DECAY_RANK, RW_W),
        "rwkv_a0": vec(E + (RW_W,), 0.0, 0.1),
        "rwkv_a2": dense(E, RW_A_RANK, RW_W),
        "rwkv_g2": dense(E, RW_GATE_RANK, RW_W),
        "rwkv_k_k": vec(E + (RW_W,), 0.85, 0.02),
        "rwkv_k_a": vec(E + (RW_W,), 1.0, 0.02),
        "rwkv_r_k": vec(E + (RW_HEADS, RW_N), 0.0, 0.1),
        "rwkv_ln_g": vec(E + (RW_W,), 1.0, 0.02),
        "rwkv_ln_b": vec(E + (RW_W,), 0.0, 0.02),
        "even_w_out": dense(E, EVEN_MIX, D_MODEL, DN_BETA),
        "mla_w_in": dense(O, D_MODEL, ODD_IN),
        "mla_q_norm_g": vec(O + (MLA_Q_RANK,), 1.0, 0.02),
        "mla_w_q_b": dense(O, MLA_Q_RANK, MLA_HEADS * (MLA_NOPE + MLA_ROPE)),
        "mla_kv_norm_g": vec(O + (MLA_KV_RANK,), 1.0, 0.02),
        "mla_w_kv_b": mla_w_kv_b.reshape(O + (MLA_KV_RANK, MLA_HEADS * (MLA_NOPE + MLA_V))),
        "mla_w_out": dense(O, MLA_MIX, D_MODEL, DN_BETA),
        "ffn_w_gate_up": dense((DEPTH_2,), D_MODEL, 2 * FFN_HIDDEN, DN_BETA),
        "ffn_w_down": dense((DEPTH_2,), FFN_HIDDEN, D_MODEL, DN_BETA),
        "ln_g": vec((DEPTH_2, 2, D_MODEL), 1.0, 0.02),
        "ln_b": vec((DEPTH_2, 2, D_MODEL), 0.0, 0.02),
    }

def second_block(x, positions, even_w_in, gla_gate_w2, gla_gate_b, gla_norm_g, rwkv_mu, rwkv_w0, rwkv_w2,
              rwkv_a0, rwkv_a2, rwkv_g2, rwkv_k_k, rwkv_k_a, rwkv_r_k, rwkv_ln_g, rwkv_ln_b, even_w_out,
              mla_w_in, mla_q_norm_g, mla_w_q_b, mla_kv_norm_g, mla_w_kv_b, mla_w_out,
              ffn_w_gate_up, ffn_w_down, ln_g, ln_b):
    for i in range(DEPTH_2):
        j = i // 2
        if i % 2 == 0:
            h = even_mixer(x, even_w_in[j], gla_gate_w2[j], gla_gate_b[j], gla_norm_g[j], rwkv_mu[j],
                           rwkv_w0[j], rwkv_w2[j], rwkv_a0[j], rwkv_a2[j], rwkv_g2[j], rwkv_k_k[j],
                           rwkv_k_a[j], rwkv_r_k[j], rwkv_ln_g[j], rwkv_ln_b[j], even_w_out[j])
        else:
            h = odd_mixer(x, positions, mla_w_in[j], mla_q_norm_g[j], mla_w_q_b[j], mla_kv_norm_g[j],
                          mla_w_kv_b[j], mla_w_out[j])
        x = layer_norm(DN_ALPHA * x + h, ln_g[i, 0], ln_b[i, 0])
        x = layer_norm(DN_ALPHA * x + swiglu_ffn(x, ffn_w_gate_up[i], ffn_w_down[i]), ln_g[i, 1], ln_b[i, 1])
    return x


def setup_inputs(seed=0):
    out = dict(first_inputs(seed))
    for name, value in second_inputs(seed + 1).items():
        if name != "x":
            out[name + "_2"] = value
    return out


def reference(
    x, norm1, w_in, forget_bias, rel_bias, w_branch_a, w_branch_b, w_out, norm2, w_up, w_down,
    final_norm, positions_2, even_w_in_2, gla_gate_w2_2, gla_gate_b_2, gla_norm_g_2, rwkv_mu_2,
    rwkv_w0_2, rwkv_w2_2, rwkv_a0_2, rwkv_a2_2, rwkv_g2_2, rwkv_k_k_2, rwkv_k_a_2, rwkv_r_k_2,
    rwkv_ln_g_2, rwkv_ln_b_2, even_w_out_2, mla_w_in_2, mla_q_norm_g_2, mla_w_q_b_2,
    mla_kv_norm_g_2, mla_w_kv_b_2, mla_w_out_2, ffn_w_gate_up_2, ffn_w_down_2, ln_g_2, ln_b_2,
):
    x = first_block(
        x, norm1, w_in, forget_bias, rel_bias, w_branch_a, w_branch_b, w_out, norm2, w_up,
        w_down, final_norm,
    )
    return second_block(
        x, positions_2, even_w_in_2, gla_gate_w2_2, gla_gate_b_2, gla_norm_g_2, rwkv_mu_2,
        rwkv_w0_2, rwkv_w2_2, rwkv_a0_2, rwkv_a2_2, rwkv_g2_2, rwkv_k_k_2, rwkv_k_a_2,
        rwkv_r_k_2, rwkv_ln_g_2, rwkv_ln_b_2, even_w_out_2, mla_w_in_2, mla_q_norm_g_2,
        mla_w_q_b_2, mla_kv_norm_g_2, mla_w_kv_b_2, mla_w_out_2, ffn_w_gate_up_2, ffn_w_down_2,
        ln_g_2, ln_b_2,
    )


_drawn_inputs = setup_inputs


def setup_inputs(seed=0):
    import zlib

    import numpy as np

    out = dict(_drawn_inputs(seed))
    spreads = {}
    factors = {'norm1': 7.732,
     'norm2': 3.188,
     'gla_gate_b_2': 7.721,
     'gla_norm_g_2': 8.0,
     'rwkv_w2_2': 2.979,
     'rwkv_a0_2': 8.0,
     'rwkv_k_k_2': 8.0,
     'rwkv_k_a_2': 8.0,
     'rwkv_r_k_2': 3.261,
     'rwkv_ln_g_2': 8.0,
     'rwkv_ln_b_2': 8.0,
     'mla_q_norm_g_2': 8.0,
     'mla_w_q_b_2': 3.131,
     'mla_kv_norm_g_2': 8.0}
    for name, (base, spread) in spreads.items():
        noise = np.random.default_rng([zlib.crc32(name.encode()), seed]).standard_normal(out[name].shape)
        drawn = base * np.exp(spread * noise) if base else spread * noise
        out[name] = __import__('jax').numpy.asarray(drawn.astype(out[name].dtype))
    for name, factor in factors.items():
        out[name] = (out[name] * factor).astype(out[name].dtype)
    return out
```

```python
from contextlib import ExitStack

import numpy as np

import concourse.bass as bass
from concourse import mybir

F32 = mybir.dt.float32
F32R = mybir.dt.float32r
BF16 = mybir.dt.bfloat16
I32 = mybir.dt.int32
ACT = mybir.ActivationFunctionType
ALU = mybir.AluOpType
AX = mybir.AxisListType

P = 128
T = 512
D = 1024
KD = D // P
NT = T // P
HD = 64
C32 = 32
NCH = T // C32
CPT = P // C32
MASKED = -1e30
FFN1 = 4096
FFN2 = 2816
DN_ALPHA = 4.0 ** 0.25
GLA_IN, RW_IN = 1552, 1824
MAX_REL = 128


class Signal:

    def __init__(self, sem):
        self.sem, self.base = sem, 0

    def at(self, n):
        return self.sem, n + self.base


class Chain:

    def __init__(self, eng, signal, before=0):
        self.eng, self.counter, self.before, self.n = eng, signal, before, 0

    def link(self, instruction):
        self.n += 1
        instruction.then_inc(self.counter.sem, 1)
        self.eng.wait_ge(*self.counter.at(self.n + self.before))


class Core:

    def __init__(self, nc, ctx):
        self.nc, self.ctx, self.counters, self.stage_no = nc, ctx, {}, 0

    def sb(self, ctx, name, shape, dtype=F32):
        return ctx.enter_context(self.nc.sbuf_tensor(f"{name}_{self.stage_no}", shape, dtype))

    def ps(self, ctx, name, shape):
        return ctx.enter_context(self.nc.psum_tensor(f"{name}_{self.stage_no}", shape, F32))

    def sig(self, name):
        if name not in self.counters:
            self.counters[name] = Signal(self.ctx.enter_context(self.nc.semaphore(name)))
        return self.counters[name]

    def ended(self, **counts):
        for name, n in counts.items():
            self.counters[name].base += n
        self.stage_no += 1



COUNT_FROM_ONE = ("at_scored", "at_v_turned", "at_maxed", "at_exped", "at_p_ready", "at_o_kept", "at_v_ready",
                  "rw_pe", "rw_dve", "rw_act")


def constants_stage(core, A):
    nc, ctx = core.nc, core.ctx
    core.x = core.sb(ctx, "x", [P, KD, T])
    core.ident = core.sb(ctx, "ident", [P, P])
    core.ident16 = core.sb(ctx, "ident16", [P, P], BF16)
    core.ones = core.sb(ctx, "ones", [P, P])
    core.head_ones = core.sb(ctx, "head_ones", [P, P])
    core.head_ident = core.sb(ctx, "head_ident", [P, HD])
    core.causal_mask = core.sb(ctx, "causal_mask", [P, P], BF16)
    core.chunk_mask = core.sb(ctx, "chunk_mask", [P, P], BF16)
    core.tri = core.sb(ctx, "tri", [P, 3, P])
    core.in_chunk = core.sb(ctx, "in_chunk", [P, CPT, HD])
    core.scan_keep = core.sb(ctx, "scan_keep", [P, T])

    vectors = [("norm1", A["norm1"][0]), ("norm2", A["norm2"][0]), ("final", A["final_norm"]),
               ("gla_b", A["gla_gate_b_2"][0]), ("gla_g", A["gla_norm_g_2"][0]),
               ("w0", A["rwkv_w0_2"][0]), ("a0", A["rwkv_a0_2"][0]), ("k_k", A["rwkv_k_k_2"][0]),
               ("k_a", A["rwkv_k_a_2"][0]), ("r_k", A["rwkv_r_k_2"][0].rearrange("h n -> (h n)")),
               ("rln_g", A["rwkv_ln_g_2"][0]), ("rln_b", A["rwkv_ln_b_2"][0]),
               ("mu", A["rwkv_mu_2"][0][0:14 * P]), ("mu_tail", A["rwkv_mu_2"][0][RW_IN - P:RW_IN]),
               ("q_g", A["mla_q_norm_g_2"][0]), ("kv_g", A["mla_kv_norm_g_2"][0])]
    for layer in range(2):
        for half in range(2):
            vectors += [(f"ln_g{layer}{half}", A["ln_g_2"][layer, half]),
                        (f"ln_b{layer}{half}", A["ln_b_2"][layer, half])]
    places, at = [], 0
    for name, src in vectors:
        n = src.shape[0] // P
        if at % P + n > P:
            at = -(-at // P) * P
        places.append((name, src, at, n))
        at += n
    row_tiles = -(-at // P)
    core.vec = core.sb(ctx, "vec", [P, row_tiles * P])
    core.v = {name: core.vec[:, at:at + n] for name, _, at, n in places}

    with ExitStack() as c:
        x_tok = core.sb(c, "x_tok", [P, NT, D])
        rows = core.sb(c, "rows", [P, row_tiles, P])
        bank = [core.ps(c, f"bank{b}", [P, T]) for b in range(2)]
        loaded_x, loaded_rows = core.sig("loaded_x"), core.sig("loaded_rows")
        masks, rows_zero = core.sig("masks"), core.sig("rows_zero")
        turned, copied = core.sig("turned"), core.sig("copied")
        block = c.enter_context(nc.Block())

        @block.sync
        def _(e):
            e.dma_start(x_tok[:, :, :], A["x"][0].rearrange("(t p) d -> p t d", p=P)).then_inc(loaded_x.sem, 16)
            e.wait_ge(*rows_zero.at(1))
            for _, src, at, n in places:
                e.dma_start(rows[at % P:at % P + n, at // P, :], src.rearrange("(k p) -> k p", p=P))\
                 .then_inc(loaded_rows.sem, 16)

        @block.gpsimd
        def _(e):
            for name in COUNT_FROM_ONE:
                e.sem_inc(core.sig(name).sem, 1)
            chain = Chain(e, masks)
            e.memset(rows[:, :, :], 0.0).then_inc(rows_zero.sem, 1)
            chain.link(e.memset(core.ident[:, :], 0.0))
            chain.link(e.affine_select(out=core.ident[:, :], in_=core.ident[:, :], compare_op=ALU.not_equal,
                                       fill=1.0, base=0, pattern=[[-1, P]], channel_multiplier=1))
            chain.link(e.tensor_copy(core.ident16[:, :], core.ident[:, :]))
            chain.link(e.memset(core.ones[:, :], 1.0))
            chain.link(e.memset(core.head_ones[:, :], 0.0))
            for h in range(2):
                part = core.head_ones[HD * h:HD * h + HD, HD * h:HD * h + HD]
                chain.link(e.memset(part, 1.0))
            chain.link(e.tensor_tensor(core.head_ident[:, :], core.ident[:, 0:HD], core.ident[:, HD:P], ALU.add))
            chain.link(e.memset(core.causal_mask[:, :], 0.0))
            chain.link(e.affine_select(out=core.causal_mask[:, :], in_=core.causal_mask[:, :],
                                       compare_op=ALU.is_ge, fill=MASKED, base=0,
                                       pattern=[[-1, P]], channel_multiplier=1))
            chain.link(e.memset(core.chunk_mask[:, :], 0.0))
            chain.link(e.memset(core.chunk_mask[0:HD, HD:P], MASKED))
            chain.link(e.memset(core.scan_keep[:, :], 1.0))
            chain.link(e.memset(core.scan_keep[:, 0:T:C32], 0.0))
            chain.link(e.memset(core.in_chunk[:, :, :], 1.0))
            chain.link(e.affine_select(out=core.in_chunk[:, :, :], in_=core.in_chunk[:, :, :],
                                       compare_op=ALU.is_ge, fill=0.0, base=0,
                                       pattern=[[-C32, CPT], [0, HD]], channel_multiplier=1))
            chain.link(e.affine_select(out=core.in_chunk[:, :, :], in_=core.in_chunk[:, :, :],
                                       compare_op=ALU.is_ge, fill=0.0, base=C32 - 1,
                                       pattern=[[C32, CPT], [0, HD]], channel_multiplier=-1))
            for n, (base, step) in enumerate([(-1, 1), (0, 1), (-1, -1)]):
                tri = core.tri[:, n, :].rearrange("p (c f) -> p c f", f=C32)
                chain.link(e.tensor_copy(tri, core.in_chunk[:, :, 0:C32]))
                chain.link(e.affine_select(out=core.tri[:, n, :], in_=core.tri[:, n, :], compare_op=ALU.is_ge,
                                           fill=0.0, base=base, pattern=[[step, P]], channel_multiplier=-step))
            core.n_masks = chain.n

        @block.vector
        def _(e):
            e.sem_inc(core.sig("w_lo_ready").sem, 2)
            e.sem_inc(core.sig("epi_dve_done").sem, 2)

        @block.tensor
        def _(e):
            e.sem_inc(core.sig("w_used").sem, 2)
            e.wait_ge(*masks.at(core.n_masks))
            e.wait_ge(*loaded_rows.at(16 * len(places)))
            for r in range(row_tiles):
                last = e.transpose(bank[0][:, r * P:(r + 1) * P], rows[:, r, :], core.ident[:, :])
            last.then_inc(turned.sem, 1)
            e.wait_ge(*loaded_x.at(16))
            for k in range(KD):
                if k >= 1:
                    e.wait_ge(*copied.at(k))
                for t in range(NT):
                    last = e.transpose(bank[(k + 1) % 2][:, t * P:(t + 1) * P], x_tok[:, t, k * P:(k + 1) * P],
                                       core.ident[:, :])
                last.then_inc(turned.sem, 1)

        @block.scalar
        def _(e):
            e.sem_inc(core.sig("w_hi_ready").sem, 2)
            e.sem_inc(core.sig("epi_act_done").sem, 2)
            e.wait_ge(*turned.at(1))
            e.activation(core.vec[:, :], bank[0][:, 0:row_tiles * P], ACT.Copy).then_inc(copied.sem, 1)
            for k in range(KD):
                e.wait_ge(*turned.at(k + 2))
                e.activation(core.x[:, k, :], bank[(k + 1) % 2][:, :], ACT.Copy).then_inc(copied.sem, 1)
    core.ended(**dict.fromkeys(COUNT_FROM_ONE, 1))
    core.ended(loaded_x=16, loaded_rows=16 * len(places), masks=core.n_masks, rows_zero=1,
               turned=KD + 1, copied=KD + 1)



def activations(core, ctx):
    core.AH = core.sb(ctx, "act_hi", [P, KD, T], F32R)
    core.AL = core.sb(ctx, "act_lo", [P, KD, T], F32R)


def norm_stage(core, kind, src, n, out32=None, at=0, g=None, b=None, eps=0.0, features=D, parts=True):
    nc = core.nc
    with ExitStack() as c:
        scratch = core.sb(c, "norm_y", [P, n, T]) if kind != "split" and out32 is None else None
        y = out32 if out32 is not None else scratch
        y = src if kind == "split" else y
        squares = core.sb(c, "squares", [P, 2, T])
        root = core.sb(c, "root", [P, 3, T])
        sums = core.ps(c, "sums", [P, T])
        mean = core.ps(c, "mean", [P, T])
        squared, summed = core.sig("norm_squared"), core.sig("norm_summed")
        centred, var_ready = core.sig("norm_centred"), core.sig("norm_var")
        rooted, scaled, hi_ready = core.sig("norm_rooted"), core.sig("norm_scaled"), core.sig("norm_hi")
        own = core.sig("norm_chain")
        block = c.enter_context(nc.Block())
        taken = y if kind == "ln" else src

        @block.tensor
        def _(e):
            if kind == "split":
                return
            if kind == "ln":
                for k in range(n):
                    last = e.matmul(mean[:, :], core.ones[:, :], src[:, k, :], start=(k == 0), stop=(k == n - 1))
                last.then_inc(summed.sem, n)
            for k in range(n):
                e.wait_ge(*squared.at(k + 1))
                e.matmul(sums[:, :], core.ones[:, :], squares[:, k % 2, :], start=(k == 0), stop=(k == n - 1))\
                 .then_inc(summed.sem, 1)

        offset = n if kind == "ln" else 0

        @block.scalar
        def _(e):
            if kind != "split":
                for k in range(n):
                    if kind == "ln":
                        e.wait_ge(*centred.at(k + 1))
                    if k >= 2:
                        e.wait_ge(*summed.at(offset + k - 1))
                    e.activation(squares[:, k % 2, :], taken[:, k, :], ACT.Square).then_inc(squared.sem, 1)
                e.wait_ge(*var_ready.at(1))
                e.activation(root[:, 2, :], root[:, 1, :], ACT.Sqrt).then_inc(rooted.sem, 1)
            for k in range(n if parts else 0):
                if kind != "split":
                    e.wait_ge(*scaled.at(k + 1))
                e.activation(core.AH[:, at + k, :], y[:, k, :], ACT.Copy).then_inc(hi_ready.sem, 1)

        @block.vector
        def _(e):
            chain = Chain(e, own)
            if kind == "ln":
                e.wait_ge(*summed.at(n))
                chain.link(e.tensor_scalar(root[:, 0, :], mean[:, :], 1.0 / features, None, ALU.mult))
                for k in range(n):
                    e.tensor_tensor(y[:, k, :], src[:, k, :], root[:, 0, :], ALU.subtract).then_inc(centred.sem, 1)
            if kind != "split":
                e.wait_ge(*summed.at(offset + n))
                chain.link(e.tensor_scalar(root[:, 0, :], sums[:, :], 1.0 / features, eps, ALU.mult, ALU.add))
                e.reciprocal(root[:, 1, :], root[:, 0, :]).then_inc(var_ready.sem, 1)
                e.wait_ge(*rooted.at(1))
                for k in range(n):
                    ins = e.scalar_tensor_tensor(out=y[:, k, :], in0=taken[:, k, :], scalar=g[:, k:k + 1],
                                                 in1=root[:, 2, :], op0=ALU.mult, op1=ALU.mult)
                    if b is not None:
                        chain.link(ins)
                        ins = e.tensor_scalar(y[:, k, :], y[:, k, :], b[:, k:k + 1], None, ALU.add)
                    ins.then_inc(scaled.sem, 1)
            for k in range(n if parts else 0):
                e.wait_ge(*hi_ready.at(k + 1))
                e.tensor_tensor(core.AL[:, at + k, :], y[:, k, :], core.AH[:, at + k, :].bitcast(F32), ALU.subtract)
            core.n_chain = chain.n

    norm = kind != "split"
    core.ended(norm_squared=n * norm, norm_summed=(n + offset) * norm, norm_centred=offset,
               norm_var=norm, norm_rooted=norm, norm_scaled=n * norm, norm_hi=n * parts, norm_chain=core.n_chain)



UN = 2 * P


class Job:

    def __init__(self, units, load, act, epilogue, subs=(KD,), tiles=2, pieces=1, after=False):
        self.units, self.load, self.act, self.tiles, self.pieces, self.after = units, load, act, tiles, pieces, after
        self.epi_act, self.epi_dve, self.links = epilogue
        self.subs, self.S = list(subs), len(subs)


def signal_after(e, instruction, signal):
    if instruction is None:
        e.sem_inc(signal.sem, 1)
    else:
        instruction.then_inc(signal.sem, 1)


def columns(w, first=0, tile_step=P, unit_step=UN):
    view = w.rearrange("(k p) n -> p k n", p=P)

    def load(u, s, t):
        n = min(KD, w.shape[0] // P - KD * s)
        return view[:, KD * s:KD * s + n, bass.ds(u * unit_step + (first + t * tile_step), P)]
    return load


def act_tiles(core, at=0):
    return lambda s, t, k: (core.AH[:, at + k, :], core.AL[:, at + k, :])



def keep(dst, tiles=2, scale=1.0):
    def act(e, u, acc, slot):
        return e.activation(dst[:, bass.ds(u * tiles, tiles), 0:T // 2], acc[:, 0:tiles, 0:T // 2], ACT.Copy)

    def dve(e, chain, u, acc, slot):
        return e.tensor_copy(dst[:, bass.ds(u * tiles, tiles), T // 2:T], acc[:, 0:tiles, T // 2:T])
    return act, dve, 0


def keep_sigmoid(dst):
    def act(e, u, acc, slot):
        return e.activation(dst[:, bass.ds(u * 2, 2), :], acc[:, :, :], ACT.Sigmoid)
    return act, lambda e, chain, u, acc, slot: None, 0


def residual(core, alpha=1.0):
    def dve(e, chain, u, acc, slot):
        x = core.x[:, bass.ds(u * 2, 2), :]
        return e.scalar_tensor_tensor(out=x, in0=x, scalar=alpha, in1=acc[:, :, :], op0=ALU.mult, op1=ALU.add)
    return lambda e, u, acc, slot: None, dve, 0


def relu_squared(core, hid_hi, hid_lo):
    def act(e, u, acc, slot):
        return e.activation(core.tmp_act[:, slot, :, :], acc[:, :, :], ACT.Relu)

    def dve(e, chain, u, acc, slot):
        r, y = core.tmp_act[:, slot, :, :], core.tmp_dve[:, :, :]
        hi, lo = hid_hi[:, bass.ds(u * 2, 2), :], hid_lo[:, bass.ds(u * 2, 2), :]
        chain.link(e.tensor_tensor(y, r, r, ALU.mult))
        chain.link(e.tensor_copy(hi, y))
        return e.tensor_tensor(lo, y, hi.bitcast(F32), ALU.subtract)
    return act, dve, 2


def silu_times(core, hid_hi, hid_lo):
    def act(e, u, acc, slot):
        return e.activation(core.tmp_act[:, slot, 0, :], acc[:, 0, :], ACT.Silu)

    def dve(e, chain, u, acc, slot):
        y = core.tmp_dve[:, 0, :]
        hi, lo = hid_hi[:, bass.ds(u, 1), :], hid_lo[:, bass.ds(u, 1), :]
        chain.link(e.tensor_tensor(y, core.tmp_act[:, slot, 0, :], acc[:, 1, :], ALU.mult))
        chain.link(e.tensor_copy(hi, core.tmp_dve[:, 0:1, :]))
        return e.tensor_tensor(lo, core.tmp_dve[:, 0:1, :], hi.bitcast(F32), ALU.subtract)
    return act, dve, 2


def gated_sum(core, gates):
    def dve(e, chain, u, acc, slot):
        g_a, g_b = gates[:, bass.ds(u, 1), :], gates[:, bass.ds(u + KD, 1), :]
        chain.link(e.tensor_tensor(core.tmp_dve[:, 0:1, :], g_b, acc[:, 1:2, :], ALU.mult))
        chain.link(e.tensor_tensor(g_a, g_a, acc[:, 0:1, :], ALU.mult))
        return e.tensor_tensor(g_a, g_a, core.tmp_dve[:, 0:1, :], ALU.add)
    return lambda e, u, acc, slot: None, dve, 2


def gemm_stage(core, jobs):
    nc = core.nc
    RING = 2
    with ExitStack() as c:
        w32 = core.sb(c, "w32", [P, RING, KD, UN])
        w_hi = [core.sb(c, f"w_hi{r}", [P, KD, UN], F32R) for r in range(RING)]
        w_lo = [core.sb(c, f"w_lo{r}", [P, KD, UN], F32R) for r in range(RING)]
        core.tmp_act = core.sb(c, "tmp_act", [P, 2, 2, T])
        core.tmp_dve = core.sb(c, "tmp_dve", [P, 2, T])
        acc = [core.ps(c, f"acc{r}", [P, 2, T]) for r in range(2)]
        landed = [core.sig(f"w_landed{r}") for r in range(RING)]
        hi, lo = core.sig("w_hi_ready"), core.sig("w_lo_ready")
        used = core.sig("w_used")
        act_done, dve_done = core.sig("epi_act_done"), core.sig("epi_dve_done")
        chained = core.sig("epi_chain")
        block = c.enter_context(nc.Block())

        U = G = links = 0
        loads = [0] * RING
        for j in jobs:
            j.U0, j.G0 = U, G
            j.base = list(loads)
            j.C0 = links
            links += j.units * j.links
            for n in range(j.units * j.S):
                loads[(G + n) % RING] += 16 * j.tiles * j.pieces
            U += j.units
            G += j.units * j.S
        all_units, all_parts = U, G

        def walk(e, body):
            for n, j in enumerate(jobs):
                if e is nc.tensor and j.after:
                    e.wait_ge(*act_done.at(j.U0 + 2))
                    e.wait_ge(*dve_done.at(j.U0 + 2))
                rounds = (j.units - 1) // 2
                if rounds >= 2:
                    with e.Fori(0, rounds) as it:
                        for r in range(2):
                            body(n, j, it * 2 + r, it, r, False)
                else:
                    rounds = 0
                for u in range(2 * rounds, j.units):
                    body(n, j, u, 0, u, u == j.units - 1)

        def landed_at(j, it, part):
            slot = (j.G0 + part) % RING
            first = (slot - j.G0) % RING
            return slot, it * (j.S * 16 * j.tiles * j.pieces) + (j.base[slot] + ((part - first) // RING + 1) * 16 * j.tiles * j.pieces)

        def split_width(j, s):
            return j.subs[s], j.tiles * P

        @block.sync
        def _(e):
            def body(n, j, u, it, r, last):
                for s, kt in enumerate(j.subs):
                    part = r * j.S + s
                    e.wait_ge(*lo.at(it * (2 * j.S) + (j.G0 + part + 1)))
                    slot, _ = landed_at(j, it, part)
                    for t in range(j.tiles):
                        wide = P // j.pieces
                        for i in range(j.pieces):
                            src = j.load(u, s, t) if j.pieces == 1 else j.load(u, s, t, i)
                            e.dma_start(w32[:, slot, 0:kt, t * P + i * wide:t * P + (i + 1) * wide], src)\
                             .then_inc(landed[slot].sem, 16)
            walk(e, body)

        @block.tensor
        def _(e):
            def body(n, j, u, it, r, last):
                e.wait_ge(*act_done.at(it * 2 + (j.U0 + r + 1)))
                e.wait_ge(*dve_done.at(it * 2 + (j.U0 + r + 1)))
                for s, kt in enumerate(j.subs):
                    part = r * j.S + s
                    slot = (j.G0 + part) % RING
                    e.wait_ge(*hi.at(it * (2 * j.S) + (j.G0 + part + 3)))
                    e.wait_ge(*lo.at(it * (2 * j.S) + (j.G0 + part + 3)))
                    for t in range(j.tiles):
                        cols = slice(t * P, (t + 1) * P)
                        out = acc[(j.U0 + r) % 2][:, t, :]
                        for k in range(kt):
                            a_hi, a_lo = j.act(s, t, k)
                            ends = s == j.S - 1 and k == kt - 1
                            e.matmul(out, w_hi[slot][:, k, cols], a_hi, start=(s == 0 and k == 0), stop=False)
                            e.matmul(out, w_hi[slot][:, k, cols], a_lo, start=False, stop=False)
                            mm = e.matmul(out, w_lo[slot][:, k, cols], a_hi, start=False, stop=ends)
                    mm.then_inc(used.sem, 1)
            walk(e, body)

        def splitter(e, first, one):
            def body(n, j, u, it, r, last):
                for s in range(j.S):
                    part = r * j.S + s + 1
                    ends = s == j.S - 1
                    if not (last and ends):
                        one(j, it, part, (s + 1) % j.S)
                    elif n + 1 < len(jobs):
                        one(jobs[n + 1], 0, 0, 0)
                    if ends:
                        first(j, u, it, r)
            one(jobs[0], 0, 0, 0)
            walk(e, body)

        @block.scalar
        def _(e):
            def one(j, it, part, s):
                slot, count = landed_at(j, it, part)
                kt, cols = split_width(j, s)
                e.wait_ge(*landed[slot].at(count))
                e.wait_ge(*used.at(it * (2 * j.S) + (j.G0 + part + 1)))
                e.activation(w_hi[slot][:, 0:kt, 0:cols], w32[:, slot, 0:kt, 0:cols], ACT.Copy)\
                 .then_inc(hi.sem, 1)

            def epilogue(j, u, it, r):
                e.wait_ge(*used.at(it * (2 * j.S) + (j.G0 + (r + 1) * j.S + 2)))
                e.wait_ge(*dve_done.at(it * 2 + (j.U0 + r + 1)))
                signal_after(e, j.epi_act(e, u, acc[(j.U0 + r) % 2], (j.U0 + r) % 2), act_done)
            splitter(e, epilogue, one)

        @block.vector
        def _(e):
            def one(j, it, part, s):
                slot, _ = landed_at(j, it, part)
                kt, cols = split_width(j, s)
                e.wait_ge(*hi.at(it * (2 * j.S) + (j.G0 + part + 3)))
                e.tensor_tensor(w_lo[slot][:, 0:kt, 0:cols], w32[:, slot, 0:kt, 0:cols],
                                w_hi[slot][:, 0:kt, 0:cols].bitcast(F32), ALU.subtract).then_inc(lo.sem, 1)

            def epilogue(j, u, it, r):
                chain = Chain(e, chained, it * (2 * j.links) + (j.C0 + r * j.links))
                e.wait_ge(*act_done.at(it * 2 + (j.U0 + r + 3)))
                e.wait_ge(*dve_done.at(it * 2 + (j.U0 + r + 2)))
                last = j.epi_dve(e, chain, u, acc[(j.U0 + r) % 2], (j.U0 + r) % 2)
                assert chain.n == j.links
                signal_after(e, last, dve_done)
            splitter(e, epilogue, one)

    core.ended(w_hi_ready=all_parts, w_lo_ready=all_parts, w_used=all_parts, epi_act_done=all_units,
               epi_dve_done=all_units, epi_chain=links,
               **{f"w_landed{r}": loads[r] for r in range(RING)})


QUAD = 4
PER_QUAD = QUAD * NT
S_SLOTS, P_SLOTS = 2, 3


def attention_stage(core, quads, q, k, v, out, scale, mask, bias=None, rope=None):
    nc = core.nc
    links = [2 + (bias.links[i] if bias else 0) for i in range(NT)] * QUAD
    all_links = sum(links)
    with ExitStack() as c:
        qs, ks, v_raw = (core.sb(c, s, [P, 2, T]) for s in ("q_now", "k_now", "v_raw"))
        qr = core.sb(c, "q_rope_now", [P, T]) if rope else None
        v_tok = core.sb(c, "v_tok", [P, 2, NT, P])
        biased = core.sb(c, "biased", [P, S_SLOTS, T]) if bias else None
        probs = core.sb(c, "probs", [P, P_SLOTS, T])
        probs_T = core.sb(c, "probs_T", [P, 2, NT, P])
        stat = core.sb(c, "stat", [P, 4, 4])
        score = [core.ps(c, f"score{s}", [P, T]) for s in range(S_SLOTS)]
        turned = [core.ps(c, f"turned{s}", [P, NT, P]) for s in range(2)]
        v_bank = core.ps(c, "v_bank", [P, NT, P])
        o_bank = [core.ps(c, f"o_bank{s}", [P, T]) for s in range(2)]
        staged, v_turned, v_ready = core.sig("at_staged"), core.sig("at_v_turned"), core.sig("at_v_ready")
        scored, maxed, exped = core.sig("at_scored"), core.sig("at_maxed"), core.sig("at_exped")
        normed, p_turned = core.sig("at_normed"), core.sig("at_p_turned")
        p_ready, pv_done, o_kept = core.sig("at_p_ready"), core.sig("at_pv_done"), core.sig("at_o_kept")
        chained = core.sig("at_chain")
        n_staged = 4 if rope else 3
        block = c.enter_context(nc.Block())

        def unit(n):
            return n // 8, n // 4 % 2, n % 4, (n % 4 + 1) * P

        @block.gpsimd
        def _(e):
            with e.Fori(0, quads) as it:
                e.wait_ge(*scored.at(it * PER_QUAD))
                e.wait_ge(*v_turned.at(it * 2))
                e.tensor_copy(v_raw[:, :, :], v(it)).then_inc(staged.sem, 1)
                e.tensor_copy(qs[:, :, :], q(it)).then_inc(staged.sem, 1)
                e.tensor_copy(ks[:, :, :], k(it)).then_inc(staged.sem, 1)
                if rope:
                    e.tensor_copy(qr[:, :], rope[0](it)).then_inc(staged.sem, 1)

        @block.tensor
        def _(e):
            def scores(it, n):
                a, j, i, keys = unit(n)
                rows = slice(HD * j, HD * j + HD)
                cols = slice(P * i, P * i + P)
                if n == 0:
                    e.wait_ge(*staged.at(it * n_staged + n_staged))
                if n < S_SLOTS:
                    e.wait_ge(*(maxed if bias else exped).at(it * PER_QUAD))
                else:
                    e.wait_ge(*(maxed if bias else exped).at(it * PER_QUAD + n - S_SLOTS + 1))
                s = score[n % S_SLOTS]
                e.matmul(s[:, 0:keys], qs[rows, a, cols], ks[rows, a, 0:keys], start=True, stop=False)
                if rope:
                    rr = slice(32 * (2 * a + j), 32 * (2 * a + j) + 32)
                    e.matmul(s[:, 0:keys], qr[rr, cols], rope[1][rr, 0:keys], start=False, stop=False,
                             tile_position=(32 * (2 * a + j), 0))
                e.matmul(s[:, cols], core.ident16[:, :], mask[:, :], start=False, stop=True)\
                 .then_inc(scored.sem, 1)

            def turn(it, n):
                i = unit(n)[2]
                e.wait_ge(*normed.at(it * PER_QUAD + n + 1))
                if n >= 2:
                    e.wait_ge(*p_ready.at(it * PER_QUAD + n - 1))
                else:
                    e.wait_ge(*p_ready.at(it * PER_QUAD))
                for kt in range(i + 1):
                    last = e.transpose(turned[n % 2][:, kt, :], probs[:, n % P_SLOTS, kt * P:(kt + 1) * P],
                                       core.ident[:, :])
                last.then_inc(p_turned.sem, 1)

            def values(it, n):
                a, j, i, _ = unit(n)
                e.wait_ge(*p_ready.at(it * PER_QUAD + n + 1))
                if n % 8 == 0:
                    e.wait_ge(*v_ready.at(it * 2 + a + 1))
                    e.wait_ge(*o_kept.at(it * 2))
                for kt in range(i + 1):
                    last = e.matmul(o_bank[a][HD * j:HD * j + HD, P * i:P * i + P],
                                    v_tok[:, a, kt, HD * j:HD * j + HD], probs_T[:, n % 2, kt, :],
                                    start=(kt == 0), stop=(kt == i))
                last.then_inc(pv_done.sem, 1)

            with e.Fori(0, quads) as it:
                for a in range(2):
                    e.wait_ge(*staged.at(it * n_staged + 1))
                    e.wait_ge(*v_ready.at(it * 2 + a))
                    for kt in range(NT):
                        last = e.transpose(v_bank[:, kt, :], v_raw[:, a, kt * P:(kt + 1) * P], core.ident[:, :])
                    last.then_inc(v_turned.sem, 1)
                    if a == 0:
                        scores(it, 0)
                for n in range(1, PER_QUAD + 3):
                    if n < PER_QUAD:
                        scores(it, n)
                    if 2 <= n < PER_QUAD + 2:
                        turn(it, n - 2)
                    if n >= 3:
                        values(it, n - 3)

        @block.vector
        def _(e):
            def maximum(it, n):
                a, j, i, keys = unit(n)
                chain = Chain(e, chained, it * all_links + chain_at[0])
                e.wait_ge(*scored.at(it * PER_QUAD + n + 1))
                if n >= S_SLOTS:
                    e.wait_ge(*exped.at(it * PER_QUAD + n - 1))
                src = score[n % S_SLOTS]
                if bias:
                    src = biased[:, n % S_SLOTS, :]
                    bias.add(e, chain, score[n % S_SLOTS], src, it, 2 * a + j, i)
                    src = biased[:, n % S_SLOTS, 0:keys]
                else:
                    src = src[:, 0:keys]
                chain.link(e.tensor_reduce(stat[:, n % 4, 3:4], src, AX.X, ALU.max))
                e.tensor_scalar(stat[:, n % 4, 0:1], stat[:, n % 4, 3:4], -1.0 if bias else -scale, None,
                                ALU.mult).then_inc(maxed.sem, 1)
                chain_at[0] += chain.n

            def normalise(it, n):
                keys = unit(n)[3]
                chain = Chain(e, chained, it * all_links + chain_at[0])
                e.wait_ge(*exped.at(it * PER_QUAD + n + 1))
                chain.link(e.reciprocal(stat[:, n % 4, 2:3], stat[:, n % 4, 1:2]))
                p = probs[:, n % P_SLOTS, 0:keys]
                e.tensor_scalar(p, p, stat[:, n % 4, 2:3], None, ALU.mult).then_inc(normed.sem, 1)
                chain_at[0] += chain.n

            def keep_o(it, a):
                e.wait_ge(*pv_done.at(it * PER_QUAD + 8 * (a + 1)))
                e.tensor_copy(out(it, a), o_bank[a][:, :]).then_inc(o_kept.sem, 1)

            chain_at = [0]
            with e.Fori(0, quads) as it:
                chain_at[0] = 0
                for n in range(PER_QUAD + 1):
                    if n < PER_QUAD:
                        maximum(it, n)
                    if n >= 1:
                        normalise(it, n - 1)
                    if n == 12:
                        keep_o(it, 0)
                keep_o(it, 1)
            core.n_chain = chain_at[0]

        @block.scalar
        def _(e):
            def exponentials(it, n):
                keys = unit(n)[3]
                e.wait_ge(*maxed.at(it * PER_QUAD + n + 1))
                if n >= P_SLOTS:
                    e.wait_ge(*p_turned.at(it * PER_QUAD + n - P_SLOTS + 1))
                src = biased[:, n % S_SLOTS, 0:keys] if bias else score[n % S_SLOTS][:, 0:keys]
                e.activation(probs[:, n % P_SLOTS, 0:keys], src, ACT.Exp, bias=stat[:, n % 4, 0:1],
                             scale=1.0 if bias else scale, accum_out=stat[:, n % 4, 1:2]).then_inc(exped.sem, 1)

            def copy_turned(it, n):
                i = unit(n)[2]
                e.wait_ge(*p_turned.at(it * PER_QUAD + n + 1))
                if n >= 2:
                    e.wait_ge(*pv_done.at(it * PER_QUAD + n - 1))
                e.activation(probs_T[:, n % 2, 0:i + 1, :], turned[n % 2][:, 0:i + 1, :], ACT.Copy)\
                 .then_inc(p_ready.sem, 1)

            def copy_v(it, a):
                e.wait_ge(*v_turned.at(it * 2 + a + 1))
                e.activation(v_tok[:, a, :, :], v_bank[:, :, :], ACT.Copy).then_inc(v_ready.sem, 1)

            with e.Fori(0, quads) as it:
                copy_v(it, 0)
                copy_v(it, 1)
                for n in range(PER_QUAD + 2):
                    if n < PER_QUAD:
                        exponentials(it, n)
                    if n >= 2:
                        copy_turned(it, n - 2)

    per_iteration = dict.fromkeys(("at_scored", "at_maxed", "at_exped", "at_normed", "at_p_turned",
                                   "at_p_ready", "at_pv_done"), PER_QUAD)
    per_iteration |= {"at_staged": n_staged, "at_v_turned": 2, "at_v_ready": 2, "at_o_kept": 2,
                      "at_chain": all_links}
    assert core.n_chain == all_links
    core.ended(**{name: n * quads for name, n in per_iteration.items()})


def forget_stage(core, fa, forget_bias, neg_c):
    nc, H = core.nc, 8
    with ExitStack() as c:
        fb = core.sb(c, "forget_bias", [H, 1])
        z, mag, soft, log_f, cum, one = (core.sb(c, s, [H, T]) for s in
                                         ("f_z", "f_abs", "f_soft", "f_log", "f_cum", "f_one"))
        pick = core.sb(c, "pick_head", [H, H, P])
        bank = [core.ps(c, f"f_bank{s}", [P, T]) for s in range(2)]
        loaded, picked, soft_ready = core.sig("f_loaded"), core.sig("f_picked"), core.sig("f_soft_ready")
        mag_ready, cum_ready = core.sig("f_abs_ready"), core.sig("f_cum_ready")
        spread, kept, own, act_own = core.sig("f_spread"), core.sig("f_kept"), core.sig("f_chain"), core.sig("f_act_chain")
        block = c.enter_context(nc.Block())

        @block.sync
        def _(e):
            e.dma_start(fb[:, :], forget_bias[0].rearrange("(h o) -> h o", o=1)).then_inc(loaded.sem, 16)

        @block.gpsimd
        def _(e):
            e.memset(one[:, :], 1.0).then_inc(picked.sem, 1)
            e.memset(pick[:, :, :], 0.0).then_inc(picked.sem, 1)
            e.wait_ge(*picked.at(2))
            e.affine_select(out=pick[:, :, :], in_=pick[:, :, :], compare_op=ALU.not_equal, fill=1.0, base=0,
                            pattern=[[-1, H], [0, P]], channel_multiplier=1).then_inc(picked.sem, 1)

        @block.vector
        def _(e):
            chain = Chain(e, own)
            e.wait_ge(*loaded.at(16))
            chain.link(e.tensor_scalar(z[:, :], fa[0:H, :], fb[:, 0:1], None, ALU.add))
            e.scalar_tensor_tensor(out=mag[:, :], in0=z[:, :], scalar=-1.0, in1=z[:, :], op0=ALU.mult, op1=ALU.max)\
             .then_inc(mag_ready.sem, 1)
            e.wait_ge(*soft_ready.at(1))
            chain.link(e.scalar_tensor_tensor(out=log_f[:, :], in0=z[:, :], scalar=0.0, in1=soft[:, :],
                                              op0=ALU.min, op1=ALU.subtract))
            e.wait_ge(*picked.at(1))
            chain.link(e.tensor_tensor_scan(cum[:, :], one[:, :], log_f[:, :], 0.0, ALU.mult, ALU.add))
            e.tensor_scalar(cum[:, :], cum[:, :], -1.0, None, ALU.mult).then_inc(cum_ready.sem, 1)
            core.n_chain = chain.n

        @block.scalar
        def _(e):
            e.wait_ge(*mag_ready.at(1))
            Chain(e, act_own).link(e.activation(mag[:, :], mag[:, :], ACT.Exp, scale=-1.0))
            e.activation(soft[:, :], mag[:, :], ACT.Ln, bias=1.0).then_inc(soft_ready.sem, 1)
            for h in range(H):
                e.wait_ge(*spread.at(h + 1))
                e.activation(neg_c[:, h, :], bank[h % 2][:, :], ACT.Copy).then_inc(kept.sem, 1)

        @block.tensor
        def _(e):
            e.wait_ge(*picked.at(3))
            e.wait_ge(*cum_ready.at(1))
            for h in range(H):
                if h >= 2:
                    e.wait_ge(*kept.at(h - 1))
                e.matmul(bank[h % 2][:, :], pick[:, h, :], cum[:, :], start=True, stop=True).then_inc(spread.sem, 1)
    core.ended(f_loaded=16, f_picked=3, f_soft_ready=1, f_abs_ready=1, f_cum_ready=1, f_spread=H, f_kept=H,
               f_chain=core.n_chain, f_act_chain=1)


class Bias:

    def __init__(self, add, links):
        self.add, self.links = add, links


def forget_bias_add(neg_c, scale):
    def add(e, chain, score, dst, it, h, i):
        keys = (i + 1) * P
        chain.link(e.scalar_tensor_tensor(out=dst[:, 0:keys], in0=score[:, 0:keys], scalar=scale,
                                          in1=neg_c[:, bass.ds(it * QUAD + h, 1), 0:keys].rearrange("p o k -> p (o k)"),
                                          op0=ALU.mult, op1=ALU.add))
    return Bias(add=add, links=[1] * NT)


WINDOW = 2 * P
EXTENDED = MAX_REL * 2 + 1 + P - 1


def relative_stage(core, rel_bias, scratch, near, far):
    nc, H, last = core.nc, 8, 2 * MAX_REL
    with ExitStack() as c:
        ext = core.sb(c, "rel_extended", [H, EXTENDED])
        window = core.sb(c, "rel_window", [P, H, WINDOW])
        loaded, extended = core.sig("rel_loaded"), core.sig("rel_extended")
        stored, windows = core.sig("rel_stored"), core.sig("rel_windows")
        block = c.enter_context(nc.Block())

        @block.sync
        def _(e):
            e.dma_start(ext[:, 0:last + 1], rel_bias[0]).then_inc(loaded.sem, 16)
            e.wait_ge(*extended.at(1))
            e.dma_start(scratch, ext[:, :]).then_inc(stored.sem, 16)
            e.wait_ge(*stored.at(16))
            e.dma_start(window[:, :, :], bass.AP(scratch.tensor, 1, [[1, P], [EXTENDED, H], [1, WINDOW]]))\
             .then_inc(windows.sem, 16)
            e.dma_start(far[:, :], bass.AP(scratch.tensor, last, [[0, P], [EXTENDED, H]]),
                        allow_slow_non_contiguous=True).then_inc(windows.sem, 16)
            e.wait_ge(*windows.at(32))

        @block.vector
        def _(e):
            e.wait_ge(*loaded.at(16))
            e.tensor_copy(ext[:, last + 1:EXTENDED],
                          ext[:, last:last + 1].broadcast_to([H, EXTENDED - last - 1])).then_inc(extended.sem, 1)
            e.wait_ge(*windows.at(32))
            e.tensor_copy(near[:, :, :], window[:, :, ::-1])
    core.ended(rel_loaded=16, rel_extended=1, rel_stored=16, rel_windows=32)


def relative_bias_add(near, far, scale):
    def add(e, chain, score, dst, it, h, i):
        keys = (i + 1) * P
        first = max(0, i - 1) * P
        width = keys - first
        table = near[:, bass.ds(it * QUAD + h, 1), WINDOW - width:WINDOW].rearrange("p o k -> p (o k)")
        chain.link(e.scalar_tensor_tensor(out=dst[:, first:keys], in0=score[:, first:keys], scalar=scale, in1=table,
                                          op0=ALU.mult, op1=ALU.add))
        if first:
            chain.link(e.tensor_scalar(dst[:, 0:first], score[:, 0:first], scale,
                                       far[:, bass.ds(it * QUAD + h, 1)], ALU.mult, ALU.add))
    return Bias(add=add, links=[1, 1, 2, 2])

class Results:

    def __init__(self, signal, names):
        self.counter, self.names = signal, list(names)
        self.index = {name: n + 1 for n, name in enumerate(self.names)}
        assert len(self.index) == len(self.names)
        self.marked = 0

    def mark(self, instruction, name):
        assert self.names[self.marked] == name, (self.names[self.marked], name)
        self.marked += 1
        instruction.then_inc(self.counter.sem, 1)

    def at(self, name, it=0):
        return self.counter.at(it * len(self.names) + self.index[name])

    def before(self, it):
        return self.counter.at(it * len(self.names))


def spread(ap, count, axis=1):
    shape = list(ap.shape)
    shape.insert(axis, count)
    return ap.unsqueeze(axis).broadcast_to(shape)


GLA_HEADS, GLA_RANK, GLA_EXP = 4, 16, 40.0


def gla_stage(core, A, gla, glr, o):
    nc = core.nc
    H, pairs = range(GLA_HEADS), range(2)
    dve_names = ([f"{s}{p}" for p in pairs for s in ("z", "mag")] +
                 [f"{s}{p}" for p in pairs for s in ("la", "scan", "b", "d", "c1", "c2", "d4")] +
                 [f"{s}{p}" for p in pairs for s in ("qg", "kg", "qx", "kx")] +
                 [f"AT{h}" for h in H] + ["S_zero0", "S_zero1"] +
                 [f"S{p}_{c}" for p in pairs for c in range(1, NCH)] +
                 [f"{s}{h}" for h in H for s in ("var", "rvar")] + [f"{s}{h}" for h in H for s in ("y", "out")])
    act_names = ([f"{s}{p}" for p in pairs for s in ("e", "l")] + [f"v{h}" for h in H] +
                 [f"{s}{p}" for p in pairs for s in ("E1", "E2", "E3", "E4")] + ["kt0", "kt1"] +
                 [f"{s}{h}" for h in H for s in ("o", "sq")] + [f"R{h}" for h in H] + [f"silu{h}" for h in H])
    pe_names = (["Z0", "Z1"] + [f"V{h}" for h in H] + ["KX0", "KX1"] + [f"A{h}" for h in H] +
                [f"U0{t}" for t in range(NT)] + ["O0", "O1"] + [f"U1{t}" for t in range(NT)] + ["O2", "O3"] +
                [f"N{h}" for h in H])
    pool_names = [f"kxm{p}{t}" for p in pairs for t in range(NT)]
    with ExitStack() as c:
        w2 = core.sb(c, "gla_w2", [GLA_RANK, 2 * P])
        z, mag, b, d, c1, c2, d4 = (core.sb(c, f"gla_{s}", [P, 2, T]) for s in ("z", "mag", "b", "d", "c1", "c2", "d4"))
        E1, E2, E3, E4 = c1, c2, core.sb(c, "gla_E3", [P, 2, T]), d4
        qg, kg, qx, kx = (core.sb(c, f"gla_{s}", [P, 2, T]) for s in ("qg", "kg", "qx", "kx"))
        v_tok = core.sb(c, "gla_v_tok", [P, GLA_HEADS, NT, P])
        kx_tok = core.sb(c, "gla_kx_tok", [P, 2, NT, P])
        kxm = core.sb(c, "gla_kx_masked", [P, NT, CPT, P])
        AT = core.sb(c, "gla_AT", [P, GLA_HEADS, NT, P])
        S = [core.sb(c, f"gla_S{p}", [P, NCH, P]) for p in pairs]
        raw = qg, kg
        sq = core.sb(c, "gla_sq", [P, GLA_HEADS, T])
        bank = [core.ps(c, f"gla_bank{n}", [P, T]) for n in range(8)]
        loaded = core.sig("gla_loaded")
        dve, act = Results(core.sig("gla_dve"), dve_names), Results(core.sig("gla_act"), act_names)
        pe, pool = Results(core.sig("gla_pe"), pe_names), Results(core.sig("gla_pool"), pool_names)
        block = c.enter_context(nc.Block())

        def chunks(ap):
            return ap.rearrange("p (c t) -> p c t", t=C32)

        def of_chunk(ap, t):
            return chunks(ap)[:, :, t:t + 1].broadcast_to([P, NCH, C32])

        def stat(h):
            return (z, d)[h // 2][:, h % 2, :]

        def raw_o(h):
            return raw[h // 2][:, h % 2, :]

        @block.sync
        def _(e):
            e.dma_start(w2[:, :], A["gla_gate_w2_2"][0]).then_inc(loaded.sem, 16)

        @block.tensor
        def _(e):
            e.wait_ge(*loaded.at(16))
            for p in pairs:
                pe.mark(e.matmul(bank[6 + p][:, :], w2[:, p * P:(p + 1) * P], glr[0:GLA_RANK, :],
                                 start=True, stop=True), f"Z{p}")
            turned = ([(f"V{h}", gla[:, 4 + h, :], f"v{h}") for h in H] + [(f"KX{p}", kx[:, p, :], f"kt{p}") for p in pairs])
            for n, (name, src, _) in enumerate(turned):
                if n >= 2:
                    e.wait_ge(*act.at(turned[n - 2][2]))
                if name[0] == "K":
                    e.wait_ge(*dve.at(f"kx{name[2]}"))
                for t in range(NT):
                    last = e.transpose(bank[4 + n % 2][:, t * P:(t + 1) * P], src[:, t * P:(t + 1) * P], core.ident[:, :])
                pe.mark(last, name)
            for h in H:
                p, rows = h // 2, slice(HD * (h % 2), HD * (h % 2) + HD)
                e.wait_ge(*dve.at(f"kg{p}"))
                if h >= 2:
                    e.wait_ge(*dve.at(f"AT{h - 2}"))
                for t in range(NT):
                    cols = slice(t * P, (t + 1) * P)
                    last = e.matmul(bank[6 + h % 2][:, cols], kg[rows, p, cols], qg[rows, p, cols], start=True, stop=True)
                pe.mark(last, f"A{h}")
            for p in pairs:
                for t in range(NT):
                    e.wait_ge(*pool.at(f"kxm{p}{t}"))
                    if p:
                        e.wait_ge(*dve.at(f"S0_{min(4 * t + 4, NCH - 1)}"))
                    for j in range(2):
                        for ch in range(CPT):
                            last = e.matmul(bank[t][HD * j:HD * j + HD, ch * P:(ch + 1) * P],
                                            kxm[:, t, ch, HD * j:HD * j + HD], v_tok[:, 2 * p + j, t, :],
                                            start=True, stop=True)
                    pe.mark(last, f"U{p}{t}")
                for h in (2 * p, 2 * p + 1):
                    rows = slice(HD * (h % 2), HD * (h % 2) + HD)
                    e.wait_ge(*act.at("kt1" if p == 0 else f"o{h - 2}"))
                    e.wait_ge(*dve.at(f"AT{h}"))
                    e.wait_ge(*dve.at(f"S{p}_{NCH - 1}"))
                    for t in range(NT):
                        e.matmul(bank[4 + h % 2][:, t * P:(t + 1) * P], v_tok[:, h, t, :], AT[:, h, t, :],
                                 start=True, stop=False)
                        for ch in range(CPT):
                            n = t * CPT + ch
                            cols = slice(n * C32, (n + 1) * C32)
                            last = e.matmul(bank[4 + h % 2][:, cols], S[p][rows, n, :], qx[rows, p, cols],
                                            start=False, stop=(ch == CPT - 1))
                    pe.mark(last, f"O{h}")
            for h in H:
                e.wait_ge(*act.at(f"sq{h}"))
                e.wait_ge(*dve.at(f"AT{h}" if h < 2 else f"var{h - 2}"))
                pe.mark(e.matmul(bank[6 + h % 2][:, :], core.ones[:, :], sq[:, h, :], start=True, stop=True), f"N{h}")

        @block.gpsimd
        def _(e):
            for p in pairs:
                e.wait_ge(*act.at(f"kt{p}"))
                for t in range(NT):
                    if p:
                        e.wait_ge(*pe.at(f"U0{t}"))
                    src = kx_tok[:, p, t, :].rearrange("p (j k) -> p j k", j=2)
                    for ch in range(CPT):
                        last = e.tensor_tensor(kxm[:, t, ch, :].rearrange("p (j k) -> p j k", j=2), src,
                                               spread(core.in_chunk[:, ch, :], 2), ALU.mult)
                    pool.mark(last, f"kxm{p}{t}")

        @block.vector
        def _(e):
            gb = core.v["gla_b"]
            for p in pairs:
                e.wait_ge(*pe.at(f"Z{p}"))
                dve.mark(e.tensor_scalar(z[:, p, :], bank[6 + p][:, :], gb[:, p:p + 1], None, ALU.add), f"z{p}")
                e.wait_ge(*dve.at(f"z{p}"))
                dve.mark(e.scalar_tensor_tensor(out=mag[:, p, :], in0=z[:, p, :], scalar=-1.0, in1=z[:, p, :],
                                                op0=ALU.mult, op1=ALU.max), f"mag{p}")
            for p in pairs:
                zp, bp, dp = z[:, p, :], b[:, p, :], d[:, p, :]
                e.wait_ge(*act.at(f"l{p}"))
                dve.mark(e.scalar_tensor_tensor(out=zp, in0=zp, scalar=0.0, in1=mag[:, p, :], op0=ALU.min,
                                                op1=ALU.subtract), f"la{p}")
                e.wait_ge(*dve.at(f"la{p}"))
                dve.mark(e.tensor_tensor_scan(dp, core.scan_keep[:, :], zp, 0.0, ALU.mult, ALU.add), f"scan{p}")
                e.wait_ge(*dve.at(f"scan{p}"))
                dve.mark(e.tensor_scalar(bp, dp, 1.0 / 16.0, None, ALU.mult), f"b{p}")
                e.wait_ge(*dve.at(f"b{p}"))
                dve.mark(e.tensor_tensor(chunks(dp), chunks(bp), of_chunk(bp, C32 // 2 - 1), ALU.subtract), f"d{p}")
                e.wait_ge(*dve.at(f"d{p}"))
                dve.mark(e.tensor_scalar(c1[:, p, :], dp, GLA_EXP, None, ALU.min), f"c1{p}")
                dve.mark(e.tensor_scalar(c2[:, p, :], dp, -1.0, GLA_EXP, ALU.mult, ALU.min), f"c2{p}")
                dve.mark(e.tensor_tensor(chunks(d4[:, p, :]), of_chunk(bp, C32 - 1), chunks(bp), ALU.subtract), f"d4{p}")
            for p in pairs:
                e.wait_ge(*act.at(f"E4{p}"))
                q, k = gla[:, p, :], gla[:, 2 + p, :]
                dve.mark(e.scalar_tensor_tensor(out=qg[:, p, :], in0=q, scalar=HD ** -0.5, in1=E1[:, p, :],
                                                op0=ALU.mult, op1=ALU.mult), f"qg{p}")
                dve.mark(e.tensor_tensor(kg[:, p, :], k, E2[:, p, :], ALU.mult), f"kg{p}")
                dve.mark(e.scalar_tensor_tensor(out=qx[:, p, :], in0=q, scalar=HD ** -0.5, in1=E3[:, p, :],
                                                op0=ALU.mult, op1=ALU.mult), f"qx{p}")
                dve.mark(e.tensor_tensor(kx[:, p, :], k, E4[:, p, :], ALU.mult), f"kx{p}")
            for h in H:
                e.wait_ge(*pe.at(f"A{h}"))
                src = bank[6 + h % 2][:, :].rearrange("p (t f) -> p t f", t=NT)
                dve.mark(e.tensor_tensor(AT[:, h, :, :], src, spread(core.tri[:, 1, :], NT), ALU.mult), f"AT{h}")
            for p in pairs:
                dve.mark(e.memset(S[p][:, 0, :], 0.0), f"S_zero{p}")
            for p in pairs:
                for ch in range(1, NCH):
                    n = ch - 1
                    e.wait_ge(*pe.at(f"U{p}{n // CPT}"))
                    e.wait_ge(*dve.at(f"S{p}_{n}" if n else f"S_zero{p}"))
                    u = bank[n // CPT][:, (n % CPT) * P:(n % CPT + 1) * P]
                    dve.mark(e.scalar_tensor_tensor(out=S[p][:, ch, :], in0=S[p][:, n, :],
                                                    scalar=E3[:, p, n * C32 + C32 - 1:n * C32 + C32], in1=u,
                                                    op0=ALU.mult, op1=ALU.add), f"S{p}_{ch}")
            for h in H:
                e.wait_ge(*pe.at(f"N{h}"))
                dve.mark(e.tensor_scalar(stat(h), bank[6 + h % 2][:, :], 1.0 / P, 1e-6, ALU.mult, ALU.add), f"var{h}")
                e.wait_ge(*dve.at(f"var{h}"))
                dve.mark(e.reciprocal(stat(h), stat(h)), f"rvar{h}")
            for h in H:
                e.wait_ge(*act.at(f"R{h}"))
                dve.mark(e.scalar_tensor_tensor(out=stat(h), in0=raw_o(h), scalar=core.v["gla_g"][:, 0:1], in1=stat(h),
                                                op0=ALU.mult, op1=ALU.mult), f"y{h}")
                e.wait_ge(*dve.at(f"y{h}"))
                e.wait_ge(*act.at(f"silu{h}"))
                dve.mark(e.tensor_tensor(o[:, h, :], stat(h), sq[:, h, :], ALU.mult), f"out{h}")

        @block.scalar
        def _(e):
            for p in pairs:
                e.wait_ge(*dve.at(f"mag{p}"))
                act.mark(e.activation(mag[:, p, :], mag[:, p, :], ACT.Exp, scale=-1.0), f"e{p}")
                e.wait_ge(*act.at(f"e{p}"))
                act.mark(e.activation(mag[:, p, :], mag[:, p, :], ACT.Ln, bias=1.0), f"l{p}")
            for h in H:
                e.wait_ge(*pe.at(f"V{h}"))
                act.mark(e.activation(v_tok[:, h, :, :], bank[4 + h % 2][:, :].rearrange("p (t f) -> p t f", t=NT),
                                      ACT.Copy), f"v{h}")
            for p in pairs:
                e.wait_ge(*dve.at(f"d4{p}"))
                act.mark(e.activation(E1[:, p, :], c1[:, p, :], ACT.Exp), f"E1{p}")
                act.mark(e.activation(E2[:, p, :], c2[:, p, :], ACT.Exp), f"E2{p}")
                act.mark(e.activation(E3[:, p, :], b[:, p, :], ACT.Exp), f"E3{p}")
                act.mark(e.activation(E4[:, p, :], d4[:, p, :], ACT.Exp), f"E4{p}")
            for p in pairs:
                e.wait_ge(*pe.at(f"KX{p}"))
                act.mark(e.activation(kx_tok[:, p, :, :], bank[4 + p][:, :].rearrange("p (t f) -> p t f", t=NT),
                                      ACT.Copy), f"kt{p}")
            for h in H:
                e.wait_ge(*pe.at(f"O{h}"))
                act.mark(e.activation(raw_o(h), bank[4 + h % 2][:, :], ACT.Copy), f"o{h}")
                e.wait_ge(*act.at(f"o{h}"))
                act.mark(e.activation(sq[:, h, :], raw_o(h), ACT.Square), f"sq{h}")
            for h in H:
                e.wait_ge(*dve.at(f"rvar{h}"))
                act.mark(e.activation(stat(h), stat(h), ACT.Sqrt), f"R{h}")
            for h in H:
                e.wait_ge(*pe.at(f"N{h}"))
                act.mark(e.activation(sq[:, h, :], gla[:, 8 + h, :], ACT.Silu), f"silu{h}")
    core.ended(gla_loaded=16, gla_dve=len(dve_names), gla_act=len(act_names), gla_pe=len(pe_names),
               gla_pool=len(pool_names))


RW_DECAY, RW_GN_EPS = 0.6065306597126334, 64e-5


def rwkv_prepare_stage(core, A, rw, decay, rate, gate):
    nc = core.nc
    tiles, pairs = range(15), range(4)
    order = [12, 13, 14] + list(range(12))
    dve_names = [f"{s}{n}" for n in order for s in ("shift", "mix")] + [f"decay{p}" for p in pairs]
    act_names = ["tanh", "sig13", "sig14"] + [f"{s}{p}" for p in pairs for s in ("w", "a", "g")]
    pe_names = [f"{s}{p}" for p in pairs for s in ("W", "A", "G")]
    with ExitStack() as c:
        w2a2 = core.sb(c, "w2a2", [P, T])
        g2 = core.sb(c, "g2", [P, 2, T])
        diff = core.sb(c, "shift_diff", [P, 2, T])
        low = core.sb(c, "low_rank", [P, 3, T])
        bank = [core.ps(c, f"rwp_bank{n}", [P, T]) for n in range(6)]
        loaded = core.sig("rwp_loaded")
        dve, act, pe = (Results(core.sig(f"rwp_{s}"), n) for s, n in
                        (("dve", dve_names), ("act", act_names), ("pe", pe_names)))
        block = c.enter_context(nc.Block())

        @block.sync
        def _(e):
            for dst, src in ((w2a2[0:HD, :], A["rwkv_w2_2"][0]), (w2a2[HD:P, :], A["rwkv_a2_2"][0]),
                             (g2[:, 0, :], A["rwkv_g2_2"][0][0:P]), (g2[96:P, 1, :], A["rwkv_g2_2"][0][P:P + 32])):
                e.dma_start(dst, src).then_inc(loaded.sem, 16)

        @block.vector
        def _(e):
            for i, n in enumerate(order):
                p, dd = rw[:, n, :], diff[:, i % 2, :]
                mu = core.v["mu_tail"][:, 0:1] if n == 14 else core.v["mu"][:, n:n + 1]
                if i >= 2:
                    e.wait_ge(*dve.at(f"mix{order[i - 2]}"))
                e.tensor_scalar(dd[:, 0:1], p[:, 0:1], -1.0, None, ALU.mult)
                dve.mark(e.tensor_tensor(dd[:, 1:T], p[:, 0:T - 1], p[:, 1:T], ALU.subtract), f"shift{n}")
                e.wait_ge(*dve.at(f"shift{n}"))
                dve.mark(e.scalar_tensor_tensor(out=p, in0=dd, scalar=mu, in1=p, op0=ALU.mult, op1=ALU.add), f"mix{n}")
            for p in pairs:
                e.wait_ge(*act.at(f"w{p}"))
                dve.mark(e.tensor_scalar(decay[:, p, :], decay[:, p, :], -RW_DECAY, None, ALU.mult), f"decay{p}")

        @block.scalar
        def _(e):
            e.wait_ge(*dve.at("mix12"))
            act.mark(e.activation(low[0:HD, 0, :], rw[0:HD, 12, :], ACT.Tanh), "tanh")
            e.wait_ge(*dve.at("mix14"))
            act.mark(e.activation(low[:, 1, :], rw[:, 13, :], ACT.Sigmoid), "sig13")
            act.mark(e.activation(low[96:P, 2, :], rw[96:P, 14, :], ACT.Sigmoid), "sig14")
            for p in pairs:
                b = 3 * (p % 2)
                e.wait_ge(*pe.at(f"W{p}"))
                act.mark(e.activation(decay[:, p, :], bank[b][:, :], ACT.Sigmoid, bias=core.v["w0"][:, p:p + 1]), f"w{p}")
                e.wait_ge(*pe.at(f"A{p}"))
                act.mark(e.activation(rate[:, p, :], bank[b + 1][:, :], ACT.Sigmoid, bias=core.v["a0"][:, p:p + 1]), f"a{p}")
                e.wait_ge(*pe.at(f"G{p}"))
                act.mark(e.activation(gate[:, p, :], bank[b + 2][:, :], ACT.Copy), f"g{p}")

        @block.tensor
        def _(e):
            e.wait_ge(*loaded.at(64))
            e.wait_ge(*act.at("sig14"))
            for p in pairs:
                cols, b = slice(p * P, (p + 1) * P), 3 * (p % 2)
                if p >= 2:
                    e.wait_ge(*act.at(f"g{p - 2}"))
                pe.mark(e.matmul(bank[b][:, :], w2a2[0:HD, cols], low[0:HD, 0, :], start=True, stop=True), f"W{p}")
                pe.mark(e.matmul(bank[b + 1][:, :], w2a2[HD:P, cols], rw[HD:P, 12, :], start=True, stop=True), f"A{p}")
                e.matmul(bank[b + 2][:, :], g2[:, 0, cols], low[:, 1, :], start=True, stop=False)
                pe.mark(e.matmul(bank[b + 2][:, :], g2[96:P, 1, cols], low[96:P, 2, :], start=False, stop=True,
                                 tile_position=(96, 0)), f"G{p}")
    core.ended(rwp_loaded=64, rwp_dve=len(dve_names), rwp_act=len(act_names), rwp_pe=len(pe_names))


def rwkv_stage(core, rw, decay, rate, gate, o, o_at):
    nc = core.nc
    J = range(2)
    both = lambda s: [f"{s}{j}" for j in J]
    fills = ([("NORM", "D"), ("BONUS", "D"), ("TA", "A"), ("TB", "A"), ("TK", "A"), ("TV", "A")] +
             [(f"{s}{j}", eng) for j in J for s, eng in (("BAa", "D"), ("BAb", "D"), ("M", "D"), ("KAa", "D"), ("KAb", "D"))] +
             [(f"{s}{j}", eng) for j in J for s, eng in (("M2", "A"), ("T2", "D"), ("AV", "A"))] +
             [(f"{s}{j}", eng) for j in J for s, eng in (("M4", "A"), ("T4", "A"), ("X2", "D"))] +
             [(f"{s}{j}", eng) for j in J for s, eng in (("M8", "A"), ("T8", "A"), ("X4", "D"))] +
             [(f"{s}{j}", eng) for j in J for s, eng in (("M16", "A"), ("X8", "D"))] +
             [(f"X16{j}", "D") for j in J] + [(f"P{j}", "A") for j in J] + [("Q", "D")] +
             [("Ga", "D"), ("Gb", "D"), ("Fa", "D"), ("Fb", "D")] +
             [(f"S{ch}", "D") for ch in range(2, NCH)] + [("Y", "A"), ("MU", "D"), ("VAR", "D")])
    number = {name: n for n, (name, _) in enumerate(fills)}
    taken_by = dict(fills)
    BANKS = 8
    dve_names = (["kk0", "NORM", "rn", "kk", "t", "kx", "scan", "cx", "ah", "bb", "bh", "kh", "rh", "rk", "BONUS"] +
                 [f"{s}{j}" for j in J for s in ("BAa", "BAb", "M", "X1", "KAa", "KAb")] +
                 both("T2") + both("X2") + both("X4") + both("X8") + both("X16") +
                 ["Q", "Ga", "Gb", "Fa", "Fb", "S_zero", "S1"] + [f"S{ch}" for ch in range(2, NCH)] +
                 ["MU", "yc", "VAR", "rv", "yg", "yb", "yo", "out"])
    act_names = (["sq", "root", "Ew", "En", "Ex", "TA", "TB", "TK", "TV"] +
                 [f"{s}{j}" for j in J for s in ("M2", "AV")] + [f"{s}{j}" for j in J for s in ("M4", "T4")] +
                 [f"{s}{j}" for j in J for s in ("M8", "T8")] + both("M16") + both("P") + ["Y", "sq2", "root2"])
    pool_names = ["v"] + [f"{s}{j}" for s in ("Bm", "Km") for j in J]
    pe_names = [name for name, _ in fills]
    with ExitStack() as c:
        f = {s: core.sb(c, f"rw_{s}", [P, T]) for s in ("kk", "k2", "cw", "cx", "En", "v", "s1", "s2", "bh", "kh")}
        f |= {"y": f["kk"], "t": f["cw"], "bonus": f["En"], "ah": f["cx"]}
        Ew = core.sb(c, "rw_Ew", [P, T])
        ar = core.sb(c, "rw_ar", [P, 2, T])
        tok_b, tok_k, tok_v = (core.sb(c, f"rw_tok_{s}", [P, NT, P]) for s in "bkv")
        av = [core.sb(c, f"rw_av{j}", [P, NT, P]) for j in J]
        ba = [core.sb(c, f"rw_ba{j}", [P, NT, 2, P]) for j in J]
        ka = [core.sb(c, f"rw_ka{j}", [P, NT, 2, P]) for j in J]
        Ms = [[core.sb(c, f"rw_M{j}{s}", [P, NT, P]) for s in range(2)] for j in J]
        Ts = [[core.sb(c, f"rw_T{j}{s}", [P, NT, P]) for s in range(2)] for j in J]
        XT = [core.sb(c, f"rw_XT{j}", [P, NT, P]) for j in J]
        PP = av
        bm = [core.sb(c, f"rw_bm{j}", [P, NT, CPT, HD]) for j in J]
        km = [core.sb(c, f"rw_km{j}", [P, NT, CPT, HD]) for j in J]
        q1 = core.sb(c, "rw_q1", [P, T])
        G = core.sb(c, "rw_G", [P, NCH, HD])
        F = core.sb(c, "rw_F", [P, NCH, HD])
        ST = core.sb(c, "rw_ST", [P, NCH, HD])
        bank = [core.ps(c, f"rw_bank{n}", [P, T]) for n in range(BANKS)]
        dve, act = Results(core.sig("rw_dve"), dve_names), Results(core.sig("rw_act"), act_names)
        pe, pool = Results(core.sig("rw_pe"), pe_names), Results(core.sig("rw_pool"), pool_names)
        steps = core.sig("rw_state_steps")
        block = c.enter_context(nc.Block())

        def taken(name, it):
            return (dve if taken_by[name] == "D" else act).at(name, it)

        def bank_of(name):
            return bank[number[name] % BANKS]

        def tiles4(name):
            return bank_of(name)[:, :].rearrange("p (t f) -> p t f", t=NT)

        def row(tensor, tile):
            return tensor[:, bass.ds(tile, 1), :].rearrange("p o t -> p (o t)")

        @block.gpsimd
        def _(e):
            with e.Fori(0, 4) as it:
                pool.marked = 0
                e.wait_ge(*pe.before(it))
                e.wait_ge(*dve.before(it))
                pool.mark(e.tensor_copy(f["v"][:, :], row(rw, it + 8)), "v")
                for s, src, dst in (("Bm", tok_b, bm), ("Km", tok_k, km)):
                    e.wait_ge(*act.at("T" + s[0], it))
                    for j in J:
                        for t in range(NT):
                            last = e.tensor_tensor(dst[j][:, t, :, :], spread(src[:, t, HD * j:HD * j + HD], CPT),
                                                   core.in_chunk[:, :, :], ALU.mult)
                        pool.mark(last, f"{s}{j}")

        @block.tensor
        def _(e):
            def fill(name, it, emit, *needs):
                n = number[name]
                if n >= BANKS:
                    e.wait_ge(*taken(fills[n - BANKS][0], it))
                for need in needs:
                    e.wait_ge(*need)
                if name[0] == "S":
                    e.sem_inc(steps.sem, 1)
                pe.mark(emit(bank_of(name)), name)

            def over_tiles(out_cols, operands):
                def emit(b):
                    for t in range(NT):
                        lhsT, rhs = operands(t)
                        last = e.matmul(b[:, t * out_cols:(t + 1) * out_cols], lhsT, rhs, start=True, stop=True)
                    return last
                return emit

            def turn(src):
                def emit(b):
                    for t in range(NT):
                        last = e.transpose(b[:, t * P:(t + 1) * P], src[:, t * P:(t + 1) * P], core.ident[:, :])
                    return last
                return emit

            with e.Fori(0, 4) as it:
                pe.marked = 0
                e.wait_ge(*dve.before(it))
                e.wait_ge(*act.before(it))
                fill("NORM", it, lambda b: e.matmul(b[:, :], core.head_ones[:, :], f["s1"][:, :], start=True, stop=True),
                     act.at("sq", it))
                fill("BONUS", it, lambda b: e.matmul(b[:, :], core.head_ones[:, :], f["t"][:, :], start=True, stop=True),
                     dve.at("rk", it))
                fill("TA", it, turn(f["ah"]), dve.at("ah", it))
                fill("TB", it, turn(f["bh"]), dve.at("bh", it))
                fill("TK", it, turn(f["kh"]), dve.at("kh", it))
                fill("TV", it, turn(f["v"]), pool.at("v", it))
                for j in J:
                    rows = slice(HD * j, HD * j + HD)
                    for s, lhs in (("BA", "bh"), ("M", None), ("KA", "kh")):
                        if s == "M":
                            fill(f"M{j}", it, over_tiles(P, lambda t: (ar[rows, 0, t * P:(t + 1) * P],
                                                                       f["bh"][rows, t * P:(t + 1) * P])))
                            continue
                        for half in range(2):
                            def emit(b):
                                for t in (2 * half, 2 * half + 1):
                                    cols = slice(t * P, (t + 1) * P)
                                    last = e.matmul(b[:, (t % 2) * 2 * P:(t % 2 + 1) * 2 * P].rearrange("p (a f) -> p a f", a=2),
                                                    f[lhs][rows, cols], ar[rows, :, cols], start=True, stop=True)
                                return last
                            fill(f"{s}{'ab'[half]}{j}", it, emit, dve.at("rh", it))
                for j in J:
                    fill(f"M2{j}", it, over_tiles(P, lambda t: (ba[j][:, t, 0, :], Ms[j][0][:, t, :])), dve.at(f"M{j}", it))
                    fill(f"T2{j}", it, over_tiles(P, lambda t: (Ms[j][0][:, t, :], ba[j][:, t, 0, :])))
                    fill(f"AV{j}", it, over_tiles(HD, lambda t: (ka[j][:, t, 0, :], tok_v[:, t, HD * j:HD * j + HD])),
                         dve.at(f"KAb{j}", it), act.at("TV", it))
                for n, power in enumerate((2, 4, 8)):
                    for j in J:
                        now, nxt = Ms[j][(n + 1) % 2], power * 2
                        tn = Ts[j][(n + 1) % 2]
                        t_ready = (dve if power == 2 else act).at(f"T{power}{j}", it)
                        fill(f"M{nxt}{j}", it, over_tiles(P, lambda t: (tn[:, t, :], now[:, t, :])),
                             act.at(f"M{power}{j}", it), t_ready)
                        if nxt < 16:
                            fill(f"T{nxt}{j}", it, over_tiles(P, lambda t: (now[:, t, :], tn[:, t, :])))
                        x_ready = dve.at(f"X{power // 2}{j}" , it)
                        fill(f"X{power}{j}", it, over_tiles(P, lambda t: (now[:, t, :], XT[j][:, t, :])), x_ready)
                for j in J:
                    fill(f"X16{j}", it, over_tiles(P, lambda t: (Ms[j][0][:, t, :], XT[j][:, t, :])),
                         act.at(f"M16{j}", it), dve.at(f"X8{j}", it))
                for j in J:
                    fill(f"P{j}", it, over_tiles(P, lambda t: (XT[j][:, t, :], av[j][:, t, :])),
                         dve.at(f"X16{j}", it), act.at(f"AV{j}", it))

                def q_products(b):
                    for j in J:
                        for t in range(NT):
                            last = e.matmul(b[HD * j:HD * j + HD, t * P:(t + 1) * P], PP[j][:, t, 0:HD], ba[j][:, t, 1, :],
                                            start=True, stop=True)
                    return last
                fill("Q", it, q_products, act.at("P1", it))
                for half in range(2):
                    def emit(b):
                        for j in J:
                            for t in (2 * half, 2 * half + 1):
                                last = e.matmul(b[HD * j:HD * j + HD, (t % 2) * 2 * P:(t % 2 + 1) * 2 * P],
                                                PP[j][:, t, 0:HD], bm[j][:, t, :, :].rearrange("p c k -> p (c k)"),
                                                start=True, stop=True)
                        return last
                    fill(f"G{'ab'[half]}", it, emit, pool.at("Bm1", it))
                for half in range(2):
                    def emit(b):
                        for j in J:
                            for n in range(8 * half, 8 * half + 8):
                                t, ch = n // CPT, n % CPT
                                out = b[HD * j:HD * j + HD, (n % 8) * HD:(n % 8 + 1) * HD]
                                e.matmul(out, bm[j][:, t, ch, :], PP[j][:, t, HD:P], start=True, stop=False)
                                last = e.matmul(out, km[j][:, t, ch, :], tok_v[:, t, HD * j:HD * j + HD],
                                                start=False, stop=True)
                        return last
                    fill(f"F{'ab'[half]}", it, emit, pool.at("Km1", it))
                for ch in range(2, NCH):
                    def emit(b):
                        for j in J:
                            rows = slice(HD * j, HD * j + HD)
                            last = e.matmul(b[rows, 0:HD], G[rows, ch - 1, :], ST[rows, ch - 1, :], start=True, stop=True)
                        return last
                    fill(f"S{ch}", it, emit, dve.at(f"S{ch - 1}", it))

                def outputs(b):
                    for j in J:
                        rows = slice(HD * j, HD * j + HD)
                        for t in range(NT):
                            out = b[rows, t * P:(t + 1) * P]
                            e.matmul(out, PP[j][:, t, HD:P], ba[j][:, t, 1, :], start=True, stop=False)
                            e.matmul(out, tok_v[:, t, HD * j:HD * j + HD], ka[j][:, t, 1, :], start=False, stop=False)
                            for ch in range(CPT):
                                n = t * CPT + ch
                                cols = slice(n * C32, (n + 1) * C32)
                                last = e.matmul(b[rows, cols], ST[rows, n, :], q1[rows, cols], start=False,
                                                stop=(ch == CPT - 1))
                    return last
                fill("Y", it, outputs, dve.at(f"S{NCH - 1}", it))
                fill("MU", it, lambda b: e.matmul(b[:, :], core.head_ones[:, :], f["y"][:, :], start=True, stop=True),
                     act.at("Y", it))
                fill("VAR", it, lambda b: e.matmul(b[:, :], core.head_ones[:, :], f["s1"][:, :], start=True, stop=True),
                     act.at("sq2", it))

        @block.vector
        def _(e):
            with e.Fori(0, 4) as it:
                dve.marked = 0
                r, k, lw, a = row(rw, it), row(rw, it + 4), row(decay, it), row(rate, it)

                def col(name):
                    return core.v[name][:, bass.ds(it, 1)]

                def do(name, instruction, *needs):
                    for need in needs:
                        e.wait_ge(*need)
                    dve.mark(instruction(), name)

                D_, A_, P_ = (lambda s: dve.at(s, it)), (lambda s: act.at(s, it)), (lambda s: pe.at(s, it))
                tt, ts, stt = e.tensor_tensor, e.tensor_scalar, e.scalar_tensor_tensor
                e.wait_ge(*pe.before(it))
                e.wait_ge(*act.before(it))
                do("kk0", lambda: ts(f["kk"][:, :], k, col("k_k"), None, ALU.mult))
                do("NORM", lambda: ts(f["s2"][:, :], bank_of("NORM")[:, :], 1e-24, None, ALU.max), P_("NORM"))
                do("rn", lambda: e.reciprocal(f["s2"][:, :], f["s2"][:, :]), D_("NORM"))
                do("kk", lambda: tt(f["kk"][:, :], f["kk"][:, :], f["s2"][:, :], ALU.mult), A_("root"))
                do("t", lambda: ts(f["k2"][:, :], a, -1.0, col("k_a"), ALU.add, ALU.mult))
                do("kx", lambda: stt(out=f["k2"][:, :], in0=f["k2"][:, :], scalar=1.0, in1=k, op0=ALU.add, op1=ALU.mult), D_("t"))
                do("scan", lambda: e.tensor_tensor_scan(f["cw"][:, :], core.scan_keep[:, :], lw, 0.0, ALU.mult, ALU.add))
                do("cx", lambda: tt(f["cx"][:, :], f["cw"][:, :], lw, ALU.subtract), D_("scan"))
                do("ah", lambda: stt(out=f["ah"][:, :], in0=f["kk"][:, :], scalar=-1.0, in1=f["cx"][:, :], op0=ALU.mult,
                                     op1=ALU.mult), A_("Ex"), D_("kk"))
                do("bb", lambda: tt(f["bh"][:, :], f["kk"][:, :], a, ALU.mult))
                do("bh", lambda: tt(f["bh"][:, :], f["bh"][:, :], f["En"][:, :], ALU.mult), D_("bb"))
                do("kh", lambda: tt(f["kh"][:, :], f["k2"][:, :], f["En"][:, :], ALU.mult), D_("kx"))
                e.tensor_copy(ar[:, 0, :], f["ah"][:, :])
                do("rh", lambda: tt(ar[:, 1, :], r, Ew[:, :], ALU.mult))
                do("rk", lambda: stt(out=f["t"][:, :], in0=r, scalar=col("r_k"), in1=f["k2"][:, :], op0=ALU.mult, op1=ALU.mult))
                do("BONUS", lambda: tt(f["bonus"][:, :], bank_of("BONUS")[:, :], f["v"][:, :], ALU.mult), P_("BONUS"),
                   pool.at("v", it))
                upper = core.tri[:, 0:2, :]
                for j in J:
                    for s, dst in (("BA", ba), ("M", None), ("KA", ka)):
                        if s == "M":
                            do(f"M{j}", lambda: tt(Ms[j][0][:, :, :], tiles4(f"M{j}"), spread(core.tri[:, 2, :], NT), ALU.mult),
                               P_(f"M{j}"))
                            do(f"X1{j}", lambda: tt(XT[j][:, :, :], ba[j][:, :, 0, :], spread(core.ident[:, :], NT), ALU.add),
                               D_(f"BAb{j}"))
                            continue
                        for half in range(2):
                            name = f"{s}{'ab'[half]}{j}"
                            src = bank_of(name)[:, :].rearrange("p (t f) -> p t f", t=2)
                            do(name, lambda: tt(dst[j][:, 2 * half:2 * half + 2, :, :].rearrange("p t a f -> p t (a f)"), src,
                                                spread(upper.rearrange("p a f -> p (a f)"), 2), ALU.mult), P_(name))
                for j in J:
                    do(f"T2{j}", lambda: e.tensor_copy(Ts[j][1][:, :, :], tiles4(f"T2{j}")), P_(f"T2{j}"))
                for power in (2, 4, 8, 16):
                    for j in J:
                        do(f"X{power}{j}", lambda: tt(XT[j][:, :, :], XT[j][:, :, :], tiles4(f"X{power}{j}"), ALU.add),
                           P_(f"X{power}{j}"), D_(f"X{power // 2}{j}"))
                do("Q", lambda: tt(q1[:, :], bank_of("Q")[:, :], ar[:, 1, :], ALU.add), P_("Q"))
                last_w = Ew[:, C32 - 1:T:C32].unsqueeze(2)
                for half in range(2):
                    name, ch = f"G{'ab'[half]}", slice(8 * half, 8 * half + 8)
                    do(name, lambda: tt(G[:, ch, :], bank_of(name)[:, :].rearrange("p (c k) -> p c k", c=8),
                                        spread(core.head_ident[:, :], 8), ALU.add), P_(name))
                for half in range(2):
                    name, ch = f"F{'ab'[half]}", slice(8 * half, 8 * half + 8)
                    do(name, lambda: tt(F[:, ch, :], bank_of(name)[:, :].rearrange("p (c k) -> p c k", c=8),
                                        last_w[:, ch, :].broadcast_to([P, 8, HD]), ALU.mult), P_(name))
                do("S_zero", lambda: e.memset(ST[:, 0, :], 0.0))
                do("S1", lambda: e.tensor_copy(ST[:, 1, :], F[:, 0, :]), D_("Fa"))
                for ch in range(2, NCH):
                    do(f"S{ch}", lambda: stt(out=ST[:, ch, :], in0=bank_of(f"S{ch}")[:, 0:HD],
                                             scalar=Ew[:, ch * C32 - 1:ch * C32], in1=F[:, ch - 1, :], op0=ALU.mult,
                                             op1=ALU.add), P_(f"S{ch}"), D_("Fb"))
                do("MU", lambda: ts(f["s2"][:, :], bank_of("MU")[:, :], 1.0 / HD, None, ALU.mult), P_("MU"))
                do("yc", lambda: tt(f["y"][:, :], f["y"][:, :], f["s2"][:, :], ALU.subtract), D_("MU"))
                do("VAR", lambda: ts(f["s2"][:, :], bank_of("VAR")[:, :], 1.0 / HD, RW_GN_EPS, ALU.mult, ALU.add), P_("VAR"))
                do("rv", lambda: e.reciprocal(f["s2"][:, :], f["s2"][:, :]), D_("VAR"))
                do("yg", lambda: stt(out=f["y"][:, :], in0=f["y"][:, :], scalar=col("rln_g"), in1=f["s2"][:, :],
                                     op0=ALU.mult, op1=ALU.mult), A_("root2"))
                do("yb", lambda: stt(out=f["y"][:, :], in0=f["y"][:, :], scalar=col("rln_b"), in1=f["bonus"][:, :],
                                     op0=ALU.add, op1=ALU.add), D_("yg"))
                do("yo", lambda: tt(f["t"][:, :], f["y"][:, :], row(gate, it), ALU.mult), D_("yb"))
                do("out", lambda: e.tensor_copy(row(o, it + o_at), f["t"][:, :]), D_("yo"))

        @block.scalar
        def _(e):
            with e.Fori(0, 4) as it:
                act.marked = 0

                def do(name, instruction, *needs):
                    for need in needs:
                        e.wait_ge(*need)
                    act.mark(instruction(), name)

                def copy_tiles(name, dst, *needs):
                    do(name, lambda: e.activation(dst, tiles4(name), ACT.Copy), pe.at(name, it), *needs)

                D_ = lambda s: dve.at(s, it)
                e.wait_ge(*pe.before(it))
                do("sq", lambda: e.activation(f["s1"][:, :], f["kk"][:, :], ACT.Square), D_("kk0"))
                do("root", lambda: e.activation(f["s2"][:, :], f["s2"][:, :], ACT.Sqrt), D_("rn"))
                do("Ew", lambda: e.activation(Ew[:, :], f["cw"][:, :], ACT.Exp), D_("scan"))
                do("En", lambda: e.activation(f["En"][:, :], f["cw"][:, :], ACT.Exp, scale=-1.0))
                do("Ex", lambda: e.activation(f["cx"][:, :], f["cx"][:, :], ACT.Exp), D_("cx"))
                for j in J:
                    src = tiles4("TA")[:, :, HD * j:HD * j + HD]
                    if j == 0:
                        e.wait_ge(*pe.at("TA", it))
                        e.activation(av[j][:, :, 0:HD], src, ACT.Copy)
                    else:
                        do("TA", lambda: e.activation(av[j][:, :, 0:HD], src, ACT.Copy))
                copy_tiles("TB", tok_b[:, :, :])
                copy_tiles("TK", tok_k[:, :, :])
                copy_tiles("TV", tok_v[:, :, :])
                for j in J:
                    copy_tiles(f"M2{j}", Ms[j][1][:, :, :])
                    do(f"AV{j}", lambda: e.activation(av[j][:, :, HD:P], bank_of(f"AV{j}")[:, 0:NT * HD].rearrange(
                        "p (t f) -> p t f", t=NT), ACT.Copy), pe.at(f"AV{j}", it))
                for n, power in enumerate((4, 8)):
                    for j in J:
                        copy_tiles(f"M{power}{j}", Ms[j][n % 2][:, :, :])
                        copy_tiles(f"T{power}{j}", Ts[j][n % 2][:, :, :])
                for j in J:
                    copy_tiles(f"M16{j}", Ms[j][0][:, :, :])
                for j in J:
                    copy_tiles(f"P{j}", PP[j][:, :, :])
                do("Y", lambda: e.activation(f["y"][:, :], bank_of("Y")[:, :], ACT.Copy), pe.at("Y", it))
                do("sq2", lambda: e.activation(f["s1"][:, :], f["y"][:, :], ACT.Square), D_("yc"))
                do("root2", lambda: e.activation(f["s2"][:, :], f["s2"][:, :], ACT.Sqrt), D_("rv"))
    for name, r in (("rw_dve", dve), ("rw_act", act), ("rw_pe", pe), ("rw_pool", pool)):
        assert r.marked == len(r.names)
        core.ended(**{name: 4 * len(r.names)})

def transformer_program(nc, A, out, stop=None, dump=None):
    with ExitStack() as ctx:
        core = Core(nc, ctx)
        scratch = nc.dram_tensor("rel_scratch", (8, EXTENDED), F32, kind="Internal").ap()
        core.out = out
        constants_stage(core, A)
        if stop in (None, "first"):
            first_block(core, A, scratch)
        if stop in (None, "even", "even_o"):
            even_layer(core, A, stop)
        if stop in (None, "odd"):
            odd_layer(core, A)
        if stop != "even_o":
            output_stage(core, core.x, out)


def output_stage(core, src, out):
    nc = core.nc
    with ExitStack() as c:
        rows = core.sb(c, "out_rows", [P, 2, D])
        bank = [core.ps(c, f"out_bank{b}", [P, T]) for b in range(4)]
        turned, copied, stored = core.sig("out_turned"), core.sig("out_copied"), core.sig("out_stored")
        block = c.enter_context(nc.Block())
        out_v = out[0].rearrange("(t p) d -> t p d", p=P)
        halves = [(t, h) for t in range(NT) for h in range(2)]

        @block.tensor
        def _(e):
            for n, (t, h) in enumerate(halves):
                if n >= 4:
                    e.wait_ge(*copied.at(n - 3))
                for k in range(4):
                    last = e.transpose(bank[n % 4][:, k * P:(k + 1) * P], src[:, 4 * h + k, t * P:(t + 1) * P],
                                       core.ident[:, :])
                last.then_inc(turned.sem, 1)

        @block.scalar
        def _(e):
            for n, (t, h) in enumerate(halves):
                e.wait_ge(*turned.at(n + 1))
                if t >= 2:
                    e.wait_ge(*stored.at(16 * (t - 1)))
                e.activation(rows[:, t % 2, h * T:(h + 1) * T], bank[n % 4][:, :], ACT.Copy).then_inc(copied.sem, 1)

        @block.sync
        def _(e):
            for t in range(NT):
                e.wait_ge(*copied.at(2 * t + 2))
                if t >= 1:
                    e.wait_ge(*stored.at(16 * t))
                e.dma_start(out_v[t], rows[:, t % 2, :]).then_inc(stored.sem, 16)
            e.wait_ge(*stored.at(16 * NT))
    core.ended(out_turned=2 * NT, out_copied=2 * NT, out_stored=16 * NT)


def first_block(core, A, scratch):
    w_in = A["w_in"][0]
    fox, width = 0, 4 * P
    chk = 3 * width + 8
    gate = chk + 3 * width
    with ExitStack() as c:
        o = core.sb(c, "o", [P, 2 * 4, T])
        activations(core, c)
        norm_stage(core, "rms", core.x, KD, g=core.v["norm1"], eps=1e-6)
        with ExitStack() as a:
            qkv = core.sb(a, "qkv", [P, 12, T])
            with ExitStack() as f:
                fa = core.sb(f, "fa", [P, 1, T])
                neg_c = core.sb(f, "neg_c", [P, 8, T])
                gemm_stage(core, [
                    Job(6, columns(w_in, fox), act_tiles(core), keep(qkv)),
                    Job(1, columns(w_in, 3 * width), act_tiles(core), keep(fa, 1), tiles=1)])
                forget_stage(core, fa[:, 0, :], A["forget_bias"], neg_c)
                attention(core, 2, qkv, o, 0, core.causal_mask, forget_bias_add(neg_c, 0.125))
            with ExitStack() as f:
                near = core.sb(f, "near", [P, 8, WINDOW])
                far = core.sb(f, "far", [P, 8])
                gemm_stage(core, [Job(6, columns(w_in, chk), act_tiles(core), keep(qkv))])
                relative_stage(core, A["rel_bias"], scratch, near, far)
                attention(core, 2, qkv, o, 4, core.chunk_mask, relative_bias_add(near, far, 0.125))
        gates = core.sb(c, "gates", [P, 2 * KD, T])
        gemm_stage(core, [Job(KD, columns(w_in, gate), act_tiles(core), keep_sigmoid(gates))])
        norm_stage(core, "split", o, KD)
        views = [A[n][0].rearrange("(k p) n -> p k n", p=P) for n in ("w_branch_a", "w_branch_b")]
        gemm_stage(core, [Job(KD, lambda u, s, t: views[t][:, :, bass.ds(u * P, P)],
                              lambda s, t, k: (core.AH[:, 4 * t + k, :], core.AL[:, 4 * t + k, :]),
                              gated_sum(core, gates), subs=(4,))])
        norm_stage(core, "split", gates, KD)
        gemm_stage(core, [Job(4, columns(A["w_out"][0], 0), act_tiles(core), residual(core))])
    with ExitStack() as c:
        activations(core, c)
        norm_stage(core, "rms", core.x, KD, g=core.v["norm2"], eps=1e-6)
        tiles = FFN1 // P // 2
        hid_hi = core.sb(c, "hid_hi", [P, tiles, T], F32R)
        hid_lo = core.sb(c, "hid_lo", [P, tiles, T], F32R)
        w_up, w_down = A["w_up"][0], A["w_down"][0]
        jobs = []
        for half in range(2):
            jobs.append(Job(tiles // 2, columns(w_up, half * tiles * P), act_tiles(core),
                            relu_squared(core, hid_hi, hid_lo)))
            jobs.append(Job(4, columns(w_down[half * tiles * P:(half + 1) * tiles * P], 0),
                            lambda s, t, k: (hid_hi[:, KD * s + k, :], hid_lo[:, KD * s + k, :]),
                            residual(core), subs=(KD, KD), after=True))
        gemm_stage(core, jobs)
        norm_stage(core, "rms", core.x, KD, out32=core.x, g=core.v["final"], eps=1e-6, parts=False)


def swiglu_stage(core, A, layer):
    half_tiles = FFN2 // P // 2
    with ExitStack() as c:
        hid_hi = core.sb(c, "hid_hi", [P, half_tiles, T], F32R)
        hid_lo = core.sb(c, "hid_lo", [P, half_tiles, T], F32R)
        w_up, w_down = A["ffn_w_gate_up_2"][layer], A["ffn_w_down_2"][layer]
        jobs = []
        for half in range(2):
            first = half * half_tiles * P
            jobs.append(Job(half_tiles, columns(w_up, first, tile_step=FFN2, unit_step=P), act_tiles(core),
                            silu_times(core, hid_hi, hid_lo)))
            jobs.append(Job(4, columns(w_down[first:first + half_tiles * P], 0),
                            lambda s, t, k: (hid_hi[:, KD * s + k, :], hid_lo[:, KD * s + k, :]),
                            residual(core, DN_ALPHA if half == 0 else 1.0), subs=(KD, half_tiles - KD), after=True))
        gemm_stage(core, jobs)


def post_norm(core, layer, half, parts):
    norm_stage(core, "ln", core.x, KD, out32=core.x, g=core.v[f"ln_g{layer}{half}"], b=core.v[f"ln_b{layer}{half}"],
               eps=1e-5, parts=parts)


def mix_out_and_ffn(core, A, layer, o, w_out):
    with ExitStack() as c:
        activations(core, c)
        norm_stage(core, "split", o, KD)
        gemm_stage(core, [Job(4, columns(w_out, 0), act_tiles(core), residual(core, DN_ALPHA))])
        post_norm(core, layer, 0, True)
        swiglu_stage(core, A, layer)
        post_norm(core, layer, 1, False)


def even_layer(core, A, stop=None):
    w_in = A["even_w_in_2"][0]
    with ExitStack() as c:
        o = core.sb(c, "o", [P, KD, T])
        with ExitStack() as r:
            gla = core.sb(r, "gla", [P, 12, T])
            glr = core.sb(r, "glr", [P, 1, T])
            with ExitStack() as g:
                activations(core, g)
                norm_stage(core, "split", core.x, KD)
                gemm_stage(core, [Job(6, columns(w_in, 0), act_tiles(core), keep(gla)),
                                  Job(1, columns(w_in, 12 * P), act_tiles(core), keep(glr, 1), tiles=1)])
            gla_stage(core, A, gla, glr[:, 0, :], o)
        with ExitStack() as r:
            rw = core.sb(r, "rw", [P, 15, T])
            decay, rate, gate = (core.sb(r, f"rw_{s}", [P, 4, T]) for s in ("decay", "rate", "gate"))
            with ExitStack() as g:
                activations(core, g)
                norm_stage(core, "split", core.x, KD)
                gemm_stage(core, [Job(7, columns(w_in, GLA_IN), act_tiles(core), keep(rw)),
                                  Job(1, columns(w_in, GLA_IN + RW_IN - P), act_tiles(core), keep(rw[:, 14:15, :], 1),
                                      tiles=1)])
            rwkv_prepare_stage(core, A, rw, decay, rate, gate)
            rwkv_stage(core, rw, decay, rate, gate, o, 4)
        if stop == "even_o":
            with ExitStack() as r:
                output_stage(core, o, core.out)
            return
        mix_out_and_ffn(core, A, 0, o, A["even_w_out_2"][0])


MLA_H, MLA_Q, MLA_KV, ROPE = 16, 768, 256, 32
TWO_PI = (6.28125, 8117 / 4194304, 6.283185307179586 - 6.28125 - 8117 / 4194304)
ROUND = 1.5 * 2 ** 23
PI_IN = 3.1415925


def rope_stage(core, A, qr, k_pe):
    nc = core.nc
    tiles = [qr[:, n, :] for n in range(4)] + [k_pe]
    dve_names = (["pos", "ang", "n", "n2", "r1", "r2", "r3", "c", "over", "c2", "sin_in", "cos_in"] +
                 [f"{s}{n}" for n in range(5) for s in ("sin", "cos", "sum")])
    with ExitStack() as c:
        pos_i = core.sb(c, "pos_i", [P, T], I32)
        freq = core.sb(c, "freq", [P, 1])
        ang, turns, cosine, over, sine = (core.sb(c, f"rope_{s}", [P, T]) for s in ("ang", "n", "cos", "over", "sin"))
        parts = core.sb(c, "rope_parts", [P, 2, T])
        swap = core.sb(c, "rope_swap", [P, P])
        bank = [core.ps(c, f"rope_bank{n}", [P, T]) for n in range(5)]
        loaded, swapped, built, table = (core.sig(f"rope_{s}") for s in ("loaded", "swapped", "built", "table"))
        dve = Results(core.sig("rope_dve"), dve_names)
        block = c.enter_context(nc.Block())

        @block.sync
        def _(e):
            e.dma_start(pos_i[:, :], A["positions_2"][0].partition_broadcast(P)).then_inc(loaded.sem, 16)
            e.dma_start(freq[:, :], A["rope_freq"]).then_inc(loaded.sem, 16)

        @block.gpsimd
        def _(e):
            chain = Chain(e, built)
            chain.link(e.memset(swap[:, :], 0.0))
            pairs = swap[:, :].rearrange("p (i two) -> p two i", two=2)
            for two, value in ((1, 1.0), (0, -1.0)):
                chain.link(e.affine_select(out=pairs[:, two, :], in_=pairs[:, two, :], compare_op=ALU.not_equal,
                                           fill=value, base=two - 1, pattern=[[-2, P // 2]], channel_multiplier=1))

        @block.tensor
        def _(e):
            e.wait_ge(*built.at(3))
            for n, x in enumerate(tiles):
                e.matmul(bank[n][:, :], swap[:, :], x, start=True, stop=True).then_inc(swapped.sem, 1)

        @block.scalar
        def _(e):
            e.wait_ge(*dve.at("cos_in"))
            e.activation(sine[:, :], ang[:, :], ACT.Sin).then_inc(table.sem, 1)
            e.activation(cosine[:, :], cosine[:, :], ACT.Sin).then_inc(table.sem, 1)

        @block.vector
        def _(e):
            def do(name, instruction):
                dve.mark(instruction, name)
                e.wait_ge(*dve.at(name))
            ts, tt, stt = e.tensor_scalar, e.tensor_tensor, e.scalar_tensor_tensor
            e.wait_ge(*loaded.at(32))
            do("pos", e.tensor_copy(ang[:, :], pos_i[:, :]))
            do("ang", ts(ang[:, :], ang[:, :], freq[:, 0:1], None, ALU.mult))
            do("n", ts(turns[:, :], ang[:, :], 1.0 / (2 * np.pi), ROUND, ALU.mult, ALU.add))
            do("n2", ts(turns[:, :], turns[:, :], -ROUND, None, ALU.add))
            for n in range(3):
                do(f"r{n + 1}", stt(out=ang[:, :], in0=turns[:, :], scalar=-TWO_PI[n], in1=ang[:, :], op0=ALU.mult,
                                    op1=ALU.add))
            do("c", ts(cosine[:, :], ang[:, :], np.pi / 2, None, ALU.add))
            do("over", ts(over[:, :], cosine[:, :], np.pi, None, ALU.is_gt))
            do("c2", stt(out=cosine[:, :], in0=over[:, :], scalar=-2 * np.pi, in1=cosine[:, :], op0=ALU.mult, op1=ALU.add))
            do("sin_in", ts(ang[:, :], ang[:, :], PI_IN, -PI_IN, ALU.min, ALU.max))
            do("cos_in", ts(cosine[:, :], cosine[:, :], PI_IN, -PI_IN, ALU.min, ALU.max))
            e.wait_ge(*table.at(2))
            for n, x in enumerate(tiles):
                e.wait_ge(*swapped.at(n + 1))
                do(f"sin{n}", tt(parts[:, 0, :], bank[n][:, :], sine[:, :], ALU.mult))
                do(f"cos{n}", tt(parts[:, 1, :], x, cosine[:, :], ALU.mult))
                do(f"sum{n}", tt(x, parts[:, 0, :], parts[:, 1, :], ALU.add))
    core.ended(rope_loaded=32, rope_built=3, rope_swapped=5, rope_table=2, rope_dve=len(dve_names))


def head_columns(w, first, width):
    heads = P // width
    return lambda u, s, t, i: w[:, :, bass.ds(u * 2 * heads + (t * heads + i), 1), first:first + width]\
        .rearrange("p k o n -> p k (o n)")


def odd_layer(core, A):
    w_in = A["mla_w_in_2"][0].rearrange("(k p) n -> p k n", p=P)
    q_b = A["mla_w_q_b_2"][0].rearrange("(k p) (h n) -> p k h n", p=P, h=MLA_H)
    kv_b = A["mla_w_kv_b_2"][0].rearrange("(k p) (h n) -> p k h n", p=P, h=MLA_H)
    with ExitStack() as c:
        o = core.sb(c, "o", [P, KD, T])
        with ExitStack() as r:
            qn, kn, v = (core.sb(r, f"mla_{s}", [P, KD, T]) for s in ("qn", "kn", "v"))
            qr = core.sb(r, "mla_qr", [P, 4, T])
            k_pe = core.sb(r, "mla_k_pe", [P, 1, T])
            with ExitStack() as g:
                activations(core, g)
                norm_stage(core, "split", core.x, KD)
                gemm_stage(core, [Job(4, columns(A["mla_w_in_2"][0], 0), act_tiles(core), keep(o)),
                                  Job(1, lambda u, s, t, i: w_in[:, :, MLA_Q + MLA_KV:], act_tiles(core),
                                      keep(k_pe, 1), tiles=1, pieces=4)])
                norm_stage(core, "rms", o[:, 0:6, :], 6, g=core.v["q_g"], eps=1e-6, features=MLA_Q)
                norm_stage(core, "rms", o[:, 6:8, :], 2, at=6, g=core.v["kv_g"], eps=1e-6, features=MLA_KV)
                gemm_stage(core, [
                    Job(4, head_columns(q_b, 0, HD), act_tiles(core), keep(qn), subs=(6,), pieces=2),
                    Job(2, head_columns(q_b, HD, ROPE), act_tiles(core), keep(qr), subs=(6,), pieces=4),
                    Job(4, head_columns(kv_b, 0, HD), act_tiles(core, 6), keep(kn), subs=(2,), pieces=2),
                    Job(4, head_columns(kv_b, HD, HD), act_tiles(core, 6), keep(v), subs=(2,), pieces=2)])
            rope_stage(core, A, qr, k_pe[:, 0, :])

            def two(x):
                return lambda it: x[:, bass.ds(it * 2, 2), :]
            attention_stage(core, 4, two(qn), two(kn), two(v),
                            lambda it, a: o[:, bass.ds(it * 2 + a, 1), :].rearrange("p o t -> p (o t)"),
                            (HD + ROPE) ** -0.5, core.chunk_mask,
                            rope=(lambda it: qr[:, bass.ds(it, 1), :].rearrange("p o t -> p (o t)"), k_pe[:, 0, :]))
        mix_out_and_ffn(core, A, 1, o, A["mla_w_out_2"][0])


def attention(core, quads, qkv, o, o_at, mask, bias):
    def tiles(first):
        return lambda it: qkv[:, bass.ds(it * 2 + first, 2), :]
    attention_stage(core, quads, tiles(0), tiles(4), tiles(8),
                    lambda it, a: o[:, bass.ds(it * 2 + (o_at + a), 1), :].rearrange("p o t -> p (o t)"),
                    0.125, mask, bias)



def kernel(**inputs):
    import numpy as _np
    import concourse.bacc as _bacc
    from concourse import mybir as _mybir
    from concourse.bass_utils import run_bass_kernel_spmd as _run

    nc = _bacc.Bacc("TRN2", target_bir_lowering=False, num_devices=1)
    arrays, aps = {}, {}
    for name in inputs:
        a = _np.ascontiguousarray(inputs[name])
        arrays[f"in_{name}"] = a
        aps[name] = nc.dram_tensor(f"in_{name}", a.shape, _mybir.dt.from_np(a.dtype), kind="ExternalInput").ap()
    arrays["in_rope_freq"] = _np.array([[10000.0 ** -(p % ROPE // 2 * 2 / ROPE)] for p in range(P)], _np.float32)
    aps["rope_freq"] = nc.dram_tensor("in_rope_freq", (P, 1), F32, kind="ExternalInput").ap()
    out = nc.dram_tensor("out_x", (1, T, D), F32, kind="ExternalOutput").ap()
    transformer_program(nc, aps, out)
    return _run(nc, [arrays], core_ids=[0]).results[0]["out_x"]
```

```python
from contextlib import ExitStack

import numpy as np

import concourse.bass as bass
from concourse import mybir

F32 = mybir.dt.float32
F32R = mybir.dt.float32r
BF16 = mybir.dt.bfloat16
I32 = mybir.dt.int32
ACT = mybir.ActivationFunctionType
ALU = mybir.AluOpType
AX = mybir.AxisListType

P = 128
T = 512
D = 1024
KD = D // P
NT = T // P
HD = 64
C32 = 32
NCH = T // C32
CPT = P // C32
MASKED = -1e30
FFN1 = 4096
FFN2 = 2816
DN_ALPHA = 4.0 ** 0.25
GLA_IN, RW_IN = 1552, 1824
MAX_REL = 128


class Signal:

    def __init__(self, sem):
        self.sem, self.base = sem, 0

    def at(self, n):
        return self.sem, n + self.base


class Chain:

    def __init__(self, eng, signal, before=0):
        self.eng, self.counter, self.before, self.n = eng, signal, before, 0

    def link(self, instruction):
        self.n += 1
        instruction.then_inc(self.counter.sem, 1)
        self.eng.wait_ge(*self.counter.at(self.n + self.before))


class Core:

    def __init__(self, nc, ctx):
        self.nc, self.ctx, self.counters, self.stage_no = nc, ctx, {}, 0

    def sb(self, ctx, name, shape, dtype=F32):
        return ctx.enter_context(self.nc.sbuf_tensor(f"{name}_{self.stage_no}", shape, dtype))

    def ps(self, ctx, name, shape):
        return ctx.enter_context(self.nc.psum_tensor(f"{name}_{self.stage_no}", shape, F32))

    def sig(self, name):
        if name not in self.counters:
            self.counters[name] = Signal(self.ctx.enter_context(self.nc.semaphore(name)))
        return self.counters[name]

    def ended(self, **counts):
        for name, n in counts.items():
            self.counters[name].base += n
        self.stage_no += 1


def spread(ap, count, axis=1):
    shape = list(ap.shape)
    shape.insert(axis, count)
    return ap.unsqueeze(axis).broadcast_to(shape)



COUNT_FROM = {"at_scored": 33, "at_maxed": 33, "at_exped": 33, "at_p_turned": 33, "at_p_ready": 33, "at_pv_done": 33,
              "at_v_turned": 5, "at_v_ready": 5, "at_o_scaled": 5, "at_o_turned": 5, "at_o_kept": 5,
              "rw_pe": 1, "rw_dve": 1, "rw_act": 1}


def constants_stage(core, A):
    nc, ctx = core.nc, core.ctx
    core.x = core.sb(ctx, "x", [P, KD, T])
    core.ident = core.sb(ctx, "ident", [P, P])
    core.ident16 = core.sb(ctx, "ident16", [P, P], BF16)
    core.ones = core.sb(ctx, "ones", [P, P])
    core.head_ones = core.sb(ctx, "head_ones", [P, P])
    core.head_ident = core.sb(ctx, "head_ident", [P, HD])
    core.causal_mask = core.sb(ctx, "causal_mask", [P, P], BF16)
    core.chunk_mask = core.sb(ctx, "chunk_mask", [P, P], BF16)
    core.tri = core.sb(ctx, "tri", [P, 3, P])
    core.in_chunk = core.sb(ctx, "in_chunk", [P, CPT, HD])
    core.scan_keep = core.sb(ctx, "scan_keep", [P, T])
    core.pick_pair_head = core.sb(ctx, "pick_pair_head", [P, 4, P])

    vectors = [("norm1", A["norm1"][0]), ("norm2", A["norm2"][0]), ("final", A["final_norm"]),
               ("gla_b", A["gla_gate_b_2"][0]), ("gla_g", A["gla_norm_g_2"][0]),
               ("w0", A["rwkv_w0_2"][0]), ("a0", A["rwkv_a0_2"][0]), ("k_k", A["rwkv_k_k_2"][0]),
               ("k_a", A["rwkv_k_a_2"][0]), ("r_k", A["rwkv_r_k_2"][0].rearrange("h n -> (h n)")),
               ("rln_g", A["rwkv_ln_g_2"][0]), ("rln_b", A["rwkv_ln_b_2"][0]),
               ("mu", A["rwkv_mu_2"][0][0:14 * P]), ("mu_tail", A["rwkv_mu_2"][0][RW_IN - P:RW_IN]),
               ("q_g", A["mla_q_norm_g_2"][0]), ("kv_g", A["mla_kv_norm_g_2"][0])]
    for layer in range(2):
        for half in range(2):
            vectors += [(f"ln_g{layer}{half}", A["ln_g_2"][layer, half]),
                        (f"ln_b{layer}{half}", A["ln_b_2"][layer, half])]
    places, at = [], 0
    for name, src in vectors:
        n = src.shape[0] // P
        if at % P + n > P:
            at = -(-at // P) * P
        places.append((name, src, at, n))
        at += n
    row_tiles = -(-at // P)
    core.vec = core.sb(ctx, "vec", [P, row_tiles * P])
    core.v = {name: core.vec[:, at:at + n] for name, _, at, n in places}

    with ExitStack() as c:
        x_tok = core.sb(c, "x_tok", [P, NT, D])
        rows = core.sb(c, "rows", [P, row_tiles, P])
        bank = [core.ps(c, f"bank{b}", [P, T]) for b in range(2)]
        loaded_x, loaded_rows = core.sig("loaded_x"), core.sig("loaded_rows")
        masks, rows_zero = core.sig("masks"), core.sig("rows_zero")
        turned, copied = core.sig("turned"), core.sig("copied")
        block = c.enter_context(nc.Block())

        @block.sync
        def _(e):
            e.dma_start(x_tok[:, :, :], A["x"][0].rearrange("(t p) d -> p t d", p=P)).then_inc(loaded_x.sem, 16)
            e.wait_ge(*rows_zero.at(1))
            for _, src, at, n in places:
                e.dma_start(rows[at % P:at % P + n, at // P, :], src.rearrange("(k p) -> k p", p=P))\
                 .then_inc(loaded_rows.sem, 16)

        @block.gpsimd
        def _(e):
            for name, n in COUNT_FROM.items():
                e.sem_inc(core.sig(name).sem, n)
            chain = Chain(e, masks)
            e.memset(rows[:, :, :], 0.0).then_inc(rows_zero.sem, 1)
            chain.link(e.memset(core.ident[:, :], 0.0))
            chain.link(e.affine_select(out=core.ident[:, :], in_=core.ident[:, :], compare_op=ALU.not_equal,
                                       fill=1.0, base=0, pattern=[[-1, P]], channel_multiplier=1))
            chain.link(e.tensor_copy(core.ident16[:, :], core.ident[:, :]))
            chain.link(e.memset(core.ones[:, :], 1.0))
            chain.link(e.memset(core.head_ones[:, :], 0.0))
            for h in range(2):
                part = core.head_ones[HD * h:HD * h + HD, HD * h:HD * h + HD]
                chain.link(e.memset(part, 1.0))
            chain.link(e.tensor_tensor(core.head_ident[:, :], core.ident[:, 0:HD], core.ident[:, HD:P], ALU.add))
            chain.link(e.memset(core.causal_mask[:, :], 0.0))
            chain.link(e.affine_select(out=core.causal_mask[:, :], in_=core.causal_mask[:, :],
                                       compare_op=ALU.is_ge, fill=MASKED, base=0,
                                       pattern=[[-1, P]], channel_multiplier=1))
            chain.link(e.memset(core.chunk_mask[:, :], 0.0))
            chain.link(e.memset(core.chunk_mask[0:HD, HD:P], MASKED))
            chain.link(e.memset(core.scan_keep[:, :], 1.0))
            chain.link(e.memset(core.scan_keep[:, 0:T:C32], 0.0))
            chain.link(e.memset(core.in_chunk[:, :, :], 1.0))
            chain.link(e.affine_select(out=core.in_chunk[:, :, :], in_=core.in_chunk[:, :, :],
                                       compare_op=ALU.is_ge, fill=0.0, base=0,
                                       pattern=[[-C32, CPT], [0, HD]], channel_multiplier=1))
            chain.link(e.affine_select(out=core.in_chunk[:, :, :], in_=core.in_chunk[:, :, :],
                                       compare_op=ALU.is_ge, fill=0.0, base=C32 - 1,
                                       pattern=[[C32, CPT], [0, HD]], channel_multiplier=-1))
            chain.link(e.memset(core.pick_pair_head[:, :, :], 0.0))
            pick = core.pick_pair_head[:, :, :].rearrange("p n (j f) -> p n j f", j=2)
            chain.link(e.affine_select(out=pick, in_=pick, compare_op=ALU.not_equal, fill=1.0, base=0,
                                       pattern=[[-32, 4], [-16, 2], [0, HD]], channel_multiplier=1))
            for n, (base, step) in enumerate([(-1, 1), (0, 1), (-1, -1)]):
                tri = core.tri[:, n, :].rearrange("p (c f) -> p c f", f=C32)
                chain.link(e.tensor_copy(tri, core.in_chunk[:, :, 0:C32]))
                chain.link(e.affine_select(out=core.tri[:, n, :], in_=core.tri[:, n, :], compare_op=ALU.is_ge,
                                           fill=0.0, base=base, pattern=[[step, P]], channel_multiplier=-step))
            core.n_masks = chain.n

        @block.vector
        def _(e):
            e.sem_inc(core.sig("w_lo_ready").sem, 2)
            e.sem_inc(core.sig("epi_dve_done").sem, 2)

        @block.tensor
        def _(e):
            e.sem_inc(core.sig("w_used").sem, 2)
            e.wait_ge(*masks.at(core.n_masks))
            e.wait_ge(*loaded_rows.at(16 * len(places)))
            for r in range(row_tiles):
                last = e.transpose(bank[0][:, r * P:(r + 1) * P], rows[:, r, :], core.ident[:, :])
            last.then_inc(turned.sem, 1)
            e.wait_ge(*loaded_x.at(16))
            for k in range(KD):
                if k >= 1:
                    e.wait_ge(*copied.at(k))
                for t in range(NT):
                    last = e.transpose(bank[(k + 1) % 2][:, t * P:(t + 1) * P], x_tok[:, t, k * P:(k + 1) * P],
                                       core.ident[:, :])
                last.then_inc(turned.sem, 1)

        @block.scalar
        def _(e):
            e.sem_inc(core.sig("w_hi_ready").sem, 2)
            e.sem_inc(core.sig("epi_act_done").sem, 2)
            e.wait_ge(*turned.at(1))
            e.activation(core.vec[:, :], bank[0][:, 0:row_tiles * P], ACT.Copy).then_inc(copied.sem, 1)
            for k in range(KD):
                e.wait_ge(*turned.at(k + 2))
                e.activation(core.x[:, k, :], bank[(k + 1) % 2][:, :], ACT.Copy).then_inc(copied.sem, 1)
    core.ended(**COUNT_FROM)
    core.ended(loaded_x=16, loaded_rows=16 * len(places), masks=core.n_masks, rows_zero=1,
               turned=KD + 1, copied=KD + 1)



def activations(core, ctx):
    core.AH = core.sb(ctx, "act_hi", [P, KD, T], F32R)
    core.AL = core.sb(ctx, "act_lo", [P, KD, T], F32R)


def norm_stage(core, kind, src, n, out32=None, at=0, g=None, b=None, eps=0.0, features=D, parts=True,
               gemm=None):
    nc = core.nc
    with ExitStack() as c:
        if kind == "split":
            y = src
        else:
            y = core.sb(c, "norm_y", [P, n, T]) if out32 is None else out32
            squares = core.sb(c, "squares", [P, 2, T])
            root = core.sb(c, "root", [P, 3, T])
        sums = core.ps(c, "sums", [P, T])
        mean = core.ps(c, "mean", [P, T])
        squared, summed = core.sig("norm_squared"), core.sig("norm_summed")
        centred, var_ready = core.sig("norm_centred"), core.sig("norm_var")
        rooted, scaled, hi_ready = core.sig("norm_rooted"), core.sig("norm_scaled"), core.sig("norm_hi")
        own = core.sig("norm_chain")
        block = c.enter_context(nc.Block())
        taken = y if kind == "ln" else src

        if gemm:
            @block.sync
            def _(e):
                gemm.first_loads(e)

        @block.tensor
        def _(e):
            if kind == "split":
                return
            if kind == "ln":
                for k in range(n):
                    last = e.matmul(mean[:, :], core.ones[:, :], src[:, k, :], start=(k == 0), stop=(k == n - 1))
                last.then_inc(summed.sem, n)
            for k in range(n):
                e.wait_ge(*squared.at(k + 1))
                e.matmul(sums[:, :], core.ones[:, :], squares[:, k % 2, :], start=(k == 0), stop=(k == n - 1))\
                 .then_inc(summed.sem, 1)

        offset = n if kind == "ln" else 0

        @block.scalar
        def _(e):
            if kind != "split":
                for k in range(n):
                    if kind == "ln":
                        e.wait_ge(*centred.at(k + 1))
                    if k >= 2:
                        e.wait_ge(*summed.at(offset + k - 1))
                    e.activation(squares[:, k % 2, :], taken[:, k, :], ACT.Square).then_inc(squared.sem, 1)
                e.wait_ge(*var_ready.at(1))
                e.activation(root[:, 2, :], root[:, 1, :], ACT.Sqrt).then_inc(rooted.sem, 1)
            for k in range(n if parts else 0):
                if kind != "split":
                    e.wait_ge(*scaled.at(k + 1))
                e.activation(core.AH[:, at + k, :], y[:, k, :], ACT.Copy).then_inc(hi_ready.sem, 1)
            if gemm:
                gemm.first_hi(e)

        @block.vector
        def _(e):
            chain = Chain(e, own)
            if kind == "ln":
                e.wait_ge(*summed.at(n))
                chain.link(e.tensor_scalar(root[:, 0, :], mean[:, :], 1.0 / features, None, ALU.mult))
                for k in range(n):
                    e.tensor_tensor(y[:, k, :], src[:, k, :], root[:, 0, :], ALU.subtract).then_inc(centred.sem, 1)
            if kind != "split":
                e.wait_ge(*summed.at(offset + n))
                chain.link(e.tensor_scalar(root[:, 0, :], sums[:, :], 1.0 / features, eps, ALU.mult, ALU.add))
                e.reciprocal(root[:, 1, :], root[:, 0, :]).then_inc(var_ready.sem, 1)
                e.wait_ge(*rooted.at(1))
                for k in range(n):
                    ins = e.scalar_tensor_tensor(out=y[:, k, :], in0=taken[:, k, :], scalar=g[:, k:k + 1],
                                                 in1=root[:, 2, :], op0=ALU.mult, op1=ALU.mult)
                    if b is not None:
                        chain.link(ins)
                        ins = e.tensor_scalar(y[:, k, :], y[:, k, :], b[:, k:k + 1], None, ALU.add)
                    ins.then_inc(scaled.sem, 1)
            for k in range(n if parts else 0):
                e.wait_ge(*hi_ready.at(k + 1))
                e.tensor_tensor(core.AL[:, at + k, :], y[:, k, :], core.AH[:, at + k, :].bitcast(F32), ALU.subtract)
            if gemm:
                gemm.first_lo(e)
            core.n_chain = chain.n

    norm = kind != "split"
    core.ended(norm_squared=n * norm, norm_summed=(n + offset) * norm, norm_centred=offset,
               norm_var=norm, norm_rooted=norm, norm_scaled=n * norm, norm_hi=n * parts, norm_chain=core.n_chain)



UN = 2 * P


class Job:

    def __init__(self, units, load, act, epilogue, subs=(KD,), tiles=2, pieces=1, after=False):
        self.units, self.load, self.act, self.tiles, self.pieces, self.after = units, load, act, tiles, pieces, after
        self.epi_act, self.epi_dve, self.links = epilogue
        self.subs, self.S = list(subs), len(subs)


def signal_after(e, instruction, signal):
    if instruction is None:
        e.sem_inc(signal.sem, 1)
    else:
        instruction.then_inc(signal.sem, 1)


def columns(w, first=0, tile_step=P, unit_step=UN):
    view = w.rearrange("(k p) n -> p k n", p=P)

    def load(u, s, t):
        n = min(KD, w.shape[0] // P - KD * s)
        return view[:, KD * s:KD * s + n, bass.ds(u * unit_step + (first + t * tile_step), P)]
    return load


def act_tiles(core, at=0):
    return lambda s, t, k: (core.AH[:, at + k, :], core.AL[:, at + k, :])



def keep(dst, tiles=2, scale=1.0):
    def act(e, u, acc, slot):
        return e.activation(dst[:, bass.ds(u * tiles, tiles), 0:T // 2], acc[:, 0:tiles, 0:T // 2], ACT.Copy)

    def dve(e, chain, u, acc, slot):
        return e.tensor_copy(dst[:, bass.ds(u * tiles, tiles), T // 2:T], acc[:, 0:tiles, T // 2:T])
    return act, dve, 0


def keep_sigmoid(dst):
    def act(e, u, acc, slot):
        return e.activation(dst[:, bass.ds(u * 2, 2), :], acc[:, :, :], ACT.Sigmoid)
    return act, lambda e, chain, u, acc, slot: None, 0


def residual(core, alpha=1.0):
    def dve(e, chain, u, acc, slot):
        x = core.x[:, bass.ds(u * 2, 2), :]
        return e.scalar_tensor_tensor(out=x, in0=x, scalar=alpha, in1=acc[:, :, :], op0=ALU.mult, op1=ALU.add)
    return lambda e, u, acc, slot: None, dve, 0


def relu_squared(core, hid_hi, hid_lo):
    def act(e, u, acc, slot):
        return e.activation(core.tmp_act[:, slot, :, :], acc[:, :, :], ACT.Relu)

    def dve(e, chain, u, acc, slot):
        r, y = core.tmp_act[:, slot, :, :], core.tmp_dve[:, :, :]
        hi, lo = hid_hi[:, bass.ds(u * 2, 2), :], hid_lo[:, bass.ds(u * 2, 2), :]
        chain.link(e.tensor_tensor(y, r, r, ALU.mult))
        chain.link(e.tensor_copy(hi, y))
        return e.tensor_tensor(lo, y, hi.bitcast(F32), ALU.subtract)
    return act, dve, 2


def silu_times(core, hid_hi, hid_lo):
    def act(e, u, acc, slot):
        return e.activation(core.tmp_act[:, slot, 0, :], acc[:, 0, :], ACT.Silu)

    def dve(e, chain, u, acc, slot):
        y = core.tmp_dve[:, 0, :]
        hi, lo = hid_hi[:, bass.ds(u, 1), :], hid_lo[:, bass.ds(u, 1), :]
        chain.link(e.tensor_tensor(y, core.tmp_act[:, slot, 0, :], acc[:, 1, :], ALU.mult))
        chain.link(e.tensor_copy(hi, core.tmp_dve[:, 0:1, :]))
        return e.tensor_tensor(lo, core.tmp_dve[:, 0:1, :], hi.bitcast(F32), ALU.subtract)
    return act, dve, 2


def gated_sum(core, gates):
    def dve(e, chain, u, acc, slot):
        g_a, g_b = gates[:, bass.ds(u, 1), :], gates[:, bass.ds(u + KD, 1), :]
        chain.link(e.tensor_tensor(core.tmp_dve[:, 0:1, :], g_b, acc[:, 1:2, :], ALU.mult))
        chain.link(e.tensor_tensor(g_a, g_a, acc[:, 0:1, :], ALU.mult))
        return e.tensor_tensor(g_a, g_a, core.tmp_dve[:, 0:1, :], ALU.add)
    return lambda e, u, acc, slot: None, dve, 2


class Gemm:
    RING = 2

    def __init__(self, core, ctx, jobs):
        R = self.RING
        self.nc, self.jobs, self.ahead = core.nc, jobs, False
        self.w32 = core.sb(ctx, "w32", [P, R, KD, UN])
        self.w_hi = [core.sb(ctx, f"w_hi{r}", [P, KD, UN], F32R) for r in range(R)]
        self.w_lo = [core.sb(ctx, f"w_lo{r}", [P, KD, UN], F32R) for r in range(R)]
        self.landed = [core.sig(f"w_landed{r}") for r in range(R)]
        self.hi, self.lo = core.sig("w_hi_ready"), core.sig("w_lo_ready")
        self.used = core.sig("w_used")
        U = G = links = 0
        loads = [0] * R
        for j in jobs:
            j.U0, j.G0 = U, G
            j.base = list(loads)
            j.C0 = links
            links += j.units * j.links
            for n in range(j.units * j.S):
                loads[(G + n) % R] += 16 * j.tiles * j.pieces
            U += j.units
            G += j.units * j.S
        self.all_units, self.all_parts, self.all_links, self.loads = U, G, links, loads

    def landed_at(self, j, it, part):
        slot = (j.G0 + part) % self.RING
        first = (slot - j.G0) % self.RING
        each = 16 * j.tiles * j.pieces
        return slot, it * (j.S * each) + (j.base[slot] + ((part - first) // self.RING + 1) * each)

    def upcoming(self, n, k):
        while n < len(self.jobs):
            j = self.jobs[n]
            if k < j.units * j.S:
                return j, k // j.S, k % j.S
            n, k = n + 1, k - j.units * j.S
        return None

    def load(self, e, j, u, s, slot):
        wide = P // j.pieces
        for t in range(j.tiles):
            for i in range(j.pieces):
                src = j.load(u, s, t) if j.pieces == 1 else j.load(u, s, t, i)
                e.dma_start(self.w32[:, slot, 0:j.subs[s], t * P + i * wide:t * P + (i + 1) * wide], src)\
                 .then_inc(self.landed[slot].sem, 16)

    def split_hi(self, e, j, it, part, s):
        slot, count = self.landed_at(j, it, part)
        kt, cols = j.subs[s], j.tiles * P
        e.wait_ge(*self.landed[slot].at(count))
        e.wait_ge(*self.used.at(it * (2 * j.S) + (j.G0 + part + 1)))
        e.activation(self.w_hi[slot][:, 0:kt, 0:cols], self.w32[:, slot, 0:kt, 0:cols], ACT.Copy)\
         .then_inc(self.hi.sem, 1)

    def split_lo(self, e, j, it, part, s):
        slot, _ = self.landed_at(j, it, part)
        kt, cols = j.subs[s], j.tiles * P
        e.wait_ge(*self.hi.at(it * (2 * j.S) + (j.G0 + part + 3)))
        e.tensor_tensor(self.w_lo[slot][:, 0:kt, 0:cols], self.w32[:, slot, 0:kt, 0:cols],
                        self.w_hi[slot][:, 0:kt, 0:cols].bitcast(F32), ALU.subtract).then_inc(self.lo.sem, 1)

    def first_loads(self, e):
        for k in range(self.RING):
            part = self.upcoming(0, k)
            if part:
                self.load(e, *part, k)

    def first_hi(self, e):
        self.split_hi(e, self.jobs[0], 0, 0, 0)

    def first_lo(self, e):
        self.split_lo(e, self.jobs[0], 0, 0, 0)


def gemm_stage(core, gemm):
    nc, jobs, RING = core.nc, gemm.jobs, gemm.RING
    hi, lo, used, w_hi, w_lo = gemm.hi, gemm.lo, gemm.used, gemm.w_hi, gemm.w_lo
    with ExitStack() as c:
        core.tmp_act = core.sb(c, "tmp_act", [P, 2, 2, T])
        core.tmp_dve = core.sb(c, "tmp_dve", [P, 2, T])
        acc = [core.ps(c, f"acc{r}", [P, 2, T]) for r in range(2)]
        act_done, dve_done = core.sig("epi_act_done"), core.sig("epi_dve_done")
        chained = core.sig("epi_chain")
        block = c.enter_context(nc.Block())

        def walk(e, body, peel=1):
            for n, j in enumerate(jobs):
                if e is nc.tensor and j.after:
                    e.wait_ge(*act_done.at(j.U0 + 2))
                    e.wait_ge(*dve_done.at(j.U0 + 2))
                rounds = (j.units - peel) // 2
                if rounds >= 2:
                    with e.Fori(0, rounds) as it:
                        for r in range(2):
                            body(n, j, it * 2 + r, it, r, False)
                else:
                    rounds = 0
                for u in range(2 * rounds, j.units):
                    body(n, j, u, 0, u, u == j.units - 1)

        @block.sync
        def _(e):
            def body(n, j, u, it, r, last):
                for s in range(j.S):
                    part = r * j.S + s
                    units_on, s_next = divmod(s + RING, j.S)
                    if isinstance(u, int):
                        target = gemm.upcoming(n, part + RING)
                    else:
                        target = j, it * 2 + (r + units_on), s_next
                    if target:
                        e.wait_ge(*lo.at(it * (2 * j.S) + (j.G0 + part + 3)))
                        gemm.load(e, *target, (j.G0 + part) % RING)
            if not gemm.ahead:
                gemm.first_loads(e)
            walk(e, body, peel=2)

        @block.tensor
        def _(e):
            def body(n, j, u, it, r, last):
                e.wait_ge(*act_done.at(it * 2 + (j.U0 + r + 1)))
                e.wait_ge(*dve_done.at(it * 2 + (j.U0 + r + 1)))
                for s, kt in enumerate(j.subs):
                    part = r * j.S + s
                    slot = (j.G0 + part) % RING
                    e.wait_ge(*hi.at(it * (2 * j.S) + (j.G0 + part + 3)))
                    e.wait_ge(*lo.at(it * (2 * j.S) + (j.G0 + part + 3)))
                    for t in range(j.tiles):
                        cols = slice(t * P, (t + 1) * P)
                        out = acc[(j.U0 + r) % 2][:, t, :]
                        for k in range(kt):
                            a_hi, a_lo = j.act(s, t, k)
                            ends = s == j.S - 1 and k == kt - 1
                            e.matmul(out, w_hi[slot][:, k, cols], a_hi, start=(s == 0 and k == 0), stop=False)
                            e.matmul(out, w_hi[slot][:, k, cols], a_lo, start=False, stop=False)
                            mm = e.matmul(out, w_lo[slot][:, k, cols], a_hi, start=False, stop=ends)
                    mm.then_inc(used.sem, 1)
            walk(e, body)

        def splitter(e, first, one):
            def body(n, j, u, it, r, last):
                for s in range(j.S):
                    part = r * j.S + s + 1
                    ends = s == j.S - 1
                    if not (last and ends):
                        one(j, it, part, (s + 1) % j.S)
                    elif n + 1 < len(jobs):
                        one(jobs[n + 1], 0, 0, 0)
                    if ends:
                        first(j, u, it, r)
            if not gemm.ahead:
                one(jobs[0], 0, 0, 0)
            walk(e, body)

        @block.scalar
        def _(e):
            def one(j, it, part, s):
                gemm.split_hi(e, j, it, part, s)

            def epilogue(j, u, it, r):
                e.wait_ge(*used.at(it * (2 * j.S) + (j.G0 + (r + 1) * j.S + 2)))
                e.wait_ge(*dve_done.at(it * 2 + (j.U0 + r + 1)))
                signal_after(e, j.epi_act(e, u, acc[(j.U0 + r) % 2], (j.U0 + r) % 2), act_done)
            splitter(e, epilogue, one)

        @block.vector
        def _(e):
            def one(j, it, part, s):
                gemm.split_lo(e, j, it, part, s)

            def epilogue(j, u, it, r):
                chain = Chain(e, chained, it * (2 * j.links) + (j.C0 + r * j.links))
                e.wait_ge(*act_done.at(it * 2 + (j.U0 + r + 3)))
                e.wait_ge(*dve_done.at(it * 2 + (j.U0 + r + 2)))
                last = j.epi_dve(e, chain, u, acc[(j.U0 + r) % 2], (j.U0 + r) % 2)
                assert chain.n == j.links
                signal_after(e, last, dve_done)
            splitter(e, epilogue, one)

    core.ended(w_hi_ready=gemm.all_parts, w_lo_ready=gemm.all_parts, w_used=gemm.all_parts,
               epi_act_done=gemm.all_units, epi_dve_done=gemm.all_units, epi_chain=gemm.all_links,
               **{f"w_landed{r}": gemm.loads[r] for r in range(RING)})


def linear(core, jobs, prepare=None):
    with ExitStack() as c:
        gemm = Gemm(core, c, jobs)
        if prepare:
            gemm.ahead = True
            prepare(gemm)
        gemm_stage(core, gemm)


QUAD = 4
OCT = 2 * QUAD
UNITS = OCT * NT
PAIRS = OCT // 2
P_SLOTS = 4


def attention_stage(core, iterations, q, k, v, out, scale, mask, bias=None, rope=None):
    nc = core.nc
    links = [0 if bias is None else bias.links[n % NT] for n in range(UNITS)]
    all_links = sum(links) + PAIRS
    with ExitStack() as c:
        if rope:
            qs, ks = (core.sb(c, s, [P, 2, QUAD, T]) for s in ("q_now", "k_now"))
        else:
            qs, ks = (core.sb(c, s, [P, 2, 2, T]) for s in ("q_now", "k_now"))
        v_raw = core.sb(c, "v_raw", [P, 2, 2, T])
        v_tok = core.sb(c, "v_tok", [P, 2, 2, NT, P])
        biased = core.sb(c, "biased", [P, 2, T]) if bias else None
        probs = core.sb(c, "probs", [P, P_SLOTS, T])
        probs_T = core.sb(c, "probs_T", [P, 2, NT, P])
        o_tok = core.sb(c, "o_tok", [P, 2, NT, P])
        neg_max = core.sb(c, "neg_max", [P, 4])
        sums = core.sb(c, "exp_sums", [P, 2, 8])
        inverse = core.sb(c, "inverse_sums", [P, 2, 8])
        score = [core.ps(c, f"score{s}", [P, T]) for s in range(2)]
        turned = [core.ps(c, f"turned{s}", [P, NT, P]) for s in range(2)]
        flip = core.ps(c, "flip", [P, NT, P])
        o_bank = [core.ps(c, f"o_bank{s}", [P, T]) for s in range(2)]
        q_staged, k_staged, v_staged = core.sig("at_q_staged"), core.sig("at_k_staged"), core.sig("at_v_staged")
        v_turned, v_ready = core.sig("at_v_turned"), core.sig("at_v_ready")
        scored, maxed, exped = core.sig("at_scored"), core.sig("at_maxed"), core.sig("at_exped")
        p_turned, p_ready, pv_done = core.sig("at_p_turned"), core.sig("at_p_ready"), core.sig("at_pv_done")
        o_scaled, o_turned, o_kept = core.sig("at_o_scaled"), core.sig("at_o_turned"), core.sig("at_o_kept")
        rope_placed, chained = core.sig("at_rope_placed"), core.sig("at_chain")
        score_read = maxed if bias else exped
        block = c.enter_context(nc.Block())

        def over(e, body):
            if iterations == 1:
                body(0)
            else:
                with e.Fori(0, iterations) as it:
                    body(it)

        def unit(n):
            return n // 16, n // 8 % 2, n // 4 % 2, n % 4, (n % 4 + 1) * P

        def operands(n):
            quad, a, j, _, _ = unit(n)
            return (slice(0, HD + 32), 2 * a + j) if rope else (slice(HD * j, HD * j + HD), a)

        @block.gpsimd
        def _(e):
            def iteration(it):
                for quad in range(2):
                    e.wait_ge(*v_turned.at(it * PAIRS + (2 * quad - 2)))
                    e.tensor_copy(v_raw[:, quad, :, :], v(it * 2 + quad)).then_inc(v_staged.sem, 1)
                    if not rope:
                        e.wait_ge(*scored.at(it * UNITS + (16 * quad - 16)))
                        e.tensor_copy(ks[:, quad, :, :], k(it * 2 + quad)).then_inc(k_staged.sem, 1)
            over(e, iteration)

        @block.tensor
        def _(e):
            def turn_v(it, r):
                quad, a = r // 2, r % 2
                e.wait_ge(*v_staged.at(it * 2 + (quad + 1)))
                if r == 0:
                    e.wait_ge(*o_kept.at(it * PAIRS))
                else:
                    e.wait_ge(*v_ready.at(it * PAIRS + r))
                for kt in range(NT):
                    last = e.transpose(flip[:, kt, :], v_raw[:, quad, a, kt * P:(kt + 1) * P], core.ident[:, :])
                last.then_inc(v_turned.sem, 1)

            def turn_o(it, r):
                e.wait_ge(*o_scaled.at(it * PAIRS + (r + 1)))
                if r == 0:
                    e.wait_ge(*v_ready.at(it * PAIRS + PAIRS))
                else:
                    e.wait_ge(*o_kept.at(it * PAIRS + r))
                for i in range(NT):
                    last = e.transpose(flip[:, i, :], o_tok[:, r % 2, i, :], core.ident[:, :])
                last.then_inc(o_turned.sem, 1)

            def scores(it, n):
                quad, a, j, i, keys = unit(n)
                rows, tile = operands(n)
                cols = slice(P * i, P * i + P)
                if n == 0 and rope:
                    e.wait_ge(*rope_placed.at(1))
                if n % 16 == 0:
                    e.wait_ge(*q_staged.at(it * 2 + (quad + 1)))
                    e.wait_ge(*k_staged.at(it * 2 + (quad + 1)))
                e.wait_ge(*score_read.at(it * UNITS + (n - 1)))
                s = score[n % 2]
                e.matmul(s[:, 0:keys], qs[rows, quad, tile, cols], ks[rows, quad, tile, 0:keys], start=True, stop=False)
                e.matmul(s[:, cols], core.ident16[:, :], mask[:, :], start=False, stop=True)\
                 .then_inc(scored.sem, 1)

            def turn(it, n):
                i = unit(n)[3]
                e.wait_ge(*exped.at(it * UNITS + (n + 1)))
                e.wait_ge(*p_ready.at(it * UNITS + (n - 1)))
                for kt in range(i + 1):
                    last = e.transpose(turned[n % 2][:, kt, :], probs[:, n % P_SLOTS, kt * P:(kt + 1) * P],
                                       core.ident[:, :])
                last.then_inc(p_turned.sem, 1)

            def values(it, n):
                quad, a, j, i, _ = unit(n)
                r = n // 8
                e.wait_ge(*p_ready.at(it * UNITS + (n + 1)))
                if n % 8 == 0:
                    e.wait_ge(*v_ready.at(it * PAIRS + (r + 1)))
                    e.wait_ge(*o_scaled.at(it * PAIRS + (r - 1)))
                for kt in range(i + 1):
                    last = e.matmul(o_bank[r % 2][:, (n % 8) * HD:(n % 8 + 1) * HD], probs_T[:, n % 2, kt, :],
                                    v_tok[:, quad, a, kt, HD * j:HD * j + HD], start=(kt == 0), stop=(kt == i))
                last.then_inc(pv_done.sem, 1)

            def iteration(it):
                turn_v(it, 0)
                scores(it, 0)
                turn_v(it, 1)
                for n in range(1, UNITS + 3):
                    if n < UNITS:
                        scores(it, n)
                    if n in (8, 10):
                        turn_v(it, 2 if n == 8 else 3)
                    if 2 <= n < UNITS + 2:
                        turn(it, n - 2)
                    if n >= 3:
                        values(it, n - 3)
                    if n % 8 == 5 and n > 8:
                        turn_o(it, n // 8 - 1)
                turn_o(it, PAIRS - 1)
            over(e, iteration)

        @block.vector
        def _(e):
            if rope:
                for quad in range(2):
                    last = e.tensor_copy(ks[HD:HD + 32, quad, :, :], spread(rope[1], QUAD))
                last.then_inc(rope_placed.sem, 1)

            def stage_k(it, quad):
                e.wait_ge(*scored.at(it * UNITS + (16 * quad - 16)))
                for j in range(2):
                    last = e.tensor_copy(ks[0:HD, quad, j:QUAD:2, :], k(it * 2 + quad)[HD * j:HD * j + HD])
                last.then_inc(k_staged.sem, 1)

            def maximum(it, n, chain):
                keys = unit(n)[4]
                e.wait_ge(*scored.at(it * UNITS + (n + 1)))
                e.wait_ge(*exped.at(it * UNITS + (n - 1)))
                src = score[n % 2]
                if bias:
                    bias.add(e, chain, src, biased[:, n % 2, :], it * OCT + n // 4, n % 4)
                    src = biased[:, n % 2, :]
                e.tensor_reduce(neg_max[:, n % 4:n % 4 + 1], src[:, 0:keys], AX.X, ALU.max, negate=True)\
                 .then_inc(maxed.sem, 1)

            def divide(it, r, chain):
                e.wait_ge(*pv_done.at(it * UNITS + 8 * (r + 1)))
                e.wait_ge(*o_turned.at(it * PAIRS + (r - 1)))
                chain.link(e.reciprocal(inverse[:, r % 2, :], sums[:, r % 2, :]))
                e.tensor_tensor(o_tok[:, r % 2, :, :].rearrange("p i (j d) -> p j i d", j=2),
                                o_bank[r % 2][:, :].rearrange("p (j i d) -> p j i d", j=2, i=NT),
                                spread(inverse[:, r % 2, :], HD, 2).rearrange("p (j i) d -> p j i d", j=2),
                                ALU.mult).then_inc(o_scaled.sem, 1)

            def keep_o(it, r):
                e.wait_ge(*o_turned.at(it * PAIRS + (r + 1)))
                e.tensor_copy(out(it * PAIRS + r), flip[:, :, :].rearrange("p i f -> p (i f)")).then_inc(o_kept.sem, 1)

            def iteration(it):
                chain = Chain(e, chained, it * all_links)
                if rope:
                    stage_k(it, 0)
                for n in range(UNITS + 1):
                    if n < UNITS:
                        maximum(it, n, chain)
                    if n == 4 and rope:
                        stage_k(it, 1)
                    if n % 8 == 3 and n > 8:
                        divide(it, n // 8 - 1, chain)
                    if n % 8 == 6 and n > 8:
                        keep_o(it, n // 8 - 1)
                divide(it, PAIRS - 1, chain)
                keep_o(it, PAIRS - 1)
                core.n_chain = chain.n
            over(e, iteration)

        @block.scalar
        def _(e):
            def stage_q(it, quad):
                e.wait_ge(*scored.at(it * UNITS + (16 * quad - 16)))
                if rope:
                    for j in range(2):
                        e.activation(qs[0:HD, quad, j:QUAD:2, :], q(it * 2 + quad)[HD * j:HD * j + HD], ACT.Copy,
                                     scale=scale)
                    for h in range(QUAD):
                        last = e.activation(qs[HD:HD + 32, quad, h, :], rope[0](it * 2 + quad)[32 * h:32 * h + 32],
                                            ACT.Copy, scale=scale)
                else:
                    last = e.activation(qs[:, quad, :, :], q(it * 2 + quad), ACT.Copy, scale=scale)
                last.then_inc(q_staged.sem, 1)

            def exponentials(it, n):
                keys = unit(n)[4]
                e.wait_ge(*maxed.at(it * UNITS + (n + 1)))
                e.wait_ge(*p_turned.at(it * UNITS + (n - P_SLOTS + 1)))
                if n % 8 == 0:
                    e.wait_ge(*o_scaled.at(it * PAIRS + (n // 8 - 1)))
                src = biased[:, n % 2, 0:keys] if bias else score[n % 2][:, 0:keys]
                e.activation(probs[:, n % P_SLOTS, 0:keys], src, ACT.Exp, bias=neg_max[:, n % 4:n % 4 + 1],
                             accum_out=sums[:, n // 8 % 2, n % 8:n % 8 + 1]).then_inc(exped.sem, 1)

            def copy_turned(it, n):
                i = unit(n)[3]
                e.wait_ge(*p_turned.at(it * UNITS + (n + 1)))
                e.wait_ge(*pv_done.at(it * UNITS + (n - 1)))
                e.activation(probs_T[:, n % 2, 0:i + 1, :], turned[n % 2][:, 0:i + 1, :], ACT.Copy)\
                 .then_inc(p_ready.sem, 1)

            def copy_v(it, r):
                e.wait_ge(*v_turned.at(it * PAIRS + (r + 1)))
                e.activation(v_tok[:, r // 2, r % 2, :, :], flip[:, :, :], ACT.Copy).then_inc(v_ready.sem, 1)

            def iteration(it):
                stage_q(it, 0)
                copy_v(it, 0)
                copy_v(it, 1)
                for n in range(UNITS + 2):
                    if n < UNITS:
                        exponentials(it, n)
                    if n == 4:
                        stage_q(it, 1)
                    if n in (8, 10):
                        copy_v(it, 2 if n == 8 else 3)
                    if n >= 2:
                        copy_turned(it, n - 2)
            over(e, iteration)

    assert core.n_chain == all_links, (core.n_chain, all_links)
    per_iteration = dict.fromkeys(("at_scored", "at_maxed", "at_exped", "at_p_turned", "at_p_ready",
                                   "at_pv_done"), UNITS)
    per_iteration |= dict.fromkeys(("at_q_staged", "at_k_staged", "at_v_staged"), 2)
    per_iteration |= dict.fromkeys(("at_v_turned", "at_v_ready", "at_o_scaled", "at_o_turned", "at_o_kept"), PAIRS)
    per_iteration["at_chain"] = all_links
    core.ended(**{name: n * iterations for name, n in per_iteration.items()})
    if rope:
        core.counters["at_rope_placed"].base += 1


def forget_stage(core, fa, forget_bias, neg_c):
    nc, H = core.nc, 8
    with ExitStack() as c:
        fb = core.sb(c, "forget_bias", [H, 1])
        z, mag, soft, log_f, cum, one = (core.sb(c, s, [H, T]) for s in
                                         ("f_z", "f_abs", "f_soft", "f_log", "f_cum", "f_one"))
        pick = core.sb(c, "pick_head", [H, H, P])
        bank = [core.ps(c, f"f_bank{s}", [P, T]) for s in range(2)]
        loaded, picked, soft_ready = core.sig("f_loaded"), core.sig("f_picked"), core.sig("f_soft_ready")
        mag_ready, cum_ready = core.sig("f_abs_ready"), core.sig("f_cum_ready")
        spread, kept, own, act_own = core.sig("f_spread"), core.sig("f_kept"), core.sig("f_chain"), core.sig("f_act_chain")
        block = c.enter_context(nc.Block())

        @block.sync
        def _(e):
            e.dma_start(fb[:, :], forget_bias[0].rearrange("(h o) -> h o", o=1)).then_inc(loaded.sem, 16)

        @block.gpsimd
        def _(e):
            e.memset(one[:, :], 1.0).then_inc(picked.sem, 1)
            e.memset(pick[:, :, :], 0.0).then_inc(picked.sem, 1)
            e.wait_ge(*picked.at(2))
            e.affine_select(out=pick[:, :, :], in_=pick[:, :, :], compare_op=ALU.not_equal, fill=1.0, base=0,
                            pattern=[[-1, H], [0, P]], channel_multiplier=1).then_inc(picked.sem, 1)

        @block.vector
        def _(e):
            chain = Chain(e, own)
            e.wait_ge(*loaded.at(16))
            chain.link(e.tensor_scalar(z[:, :], fa[0:H, :], fb[:, 0:1], None, ALU.add))
            e.scalar_tensor_tensor(out=mag[:, :], in0=z[:, :], scalar=-1.0, in1=z[:, :], op0=ALU.mult, op1=ALU.max)\
             .then_inc(mag_ready.sem, 1)
            e.wait_ge(*soft_ready.at(1))
            chain.link(e.scalar_tensor_tensor(out=log_f[:, :], in0=z[:, :], scalar=0.0, in1=soft[:, :],
                                              op0=ALU.min, op1=ALU.subtract))
            e.wait_ge(*picked.at(1))
            chain.link(e.tensor_tensor_scan(cum[:, :], one[:, :], log_f[:, :], 0.0, ALU.mult, ALU.add))
            e.tensor_scalar(cum[:, :], cum[:, :], -1.0, None, ALU.mult).then_inc(cum_ready.sem, 1)
            core.n_chain = chain.n

        @block.scalar
        def _(e):
            e.wait_ge(*mag_ready.at(1))
            Chain(e, act_own).link(e.activation(mag[:, :], mag[:, :], ACT.Exp, scale=-1.0))
            e.activation(soft[:, :], mag[:, :], ACT.Ln, bias=1.0).then_inc(soft_ready.sem, 1)
            for h in range(H):
                e.wait_ge(*spread.at(h + 1))
                e.activation(neg_c[:, h, :], bank[h % 2][:, :], ACT.Copy).then_inc(kept.sem, 1)

        @block.tensor
        def _(e):
            e.wait_ge(*picked.at(3))
            e.wait_ge(*cum_ready.at(1))
            for h in range(H):
                if h >= 2:
                    e.wait_ge(*kept.at(h - 1))
                e.matmul(bank[h % 2][:, :], pick[:, h, :], cum[:, :], start=True, stop=True).then_inc(spread.sem, 1)
    core.ended(f_loaded=16, f_picked=3, f_soft_ready=1, f_abs_ready=1, f_cum_ready=1, f_spread=H, f_kept=H,
               f_chain=core.n_chain, f_act_chain=1)


class Bias:

    def __init__(self, add, links):
        self.add, self.links = add, links


def forget_bias_add(neg_c):
    def add(e, chain, score, dst, h, i):
        keys = (i + 1) * P
        chain.link(e.tensor_tensor(dst[:, 0:keys], score[:, 0:keys],
                                   neg_c[:, bass.ds(h, 1), 0:keys].rearrange("p o k -> p (o k)"), ALU.add))
    return Bias(add=add, links=[1] * NT)


WINDOW = 2 * P
EXTENDED = MAX_REL * 2 + 1 + P - 1


def relative_stage(core, rel_bias, scratch, near, far):
    nc, H, last = core.nc, 8, 2 * MAX_REL
    with ExitStack() as c:
        ext = core.sb(c, "rel_extended", [H, EXTENDED])
        window = core.sb(c, "rel_window", [P, H, WINDOW])
        loaded, extended = core.sig("rel_loaded"), core.sig("rel_extended")
        stored, windows = core.sig("rel_stored"), core.sig("rel_windows")
        block = c.enter_context(nc.Block())

        @block.sync
        def _(e):
            e.dma_start(ext[:, 0:last + 1], rel_bias[0]).then_inc(loaded.sem, 16)
            e.wait_ge(*extended.at(1))
            e.dma_start(scratch, ext[:, :]).then_inc(stored.sem, 16)
            e.wait_ge(*stored.at(16))
            e.dma_start(window[:, :, :], bass.AP(scratch.tensor, 1, [[1, P], [EXTENDED, H], [1, WINDOW]]))\
             .then_inc(windows.sem, 16)
            e.dma_start(far[:, :], bass.AP(scratch.tensor, last, [[0, P], [EXTENDED, H]]),
                        allow_slow_non_contiguous=True).then_inc(windows.sem, 16)
            e.wait_ge(*windows.at(32))

        @block.vector
        def _(e):
            e.wait_ge(*loaded.at(16))
            e.tensor_copy(ext[:, last + 1:EXTENDED],
                          ext[:, last:last + 1].broadcast_to([H, EXTENDED - last - 1])).then_inc(extended.sem, 1)
            e.wait_ge(*windows.at(32))
            e.tensor_copy(near[:, :, :], window[:, :, ::-1])
    core.ended(rel_loaded=16, rel_extended=1, rel_stored=16, rel_windows=32)


def relative_bias_add(near, far):
    def add(e, chain, score, dst, h, i):
        keys = (i + 1) * P
        first = max(0, i - 1) * P
        table = near[:, bass.ds(h, 1), WINDOW - (keys - first):WINDOW].rearrange("p o k -> p (o k)")
        ins = e.tensor_tensor(dst[:, first:keys], score[:, first:keys], table, ALU.add)
        if first:
            ins = e.tensor_scalar(dst[:, 0:first], score[:, 0:first], far[:, bass.ds(h, 1)], None, ALU.add)
        chain.link(ins)
    return Bias(add=add, links=[1] * NT)

class Results:

    def __init__(self, signal, names):
        self.counter, self.names = signal, list(names)
        self.index = {name: n + 1 for n, name in enumerate(self.names)}
        assert len(self.index) == len(self.names)
        self.marked = 0

    def mark(self, instruction, name):
        assert self.names[self.marked] == name, (self.names[self.marked], name)
        self.marked += 1
        instruction.then_inc(self.counter.sem, 1)

    def at(self, name, it=0, ahead=0):
        return self.counter.at(it * len(self.names) + (ahead * len(self.names) + self.index[name]))

    def before(self, it):
        return self.counter.at(it * len(self.names))


GLA_HEADS, GLA_RANK, GLA_EXP = 4, 16, 40.0


def gla_stage(core, A, gla, glr, o):
    nc = core.nc
    H, pairs = range(GLA_HEADS), range(2)
    dve_names = ([f"{s}{p}" for p in pairs for s in ("z", "mag")] +
                 [f"{s}{p}" for p in pairs for s in ("la", "scan", "b", "d", "c1", "c2", "d4")] +
                 [f"{s}{p}" for p in pairs for s in ("qg", "kg", "qx", "kx")] +
                 [f"AT{h}" for h in H] + ["S_zero0", "S_zero1"] +
                 [f"S{p}_{c}" for p in pairs for c in range(1, NCH)] +
                 [f"{s}{h}" for h in H for s in ("var", "rvar")] + [f"{s}{h}" for h in H for s in ("y", "out")])
    act_names = ([f"{s}{p}" for p in pairs for s in ("e", "l")] + [f"v{h}" for h in H] +
                 [f"{s}{p}" for p in pairs for s in ("E1", "E2", "E3", "E4")] + ["kt0", "kt1"] +
                 [f"{s}{h}" for h in H for s in ("o", "sq")] + [f"R{h}" for h in H] + [f"silu{h}" for h in H])
    pe_names = (["Z0", "Z1"] + [f"V{h}" for h in H] + ["KX0", "KX1"] + [f"A{h}" for h in H] +
                [f"U0{t}" for t in range(NT)] + ["O0", "O1"] + [f"U1{t}" for t in range(NT)] + ["O2", "O3"] +
                [f"N{h}" for h in H])
    pool_names = [f"kxm{p}{t}" for p in pairs for t in range(NT)]
    with ExitStack() as c:
        w2 = core.sb(c, "gla_w2", [GLA_RANK, 2 * P])
        z, mag, b, d, c1, c2, d4 = (core.sb(c, f"gla_{s}", [P, 2, T]) for s in ("z", "mag", "b", "d", "c1", "c2", "d4"))
        E1, E2, E3, E4 = c1, c2, core.sb(c, "gla_E3", [P, 2, T]), d4
        qg, kg, qx, kx = (core.sb(c, f"gla_{s}", [P, 2, T]) for s in ("qg", "kg", "qx", "kx"))
        v_tok = core.sb(c, "gla_v_tok", [P, GLA_HEADS, NT, P])
        kx_tok = core.sb(c, "gla_kx_tok", [P, 2, NT, P])
        kxm = core.sb(c, "gla_kx_masked", [P, NT, CPT, P])
        AT = core.sb(c, "gla_AT", [P, GLA_HEADS, NT, P])
        S = [core.sb(c, f"gla_S{p}", [P, NCH, P]) for p in pairs]
        raw = qg, kg
        sq = core.sb(c, "gla_sq", [P, GLA_HEADS, T])
        bank = [core.ps(c, f"gla_bank{n}", [P, T]) for n in range(8)]
        loaded = core.sig("gla_loaded")
        dve, act = Results(core.sig("gla_dve"), dve_names), Results(core.sig("gla_act"), act_names)
        pe, pool = Results(core.sig("gla_pe"), pe_names), Results(core.sig("gla_pool"), pool_names)
        block = c.enter_context(nc.Block())

        def chunks(ap):
            return ap.rearrange("p (c t) -> p c t", t=C32)

        def of_chunk(ap, t):
            return chunks(ap)[:, :, t:t + 1].broadcast_to([P, NCH, C32])

        def stat(h):
            return (z, d)[h // 2][:, h % 2, :]

        def raw_o(h):
            return raw[h // 2][:, h % 2, :]

        @block.sync
        def _(e):
            e.dma_start(w2[:, :], A["gla_gate_w2_2"][0]).then_inc(loaded.sem, 16)

        @block.tensor
        def _(e):
            e.wait_ge(*loaded.at(16))
            for p in pairs:
                pe.mark(e.matmul(bank[6 + p][:, :], w2[:, p * P:(p + 1) * P], glr[0:GLA_RANK, :],
                                 start=True, stop=True), f"Z{p}")
            turned = ([(f"V{h}", gla[:, 4 + h, :], f"v{h}") for h in H] + [(f"KX{p}", kx[:, p, :], f"kt{p}") for p in pairs])
            for n, (name, src, _) in enumerate(turned):
                if n >= 2:
                    e.wait_ge(*act.at(turned[n - 2][2]))
                if name[0] == "K":
                    e.wait_ge(*dve.at(f"kx{name[2]}"))
                for t in range(NT):
                    last = e.transpose(bank[4 + n % 2][:, t * P:(t + 1) * P], src[:, t * P:(t + 1) * P], core.ident[:, :])
                pe.mark(last, name)
            for h in H:
                p, rows = h // 2, slice(HD * (h % 2), HD * (h % 2) + HD)
                e.wait_ge(*dve.at(f"kg{p}"))
                if h >= 2:
                    e.wait_ge(*dve.at(f"AT{h - 2}"))
                for t in range(NT):
                    cols = slice(t * P, (t + 1) * P)
                    last = e.matmul(bank[6 + h % 2][:, cols], kg[rows, p, cols], qg[rows, p, cols], start=True, stop=True)
                pe.mark(last, f"A{h}")
            for p in pairs:
                for t in range(NT):
                    e.wait_ge(*pool.at(f"kxm{p}{t}"))
                    if p:
                        e.wait_ge(*dve.at(f"S0_{min(4 * t + 4, NCH - 1)}"))
                    for j in range(2):
                        for ch in range(CPT):
                            last = e.matmul(bank[t][HD * j:HD * j + HD, ch * P:(ch + 1) * P],
                                            kxm[:, t, ch, HD * j:HD * j + HD], v_tok[:, 2 * p + j, t, :],
                                            start=True, stop=True)
                    pe.mark(last, f"U{p}{t}")
                for h in (2 * p, 2 * p + 1):
                    rows = slice(HD * (h % 2), HD * (h % 2) + HD)
                    e.wait_ge(*act.at("kt1" if p == 0 else f"o{h - 2}"))
                    e.wait_ge(*dve.at(f"AT{h}"))
                    e.wait_ge(*dve.at(f"S{p}_{NCH - 1}"))
                    for t in range(NT):
                        e.matmul(bank[4 + h % 2][:, t * P:(t + 1) * P], v_tok[:, h, t, :], AT[:, h, t, :],
                                 start=True, stop=False)
                        for ch in range(CPT):
                            n = t * CPT + ch
                            cols = slice(n * C32, (n + 1) * C32)
                            last = e.matmul(bank[4 + h % 2][:, cols], S[p][rows, n, :], qx[rows, p, cols],
                                            start=False, stop=(ch == CPT - 1))
                    pe.mark(last, f"O{h}")
            for h in H:
                e.wait_ge(*act.at(f"sq{h}"))
                e.wait_ge(*dve.at(f"AT{h}" if h < 2 else f"var{h - 2}"))
                pe.mark(e.matmul(bank[6 + h % 2][:, :], core.ones[:, :], sq[:, h, :], start=True, stop=True), f"N{h}")

        @block.gpsimd
        def _(e):
            for p in pairs:
                e.wait_ge(*act.at(f"kt{p}"))
                for t in range(NT):
                    if p:
                        e.wait_ge(*pe.at(f"U0{t}"))
                    src = kx_tok[:, p, t, :].rearrange("p (j k) -> p j k", j=2)
                    for ch in range(CPT):
                        last = e.tensor_tensor(kxm[:, t, ch, :].rearrange("p (j k) -> p j k", j=2), src,
                                               spread(core.in_chunk[:, ch, :], 2), ALU.mult)
                    pool.mark(last, f"kxm{p}{t}")

        @block.vector
        def _(e):
            gb = core.v["gla_b"]
            for p in pairs:
                e.wait_ge(*pe.at(f"Z{p}"))
                dve.mark(e.tensor_scalar(z[:, p, :], bank[6 + p][:, :], gb[:, p:p + 1], None, ALU.add), f"z{p}")
                e.wait_ge(*dve.at(f"z{p}"))
                dve.mark(e.scalar_tensor_tensor(out=mag[:, p, :], in0=z[:, p, :], scalar=-1.0, in1=z[:, p, :],
                                                op0=ALU.mult, op1=ALU.max), f"mag{p}")
            for p in pairs:
                zp, bp, dp = z[:, p, :], b[:, p, :], d[:, p, :]
                e.wait_ge(*act.at(f"l{p}"))
                dve.mark(e.scalar_tensor_tensor(out=zp, in0=zp, scalar=0.0, in1=mag[:, p, :], op0=ALU.min,
                                                op1=ALU.subtract), f"la{p}")
                e.wait_ge(*dve.at(f"la{p}"))
                dve.mark(e.tensor_tensor_scan(dp, core.scan_keep[:, :], zp, 0.0, ALU.mult, ALU.add), f"scan{p}")
                e.wait_ge(*dve.at(f"scan{p}"))
                dve.mark(e.tensor_scalar(bp, dp, 1.0 / 16.0, None, ALU.mult), f"b{p}")
                e.wait_ge(*dve.at(f"b{p}"))
                dve.mark(e.tensor_tensor(chunks(dp), chunks(bp), of_chunk(bp, C32 // 2 - 1), ALU.subtract), f"d{p}")
                e.wait_ge(*dve.at(f"d{p}"))
                dve.mark(e.tensor_scalar(c1[:, p, :], dp, GLA_EXP, None, ALU.min), f"c1{p}")
                dve.mark(e.tensor_scalar(c2[:, p, :], dp, -1.0, GLA_EXP, ALU.mult, ALU.min), f"c2{p}")
                dve.mark(e.tensor_tensor(chunks(d4[:, p, :]), of_chunk(bp, C32 - 1), chunks(bp), ALU.subtract), f"d4{p}")
            for p in pairs:
                e.wait_ge(*act.at(f"E4{p}"))
                q, k = gla[:, p, :], gla[:, 2 + p, :]
                dve.mark(e.scalar_tensor_tensor(out=qg[:, p, :], in0=q, scalar=HD ** -0.5, in1=E1[:, p, :],
                                                op0=ALU.mult, op1=ALU.mult), f"qg{p}")
                dve.mark(e.tensor_tensor(kg[:, p, :], k, E2[:, p, :], ALU.mult), f"kg{p}")
                dve.mark(e.scalar_tensor_tensor(out=qx[:, p, :], in0=q, scalar=HD ** -0.5, in1=E3[:, p, :],
                                                op0=ALU.mult, op1=ALU.mult), f"qx{p}")
                dve.mark(e.tensor_tensor(kx[:, p, :], k, E4[:, p, :], ALU.mult), f"kx{p}")
            for h in H:
                e.wait_ge(*pe.at(f"A{h}"))
                src = bank[6 + h % 2][:, :].rearrange("p (t f) -> p t f", t=NT)
                dve.mark(e.tensor_tensor(AT[:, h, :, :], src, spread(core.tri[:, 1, :], NT), ALU.mult), f"AT{h}")
            for p in pairs:
                dve.mark(e.memset(S[p][:, 0, :], 0.0), f"S_zero{p}")
            for p in pairs:
                for ch in range(1, NCH):
                    n = ch - 1
                    e.wait_ge(*pe.at(f"U{p}{n // CPT}"))
                    e.wait_ge(*dve.at(f"S{p}_{n}" if n else f"S_zero{p}"))
                    u = bank[n // CPT][:, (n % CPT) * P:(n % CPT + 1) * P]
                    dve.mark(e.scalar_tensor_tensor(out=S[p][:, ch, :], in0=S[p][:, n, :],
                                                    scalar=E3[:, p, n * C32 + C32 - 1:n * C32 + C32], in1=u,
                                                    op0=ALU.mult, op1=ALU.add), f"S{p}_{ch}")
            for h in H:
                e.wait_ge(*pe.at(f"N{h}"))
                dve.mark(e.tensor_scalar(stat(h), bank[6 + h % 2][:, :], 1.0 / P, 1e-6, ALU.mult, ALU.add), f"var{h}")
                e.wait_ge(*dve.at(f"var{h}"))
                dve.mark(e.reciprocal(stat(h), stat(h)), f"rvar{h}")
            for h in H:
                e.wait_ge(*act.at(f"R{h}"))
                dve.mark(e.scalar_tensor_tensor(out=stat(h), in0=raw_o(h), scalar=core.v["gla_g"][:, 0:1], in1=stat(h),
                                                op0=ALU.mult, op1=ALU.mult), f"y{h}")
                e.wait_ge(*dve.at(f"y{h}"))
                e.wait_ge(*act.at(f"silu{h}"))
                dve.mark(e.tensor_tensor(o[:, h, :], stat(h), sq[:, h, :], ALU.mult), f"out{h}")

        @block.scalar
        def _(e):
            for p in pairs:
                e.wait_ge(*dve.at(f"mag{p}"))
                act.mark(e.activation(mag[:, p, :], mag[:, p, :], ACT.Exp, scale=-1.0), f"e{p}")
                e.wait_ge(*act.at(f"e{p}"))
                act.mark(e.activation(mag[:, p, :], mag[:, p, :], ACT.Ln, bias=1.0), f"l{p}")
            for h in H:
                e.wait_ge(*pe.at(f"V{h}"))
                act.mark(e.activation(v_tok[:, h, :, :], bank[4 + h % 2][:, :].rearrange("p (t f) -> p t f", t=NT),
                                      ACT.Copy), f"v{h}")
            for p in pairs:
                e.wait_ge(*dve.at(f"d4{p}"))
                act.mark(e.activation(E1[:, p, :], c1[:, p, :], ACT.Exp), f"E1{p}")
                act.mark(e.activation(E2[:, p, :], c2[:, p, :], ACT.Exp), f"E2{p}")
                act.mark(e.activation(E3[:, p, :], b[:, p, :], ACT.Exp), f"E3{p}")
                act.mark(e.activation(E4[:, p, :], d4[:, p, :], ACT.Exp), f"E4{p}")
            for p in pairs:
                e.wait_ge(*pe.at(f"KX{p}"))
                act.mark(e.activation(kx_tok[:, p, :, :], bank[4 + p][:, :].rearrange("p (t f) -> p t f", t=NT),
                                      ACT.Copy), f"kt{p}")
            for h in H:
                e.wait_ge(*pe.at(f"O{h}"))
                act.mark(e.activation(raw_o(h), bank[4 + h % 2][:, :], ACT.Copy), f"o{h}")
                e.wait_ge(*act.at(f"o{h}"))
                act.mark(e.activation(sq[:, h, :], raw_o(h), ACT.Square), f"sq{h}")
            for h in H:
                e.wait_ge(*dve.at(f"rvar{h}"))
                act.mark(e.activation(stat(h), stat(h), ACT.Sqrt), f"R{h}")
            for h in H:
                e.wait_ge(*pe.at(f"N{h}"))
                act.mark(e.activation(sq[:, h, :], gla[:, 8 + h, :], ACT.Silu), f"silu{h}")
    core.ended(gla_loaded=16, gla_dve=len(dve_names), gla_act=len(act_names), gla_pe=len(pe_names),
               gla_pool=len(pool_names))


RW_DECAY, RW_GN_EPS = 0.6065306597126334, 64e-5


def rwkv_prepare_stage(core, A, rw, decay, rate, gate):
    nc = core.nc
    tiles, pairs = range(15), range(4)
    order = [12, 13, 14] + list(range(12))
    dve_names = [f"{s}{n}" for n in order for s in ("shift", "mix")] + [f"decay{p}" for p in pairs]
    act_names = ["tanh", "sig13", "sig14"] + [f"{s}{p}" for p in pairs for s in ("w", "a", "g")]
    pe_names = [f"{s}{p}" for p in pairs for s in ("W", "A", "G")]
    with ExitStack() as c:
        w2a2 = core.sb(c, "w2a2", [P, T])
        g2 = core.sb(c, "g2", [P, 2, T])
        diff = core.sb(c, "shift_diff", [P, 2, T])
        low = core.sb(c, "low_rank", [P, 3, T])
        bank = [core.ps(c, f"rwp_bank{n}", [P, T]) for n in range(6)]
        loaded = core.sig("rwp_loaded")
        dve, act, pe = (Results(core.sig(f"rwp_{s}"), n) for s, n in
                        (("dve", dve_names), ("act", act_names), ("pe", pe_names)))
        block = c.enter_context(nc.Block())

        @block.sync
        def _(e):
            for dst, src in ((w2a2[0:HD, :], A["rwkv_w2_2"][0]), (w2a2[HD:P, :], A["rwkv_a2_2"][0]),
                             (g2[:, 0, :], A["rwkv_g2_2"][0][0:P]), (g2[96:P, 1, :], A["rwkv_g2_2"][0][P:P + 32])):
                e.dma_start(dst, src).then_inc(loaded.sem, 16)

        @block.vector
        def _(e):
            for i, n in enumerate(order):
                p, dd = rw[:, n, :], diff[:, i % 2, :]
                mu = core.v["mu_tail"][:, 0:1] if n == 14 else core.v["mu"][:, n:n + 1]
                if i >= 2:
                    e.wait_ge(*dve.at(f"mix{order[i - 2]}"))
                e.tensor_scalar(dd[:, 0:1], p[:, 0:1], -1.0, None, ALU.mult)
                dve.mark(e.tensor_tensor(dd[:, 1:T], p[:, 0:T - 1], p[:, 1:T], ALU.subtract), f"shift{n}")
                e.wait_ge(*dve.at(f"shift{n}"))
                dve.mark(e.scalar_tensor_tensor(out=p, in0=dd, scalar=mu, in1=p, op0=ALU.mult, op1=ALU.add), f"mix{n}")
            for p in pairs:
                e.wait_ge(*act.at(f"w{p}"))
                dve.mark(e.tensor_scalar(decay[:, p, :], decay[:, p, :], -RW_DECAY, None, ALU.mult), f"decay{p}")

        @block.scalar
        def _(e):
            e.wait_ge(*dve.at("mix12"))
            act.mark(e.activation(low[0:HD, 0, :], rw[0:HD, 12, :], ACT.Tanh), "tanh")
            e.wait_ge(*dve.at("mix14"))
            act.mark(e.activation(low[:, 1, :], rw[:, 13, :], ACT.Sigmoid), "sig13")
            act.mark(e.activation(low[96:P, 2, :], rw[96:P, 14, :], ACT.Sigmoid), "sig14")
            for p in pairs:
                b = 3 * (p % 2)
                e.wait_ge(*pe.at(f"W{p}"))
                act.mark(e.activation(decay[:, p, :], bank[b][:, :], ACT.Sigmoid, bias=core.v["w0"][:, p:p + 1]), f"w{p}")
                e.wait_ge(*pe.at(f"A{p}"))
                act.mark(e.activation(rate[:, p, :], bank[b + 1][:, :], ACT.Sigmoid, bias=core.v["a0"][:, p:p + 1]), f"a{p}")
                e.wait_ge(*pe.at(f"G{p}"))
                act.mark(e.activation(gate[:, p, :], bank[b + 2][:, :], ACT.Copy), f"g{p}")

        @block.tensor
        def _(e):
            e.wait_ge(*loaded.at(64))
            e.wait_ge(*act.at("sig14"))
            for p in pairs:
                cols, b = slice(p * P, (p + 1) * P), 3 * (p % 2)
                if p >= 2:
                    e.wait_ge(*act.at(f"g{p - 2}"))
                pe.mark(e.matmul(bank[b][:, :], w2a2[0:HD, cols], low[0:HD, 0, :], start=True, stop=True), f"W{p}")
                pe.mark(e.matmul(bank[b + 1][:, :], w2a2[HD:P, cols], rw[HD:P, 12, :], start=True, stop=True), f"A{p}")
                e.matmul(bank[b + 2][:, :], g2[:, 0, cols], low[:, 1, :], start=True, stop=False)
                pe.mark(e.matmul(bank[b + 2][:, :], g2[96:P, 1, cols], low[96:P, 2, :], start=False, stop=True,
                                 tile_position=(96, 0)), f"G{p}")
    core.ended(rwp_loaded=64, rwp_dve=len(dve_names), rwp_act=len(act_names), rwp_pe=len(pe_names))


def rwkv_chunks_stage(core, rw, decay, rate, o, o_at, G, F):
    nc = core.nc
    J, PAIRS4 = range(2), 4
    both = lambda s: [f"{s}{j}" for j in J]
    fills = ([("TA", "A"), ("TB", "A"), ("TK", "A"), ("TV", "A")] +
             [(f"{s}{j}", eng) for j in J for s, eng in (("BAa", "D"), ("BAb", "D"), ("M", "D"), ("KAa", "D"), ("KAb", "D"))] +
             [(f"{s}{j}", eng) for j in J for s, eng in (("M2", "A"), ("T2", "D"), ("AV", "A"))] +
             [(f"{s}{j}", eng) for j in J for s, eng in (("M4", "A"), ("T4", "A"), ("X2", "D"))] +
             [(f"{s}{j}", eng) for j in J for s, eng in (("M8", "A"), ("T8", "A"), ("X4", "D"))] +
             [(f"{s}{j}", eng) for j in J for s, eng in (("M16", "A"), ("X8", "D"))] +
             [(f"X16{j}", "D") for j in J] + [(f"P{j}", "A") for j in J] + [("Q", "D")] +
             [("Ga", "D"), ("Gb", "D"), ("Fa", "A"), ("Fb", "A"), ("Y", "A")])
    number = {name: n for n, (name, _) in enumerate(fills)}
    taken_by = dict(fills)
    BANKS = 7
    dve_names = ([f"{s}{j}" for j in J for s in ("BAa", "BAb", "M", "X1", "KAa", "KAb")] +
                 both("T2") + both("X2") + both("X4") + both("X8") + both("X16") + ["Q", "Ga", "Gb"])
    act_names = (["TA", "TB", "TK", "TV"] +
                 [f"{s}{j}" for j in J for s in ("M2", "AV")] + [f"{s}{j}" for j in J for s in ("M4", "T4")] +
                 [f"{s}{j}" for j in J for s in ("M8", "T8")] + both("M16") + both("P") + ["Fa", "Fb", "Y"])
    pool_names = [f"{s}{j}" for s in ("Bm", "Km") for j in J] + ["q_decayed", "G_decayed"]
    pe_names = [name for name, _ in fills]
    ready_dve = ["kk0", "t", "kx", "scan", "cx", "last", "NORM", "rn_a", "rn_b", "kk", "ah", "bb", "bh", "kh", "rk", "BONUS", "rh"]
    ready_act = ["sq", "Ew", "En", "Ex", "root"]
    with ExitStack() as c:
        f = {s: core.sb(c, f"rw_{s}", [P, T]) for s in ("cw", "cx", "En", "Ew", "s1", "s2", "bh", "kh")}
        f |= {"kk": rw[:, 12, :], "k2": rw[:, 13, :], "v": rw[:, 14, :], "t": f["s1"], "bb": rw[:, 12, :]}
        ar = core.sb(c, "rw_ar", [P, 2, T])
        last_w = core.sb(c, "rw_last_w", [P, PAIRS4, NCH])
        tok_b, tok_k, tok_v = (core.sb(c, f"rw_tok_{s}", [P, NT, P]) for s in "bkv")
        av = [core.sb(c, f"rw_av{j}", [P, NT, P]) for j in J]
        ba = [core.sb(c, f"rw_ba{j}", [P, NT, 2, P]) for j in J]
        ka = [core.sb(c, f"rw_ka{j}", [P, NT, 2, P]) for j in J]
        Ms = [[core.sb(c, f"rw_M{j}{s}", [P, NT, P]) for s in range(2)] for j in J]
        Ts = [[core.sb(c, f"rw_T{j}{s}", [P, NT, P]) for s in range(2)] for j in J]
        XT = [core.sb(c, f"rw_XT{j}", [P, NT, P]) for j in J]
        PP = av
        bm = [core.sb(c, f"rw_bm{j}", [P, NT, CPT, HD]) for j in J]
        km = [core.sb(c, f"rw_km{j}", [P, NT, CPT, HD]) for j in J]
        bank = [core.ps(c, f"rw_bank{n}", [P, T]) for n in range(BANKS)]
        ready_bank = core.ps(c, "rw_ready_bank", [P, T])
        dve, act = Results(core.sig("rw_dve"), dve_names), Results(core.sig("rw_act"), act_names)
        pe, pool = Results(core.sig("rw_pe"), pe_names), Results(core.sig("rw_pool"), pool_names)
        made_dve, made_act = Results(core.sig("rw_made_dve"), ready_dve), Results(core.sig("rw_made_act"), ready_act)
        made_pe = Results(core.sig("rw_made_pe"), ["NORM", "BONUS"])
        made_v = core.sig("rw_made_v")
        block = c.enter_context(nc.Block())

        def taken(name, it):
            return (dve if taken_by[name] == "D" else act).at(name, it)

        def bank_of(name):
            return bank[number[name] % BANKS]

        def tiles4(name):
            return bank_of(name)[:, :].rearrange("p (t f) -> p t f", t=NT)

        def row(tensor, tile):
            return tensor[:, bass.ds(tile, 1), :].rearrange("p o t -> p (o t)")

        def over_pairs(e, body):
            with e.Fori(0, PAIRS4 - 1) as it:
                body(it, True)
            body(PAIRS4 - 1, False)

        @block.gpsimd
        def _(e):
            def copy_v(it):
                e.tensor_copy(f["v"][:, :], row(rw, it + 8)).then_inc(made_v.sem, 1)

            def pair(it, more):
                pool.marked = 0
                for s, src, dst in (("Bm", tok_b, bm), ("Km", tok_k, km)):
                    e.wait_ge(*act.at("T" + s[0], it))
                    for j in J:
                        for t in range(NT):
                            last = e.tensor_tensor(dst[j][:, t, :, :], spread(src[:, t, HD * j:HD * j + HD], CPT),
                                                   core.in_chunk[:, :, :], ALU.mult)
                        pool.mark(last, f"{s}{j}")
                if more:
                    e.wait_ge(*pe.at("TV", it))
                    e.wait_ge(*made_dve.at("BONUS", it))
                    copy_v(it + 1)
                e.wait_ge(*dve.at("Q", it))
                q = row(decay, it)[:, C32:T].rearrange("p (c t) -> p c t", t=C32)
                decays = last_w[:, bass.ds(it, 1), 0:NCH - 1].rearrange("p o c -> p (o c)").unsqueeze(2)
                pool.mark(e.tensor_tensor(q, q, decays.broadcast_to([P, NCH - 1, C32]), ALU.mult), "q_decayed")
                e.wait_ge(*dve.at("Gb", it))
                for half, first in ((0, 1), (1, 0)):
                    g = row(G[half], it).rearrange("p (c k) -> p c k", k=HD)[:, first:, :]
                    before = last_w[:, bass.ds(it, 1), 8 * half + first - 1:8 * half + 7].rearrange("p o c -> p (o c)")
                    last = e.tensor_tensor(g, g, spread(before, HD, 2), ALU.mult)
                pool.mark(last, "G_decayed")

            copy_v(0)
            over_pairs(e, pair)

        @block.tensor
        def _(e):
            def fill(name, it, emit, *needs):
                n = number[name]
                if n >= BANKS:
                    e.wait_ge(*taken(fills[n - BANKS][0], it))
                for need in needs:
                    e.wait_ge(*need)
                pe.mark(emit(bank_of(name)), name)

            def over_tiles(out_cols, operands):
                def emit(b):
                    for t in range(NT):
                        lhsT, rhs = operands(t)
                        last = e.matmul(b[:, t * out_cols:(t + 1) * out_cols], lhsT, rhs, start=True, stop=True)
                    return last
                return emit

            def turn(src):
                def emit(b):
                    for t in range(NT):
                        last = e.transpose(b[:, t * P:(t + 1) * P], src[:, t * P:(t + 1) * P], core.ident[:, :])
                    return last
                return emit

            def head_sums(name, it, ahead, src, need):
                e.wait_ge(*need)
                made_pe.mark(e.matmul(ready_bank[:, :], core.head_ones[:, :], f[src][:, :], start=True, stop=True), name)

            def norm_sums(it, ahead):
                made_pe.marked = 0
                head_sums("NORM", it, ahead, "s1", made_act.at("sq", it, ahead))

            def bonus_sums(it, ahead):
                head_sums("BONUS", it, ahead, "t", made_dve.at("rk", it, ahead))

            def pair(it, more):
                pe.marked = 0
                e.wait_ge(*dve.before(it))
                e.wait_ge(*act.before(it))
                fill("TA", it, turn(ar[:, 0, :]), made_dve.at("ah", it))
                fill("TB", it, turn(f["bh"]), made_dve.at("bh", it))
                fill("TK", it, turn(f["kh"]), made_dve.at("kh", it))
                fill("TV", it, turn(f["v"]), made_v.at(it + 1))
                for j in J:
                    rows = slice(HD * j, HD * j + HD)
                    for s, lhs in (("BA", "bh"), ("M", None), ("KA", "kh")):
                        if s == "M":
                            fill(f"M{j}", it, over_tiles(P, lambda t: (ar[rows, 0, t * P:(t + 1) * P],
                                                                       f["bh"][rows, t * P:(t + 1) * P])))
                            continue
                        for half in range(2):
                            def emit(b):
                                for t in (2 * half, 2 * half + 1):
                                    cols = slice(t * P, (t + 1) * P)
                                    last = e.matmul(b[:, (t % 2) * 2 * P:(t % 2 + 1) * 2 * P].rearrange("p (a f) -> p a f", a=2),
                                                    f[lhs][rows, cols], ar[rows, :, cols], start=True, stop=True)
                                return last
                            fill(f"{s}{'ab'[half]}{j}", it, emit, made_dve.at("rh", it))
                for j in J:
                    fill(f"M2{j}", it, over_tiles(P, lambda t: (ba[j][:, t, 0, :], Ms[j][0][:, t, :])), dve.at(f"M{j}", it))
                    fill(f"T2{j}", it, over_tiles(P, lambda t: (Ms[j][0][:, t, :], ba[j][:, t, 0, :])))
                    fill(f"AV{j}", it, over_tiles(HD, lambda t: (ka[j][:, t, 0, :], tok_v[:, t, HD * j:HD * j + HD])),
                         dve.at(f"KAb{j}", it), act.at("TV", it))
                if more:
                    norm_sums(it, 1)
                for n, power in enumerate((2, 4, 8)):
                    for j in J:
                        now, nxt = Ms[j][(n + 1) % 2], power * 2
                        tn = Ts[j][(n + 1) % 2]
                        t_ready = (dve if power == 2 else act).at(f"T{power}{j}", it)
                        fill(f"M{nxt}{j}", it, over_tiles(P, lambda t: (tn[:, t, :], now[:, t, :])),
                             act.at(f"M{power}{j}", it), t_ready)
                        if nxt < 16:
                            fill(f"T{nxt}{j}", it, over_tiles(P, lambda t: (now[:, t, :], tn[:, t, :])))
                        x_ready = dve.at(f"X{power // 2}{j}" , it)
                        fill(f"X{power}{j}", it, over_tiles(P, lambda t: (now[:, t, :], XT[j][:, t, :])), x_ready)
                for j in J:
                    fill(f"X16{j}", it, over_tiles(P, lambda t: (Ms[j][0][:, t, :], XT[j][:, t, :])),
                         act.at(f"M16{j}", it), dve.at(f"X8{j}", it))
                for j in J:
                    fill(f"P{j}", it, over_tiles(P, lambda t: (XT[j][:, t, :], av[j][:, t, :])),
                         dve.at(f"X16{j}", it), act.at(f"AV{j}", it))
                if more:
                    bonus_sums(it, 1)

                def q_products(b):
                    for j in J:
                        for t in range(NT):
                            last = e.matmul(b[HD * j:HD * j + HD, t * P:(t + 1) * P], PP[j][:, t, 0:HD], ba[j][:, t, 1, :],
                                            start=True, stop=True)
                    return last
                fill("Q", it, q_products, act.at("P1", it))
                for half in range(2):
                    def emit(b):
                        for j in J:
                            for t in (2 * half, 2 * half + 1):
                                last = e.matmul(b[HD * j:HD * j + HD, (t % 2) * 2 * P:(t % 2 + 1) * 2 * P],
                                                PP[j][:, t, 0:HD], bm[j][:, t, :, :].rearrange("p c k -> p (c k)"),
                                                start=True, stop=True)
                        return last
                    fill(f"G{'ab'[half]}", it, emit, pool.at("Bm1", it))
                for half in range(2):
                    def emit(b):
                        for j in J:
                            for n in range(8 * half, 8 * half + 8):
                                t, ch = n // CPT, n % CPT
                                out = b[HD * j:HD * j + HD, (n % 8) * HD:(n % 8 + 1) * HD]
                                e.matmul(out, bm[j][:, t, ch, :], PP[j][:, t, HD:P], start=True, stop=False)
                                last = e.matmul(out, km[j][:, t, ch, :], tok_v[:, t, HD * j:HD * j + HD],
                                                start=False, stop=True)
                        return last
                    fill(f"F{'ab'[half]}", it, emit, pool.at("Km1", it))

                def outputs(b):
                    for j in J:
                        rows = slice(HD * j, HD * j + HD)
                        for t in range(NT):
                            out = b[rows, t * P:(t + 1) * P]
                            e.matmul(out, PP[j][:, t, HD:P], ba[j][:, t, 1, :], start=True, stop=False)
                            last = e.matmul(out, tok_v[:, t, HD * j:HD * j + HD], ka[j][:, t, 1, :], start=False, stop=True)
                    return last
                fill("Y", it, outputs)

            norm_sums(0, 0)
            bonus_sums(0, 0)
            over_pairs(e, pair)

        @block.vector
        def _(e):
            tt, ts, stt = e.tensor_tensor, e.tensor_scalar, e.scalar_tensor_tensor

            def make(name, instruction, *needs):
                for need in needs:
                    e.wait_ge(*need)
                made_dve.mark(instruction(), name)

            def decays(it, ahead):
                n = it + ahead
                made_dve.marked = 0
                k, lw, a = row(rw, n + 4), row(decay, n), row(rate, n)
                make("kk0", lambda: ts(f["kk"][:, :], k, core.v["k_k"][:, bass.ds(n, 1)], None, ALU.mult))
                make("t", lambda: ts(f["k2"][:, :], a, -1.0, core.v["k_a"][:, bass.ds(n, 1)], ALU.add, ALU.mult))
                make("kx", lambda: stt(out=f["k2"][:, :], in0=f["k2"][:, :], scalar=1.0, in1=k, op0=ALU.add, op1=ALU.mult),
                     made_dve.at("t", it, ahead))
                make("scan", lambda: e.tensor_tensor_scan(f["cw"][:, :], core.scan_keep[:, :], lw, 0.0, ALU.mult, ALU.add))
                make("cx", lambda: tt(f["cx"][:, :], f["cw"][:, :], lw, ALU.subtract), made_dve.at("scan", it, ahead))

            def key_norm(it, ahead, step):
                if step == 0:
                    make("last", lambda: e.tensor_copy(last_w[:, bass.ds(it + ahead, 1), :].rearrange("p o c -> p (o c)"),
                                                       f["Ew"][:, C32 - 1:T:C32]), made_act.at("Ew", it, ahead))
                    make("NORM", lambda: ts(f["s2"][:, :], ready_bank[:, :], 1e-24, None, ALU.max),
                         made_pe.at("NORM", it, ahead))
                    e.wait_ge(*made_dve.at("NORM", it, ahead))
                half, name = ((slice(0, T // 2), "rn_a"), (slice(T // 2, T), "rn_b"))[step]
                make(name, lambda: e.reciprocal(f["s2"][:, half], f["s2"][:, half]))

            def operands(it, ahead):
                n = it + ahead
                at = lambda s: made_dve.at(s, it, ahead)
                make("kk", lambda: tt(f["kk"][:, :], f["kk"][:, :], f["s2"][:, :], ALU.mult), made_act.at("root", it, ahead))
                if ahead:
                    e.wait_ge(*pe.at("KAb1", it))
                make("ah", lambda: stt(out=ar[:, 0, :], in0=f["kk"][:, :], scalar=-1.0, in1=f["cx"][:, :], op0=ALU.mult,
                                       op1=ALU.mult), made_act.at("Ex", it, ahead), at("kk"))
                make("bb", lambda: tt(f["bb"][:, :], f["kk"][:, :], row(rate, n), ALU.mult), at("kk"))
                make("bh", lambda: tt(f["bh"][:, :], f["bb"][:, :], f["En"][:, :], ALU.mult), at("bb"))
                make("kh", lambda: tt(f["kh"][:, :], f["k2"][:, :], f["En"][:, :], ALU.mult), at("kx"))
                make("rk", lambda: stt(out=f["t"][:, :], in0=row(rw, n), scalar=core.v["r_k"][:, bass.ds(n, 1)],
                                       in1=f["k2"][:, :], op0=ALU.mult, op1=ALU.mult))

            def queries(it, ahead):
                n = it + ahead
                make("BONUS", lambda: tt(row(o, n + o_at), ready_bank[:, :], f["v"][:, :], ALU.mult),
                     made_pe.at("BONUS", it, ahead), made_v.at(it + (ahead + 1)))
                if ahead:
                    e.wait_ge(*dve.at("Q", it))
                make("rh", lambda: tt(ar[:, 1, :], row(rw, n), f["Ew"][:, :], ALU.mult))

            def pair(it, more):
                dve.marked = 0

                def do(name, instruction, *needs):
                    for need in needs:
                        e.wait_ge(*need)
                    dve.mark(instruction(), name)

                D_, P_ = (lambda s: dve.at(s, it)), (lambda s: pe.at(s, it))
                upper = core.tri[:, 0:2, :]
                for j in J:
                    for s, dst in (("BA", ba), ("M", None), ("KA", ka)):
                        if s == "M":
                            do(f"M{j}", lambda: tt(Ms[j][0][:, :, :], tiles4(f"M{j}"), spread(core.tri[:, 2, :], NT), ALU.mult),
                               P_(f"M{j}"))
                            do(f"X1{j}", lambda: tt(XT[j][:, :, :], ba[j][:, :, 0, :], spread(core.ident[:, :], NT), ALU.add),
                               D_(f"BAb{j}"))
                            continue
                        for half in range(2):
                            name = f"{s}{'ab'[half]}{j}"
                            src = bank_of(name)[:, :].rearrange("p (t f) -> p t f", t=2)
                            do(name, lambda: tt(dst[j][:, 2 * half:2 * half + 2, :, :].rearrange("p t a f -> p t (a f)"), src,
                                                spread(upper.rearrange("p a f -> p (a f)"), 2), ALU.mult), P_(name))
                if more:
                    decays(it, 1)
                for j in J:
                    do(f"T2{j}", lambda: e.tensor_copy(Ts[j][1][:, :, :], tiles4(f"T2{j}")), P_(f"T2{j}"))
                for power in (2, 4, 8, 16):
                    for j in J:
                        do(f"X{power}{j}", lambda: tt(XT[j][:, :, :], XT[j][:, :, :], tiles4(f"X{power}{j}"), ALU.add),
                           P_(f"X{power}{j}"), D_(f"X{power // 2}{j}"))
                    if more and power == 2:
                        key_norm(it, 1, 0)
                    if more and power == 4:
                        key_norm(it, 1, 1)
                    if more and power == 8:
                        operands(it, 1)
                do("Q", lambda: tt(row(decay, it), bank_of("Q")[:, :], ar[:, 1, :], ALU.add), P_("Q"))
                if more:
                    queries(it, 1)
                for half in range(2):
                    name = f"G{'ab'[half]}"
                    do(name, lambda: tt(row(G[half], it).rearrange("p (c k) -> p c k", c=8), bank_of(name)[:, :].rearrange("p (c k) -> p c k", c=8),
                                        spread(core.head_ident[:, :], 8), ALU.add), P_(name))

            decays(0, 0)
            key_norm(0, 0, 0)
            key_norm(0, 0, 1)
            operands(0, 0)
            queries(0, 0)
            over_pairs(e, pair)

        @block.scalar
        def _(e):
            def make(name, instruction, *needs):
                for need in needs:
                    e.wait_ge(*need)
                made_act.mark(instruction(), name)

            def exponentials(it, ahead):
                made_act.marked = 0
                at = lambda s: made_dve.at(s, it, ahead)
                make("sq", lambda: e.activation(f["s1"][:, :], f["kk"][:, :], ACT.Square), at("kk0"))
                make("Ew", lambda: e.activation(f["Ew"][:, :], f["cw"][:, :], ACT.Exp), at("scan"))
                make("En", lambda: e.activation(f["En"][:, :], f["cw"][:, :], ACT.Exp, scale=-1.0))
                make("Ex", lambda: e.activation(f["cx"][:, :], f["cx"][:, :], ACT.Exp), at("cx"))

            def root(it, ahead):
                make("root", lambda: e.activation(f["s2"][:, :], f["s2"][:, :], ACT.Sqrt), made_dve.at("rn_b", it, ahead))

            def pair(it, more):
                act.marked = 0

                def do(name, instruction, *needs):
                    for need in needs:
                        e.wait_ge(*need)
                    act.mark(instruction(), name)

                def copy_tiles(name, dst, *needs):
                    do(name, lambda: e.activation(dst, tiles4(name), ACT.Copy), pe.at(name, it), *needs)

                for j in J:
                    src = tiles4("TA")[:, :, HD * j:HD * j + HD]
                    if j == 0:
                        e.wait_ge(*pe.at("TA", it))
                        e.activation(av[j][:, :, 0:HD], src, ACT.Copy)
                    else:
                        do("TA", lambda: e.activation(av[j][:, :, 0:HD], src, ACT.Copy))
                copy_tiles("TB", tok_b[:, :, :])
                copy_tiles("TK", tok_k[:, :, :])
                copy_tiles("TV", tok_v[:, :, :])
                for j in J:
                    copy_tiles(f"M2{j}", Ms[j][1][:, :, :])
                    do(f"AV{j}", lambda: e.activation(av[j][:, :, HD:P], bank_of(f"AV{j}")[:, 0:NT * HD].rearrange(
                        "p (t f) -> p t f", t=NT), ACT.Copy), pe.at(f"AV{j}", it))
                if more:
                    exponentials(it, 1)
                for n, power in enumerate((4, 8)):
                    for j in J:
                        copy_tiles(f"M{power}{j}", Ms[j][n % 2][:, :, :])
                        copy_tiles(f"T{power}{j}", Ts[j][n % 2][:, :, :])
                for j in J:
                    copy_tiles(f"M16{j}", Ms[j][0][:, :, :])
                if more:
                    root(it, 1)
                for j in J:
                    copy_tiles(f"P{j}", PP[j][:, :, :])
                for half in range(2):
                    name = f"F{'ab'[half]}"
                    do(name, lambda: e.activation(row(F[half], it), bank_of(name)[:, :], ACT.Copy), pe.at(name, it))
                do("Y", lambda: e.activation(row(rw, it), bank_of("Y")[:, :], ACT.Copy), pe.at("Y", it))

            exponentials(0, 0)
            root(0, 0)
            over_pairs(e, pair)
    for name, r in (("rw_dve", dve), ("rw_act", act), ("rw_pe", pe), ("rw_pool", pool), ("rw_made_dve", made_dve),
                    ("rw_made_act", made_act), ("rw_made_pe", made_pe)):
        assert r.marked == len(r.names)
        core.ended(**{name: PAIRS4 * len(r.names)})
    core.ended(rw_made_v=PAIRS4)


def rwkv_states_stage(core, y, q, bonus, gate, G, S, g, b):
    nc = core.nc
    J, PAIRS4, HALVES = range(2), 4, range(2)
    pairs = range(PAIRS4)
    dve_names = ([f"S{h}_{n}" for n in range(1, NCH - 1) for h in HALVES] + [f"y{p}" for p in pairs] +
                 [f"yc{p}" for p in pairs] + ["var", "inverse"] + [f"{s}{p}" for p in pairs for s in ("yg", "yb")] +
                 [f"out{p}" for p in pairs])
    pe_names = ([f"S{h}_{n}" for n in range(1, NCH - 1) for h in HALVES] + ["Y"] + [f"mu{p}" for p in pairs] +
                ["var"] + [f"root{p}" for p in pairs])
    with ExitStack() as c:
        squares = core.sb(c, "rws_squares", [P, PAIRS4, T])
        stat = core.sb(c, "rws_stat", [P, 3, T])
        step_bank = [core.ps(c, f"rws_step{n}", [P, 2, 2, HD]) for n in HALVES]
        y_bank = [core.ps(c, f"rws_y{p}", [P, T]) for p in pairs]
        stat_bank = core.ps(c, "rws_stat_bank", [P, T])
        dve, pe = Results(core.sig("rws_dve"), dve_names), Results(core.sig("rws_pe"), pe_names)
        act = Results(core.sig("rws_act"), [f"sq{p}" for p in pairs] + ["root"])
        block = c.enter_context(nc.Block())

        def of_chunk(parts, rows, pair, n):
            return parts[n // 8][rows, pair, n % 8 * HD:(n % 8 + 1) * HD]

        @block.tensor
        def _(e):
            for n in range(1, NCH):
                for half in HALVES:
                    if n > 1:
                        e.wait_ge(*dve.at(f"S{half}_{n - 1}"))
                    if n < NCH - 1:
                        for i in range(2):
                            for j in J:
                                rows = slice(HD * j, HD * j + HD)
                                last = e.matmul(step_bank[half][rows, n % 2, i, :], of_chunk(G, rows, 2 * half + i, n),
                                                of_chunk(S, rows, 2 * half + i, n - 1), start=True, stop=True)
                        pe.mark(last, f"S{half}_{n}")
                    cols = slice(n * C32, (n + 1) * C32)
                    for i in range(2):
                        for j in J:
                            rows = slice(HD * j, HD * j + HD)
                            p = 2 * half + i
                            last = e.matmul(y_bank[p][rows, cols], of_chunk(S, rows, p, n - 1), q[rows, p, cols],
                                            start=True, stop=True)
            pe.mark(last, "Y")
            for p in pairs:
                e.wait_ge(*dve.at(f"y{p}"))
                pe.mark(e.matmul(y_bank[p][:, :], core.head_ones[:, :], y[:, p, :], start=True, stop=True), f"mu{p}")
            for p in pairs:
                e.wait_ge(*act.at(f"sq{p}"))
                last = e.matmul(stat_bank[32 * p:32 * p + 32, :], core.head_ones[:, 3 * HD // 4:5 * HD // 4],
                                squares[:, p, :], start=True, stop=True)
            pe.mark(last, "var")
            e.wait_ge(*act.at("root"))
            for p in pairs:
                pe.mark(e.matmul(y_bank[p][:, :], core.pick_pair_head[:, p, :], stat[:, 2, :], start=True, stop=True), f"root{p}")

        @block.vector
        def _(e):
            for n in range(1, NCH - 1):
                for half in HALVES:
                    e.wait_ge(*pe.at(f"S{half}_{n}"))
                    s = of_chunk(S, slice(0, P), slice(2 * half, 2 * half + 2), n)
                    dve.mark(e.tensor_tensor(s, s, step_bank[half][:, n % 2, :, :], ALU.add), f"S{half}_{n}")
            e.wait_ge(*pe.at("Y"))
            for p in pairs:
                dve.mark(e.tensor_tensor(y[:, p, C32:T], y[:, p, C32:T], y_bank[p][:, C32:T], ALU.add), f"y{p}")
            for p in pairs:
                e.wait_ge(*pe.at(f"mu{p}"))
                dve.mark(e.scalar_tensor_tensor(out=y[:, p, :], in0=y_bank[p][:, :], scalar=-1.0 / HD, in1=y[:, p, :],
                                                op0=ALU.mult, op1=ALU.add), f"yc{p}")
            e.wait_ge(*pe.at("var"))
            dve.mark(e.tensor_scalar(stat[:, 0, :], stat_bank[:, :], 1.0 / HD, RW_GN_EPS, ALU.mult, ALU.add), "var")
            e.wait_ge(*dve.at("var"))
            dve.mark(e.reciprocal(stat[:, 1, :], stat[:, 0, :]), "inverse")
            for p in pairs:
                e.wait_ge(*pe.at(f"root{p}"))
                dve.mark(e.scalar_tensor_tensor(out=y[:, p, :], in0=y[:, p, :], scalar=g[:, p:p + 1], in1=y_bank[p][:, :],
                                                op0=ALU.mult, op1=ALU.mult), f"yg{p}")
                e.wait_ge(*dve.at(f"yg{p}"))
                dve.mark(e.scalar_tensor_tensor(out=y[:, p, :], in0=y[:, p, :], scalar=b[:, p:p + 1], in1=bonus[:, p, :],
                                                op0=ALU.add, op1=ALU.add), f"yb{p}")
            for p in pairs:
                e.wait_ge(*dve.at(f"yb{p}"))
                dve.mark(e.tensor_tensor(bonus[:, p, :], y[:, p, :], gate[:, p, :], ALU.mult), f"out{p}")

        @block.scalar
        def _(e):
            for p in pairs:
                e.wait_ge(*dve.at(f"yc{p}"))
                act.mark(e.activation(squares[:, p, :], y[:, p, :], ACT.Square), f"sq{p}")
            e.wait_ge(*dve.at("inverse"))
            act.mark(e.activation(stat[:, 2, :], stat[:, 1, :], ACT.Sqrt), "root")
    core.ended(rws_dve=len(dve_names), rws_pe=len(pe_names), rws_act=PAIRS4 + 1)

def transformer_program(nc, A, out, stop=None, dump=None):
    with ExitStack() as ctx:
        core = Core(nc, ctx)
        scratch = nc.dram_tensor("rel_scratch", (8, EXTENDED), F32, kind="Internal").ap()
        core.out = out
        constants_stage(core, A)
        if stop in (None, "first"):
            first_block(core, A, scratch)
        if stop in (None, "even", "even_o"):
            even_layer(core, A, stop)
        if stop in (None, "odd"):
            odd_layer(core, A)
        if stop != "even_o":
            output_stage(core, core.x, out)


def output_stage(core, src, out):
    nc = core.nc
    with ExitStack() as c:
        rows = core.sb(c, "out_rows", [P, 2, D])
        bank = [core.ps(c, f"out_bank{b}", [P, T]) for b in range(4)]
        turned, copied, stored = core.sig("out_turned"), core.sig("out_copied"), core.sig("out_stored")
        block = c.enter_context(nc.Block())
        out_v = out[0].rearrange("(t p) d -> t p d", p=P)
        halves = [(t, h) for t in range(NT) for h in range(2)]

        @block.tensor
        def _(e):
            for n, (t, h) in enumerate(halves):
                if n >= 4:
                    e.wait_ge(*copied.at(n - 3))
                for k in range(4):
                    last = e.transpose(bank[n % 4][:, k * P:(k + 1) * P], src[:, 4 * h + k, t * P:(t + 1) * P],
                                       core.ident[:, :])
                last.then_inc(turned.sem, 1)

        @block.scalar
        def _(e):
            for n, (t, h) in enumerate(halves):
                e.wait_ge(*turned.at(n + 1))
                if t >= 2:
                    e.wait_ge(*stored.at(16 * (t - 1)))
                e.activation(rows[:, t % 2, h * T:(h + 1) * T], bank[n % 4][:, :], ACT.Copy).then_inc(copied.sem, 1)

        @block.sync
        def _(e):
            for t in range(NT):
                e.wait_ge(*copied.at(2 * t + 2))
                if t >= 1:
                    e.wait_ge(*stored.at(16 * t))
                e.dma_start(out_v[t], rows[:, t % 2, :]).then_inc(stored.sem, 16)
            e.wait_ge(*stored.at(16 * NT))
    core.ended(out_turned=2 * NT, out_copied=2 * NT, out_stored=16 * NT)


def first_block(core, A, scratch):
    w_in = A["w_in"][0]
    fox, width = 0, 4 * P
    chk = 3 * width + 8
    gate = chk + 3 * width
    with ExitStack() as c:
        o = core.sb(c, "o", [P, 2 * 4, T])
        activations(core, c)
        with ExitStack() as a:
            qkv = core.sb(a, "qkv", [P, 12, T])
            with ExitStack() as f:
                fa = core.sb(f, "fa", [P, 1, T])
                neg_c = core.sb(f, "neg_c", [P, 8, T])
                linear(core, [
                    Job(6, columns(w_in, fox), act_tiles(core), keep(qkv)),
                    Job(1, columns(w_in, 3 * width), act_tiles(core), keep(fa, 1), tiles=1)],
                    lambda gemm: norm_stage(core, "rms", core.x, KD, g=core.v["norm1"], eps=1e-6, gemm=gemm))
                forget_stage(core, fa[:, 0, :], A["forget_bias"], neg_c)
                attention(core, 1, qkv, o, 0, core.causal_mask, forget_bias_add(neg_c))
            with ExitStack() as f:
                near = core.sb(f, "near", [P, 8, WINDOW])
                far = core.sb(f, "far", [P, 8])
                linear(core, [Job(6, columns(w_in, chk), act_tiles(core), keep(qkv))])
                relative_stage(core, A["rel_bias"], scratch, near, far)
                attention(core, 1, qkv, o, 4, core.chunk_mask, relative_bias_add(near, far))
        gates = core.sb(c, "gates", [P, 2 * KD, T])
        linear(core, [Job(KD, columns(w_in, gate), act_tiles(core), keep_sigmoid(gates))])
        views = [A[n][0].rearrange("(k p) n -> p k n", p=P) for n in ("w_branch_a", "w_branch_b")]
        linear(core, [Job(KD, lambda u, s, t: views[t][:, :, bass.ds(u * P, P)],
                              lambda s, t, k: (core.AH[:, 4 * t + k, :], core.AL[:, 4 * t + k, :]),
                              gated_sum(core, gates), subs=(4,))],
               lambda gemm: norm_stage(core, "split", o, KD, gemm=gemm))
        linear(core, [Job(4, columns(A["w_out"][0], 0), act_tiles(core), residual(core))],
               lambda gemm: norm_stage(core, "split", gates, KD, gemm=gemm))
    with ExitStack() as c:
        activations(core, c)
        tiles = FFN1 // P // 2
        hid_hi = core.sb(c, "hid_hi", [P, tiles, T], F32R)
        hid_lo = core.sb(c, "hid_lo", [P, tiles, T], F32R)
        w_up, w_down = A["w_up"][0], A["w_down"][0]
        jobs = []
        for half in range(2):
            jobs.append(Job(tiles // 2, columns(w_up, half * tiles * P), act_tiles(core),
                            relu_squared(core, hid_hi, hid_lo)))
            jobs.append(Job(4, columns(w_down[half * tiles * P:(half + 1) * tiles * P], 0),
                            lambda s, t, k: (hid_hi[:, KD * s + k, :], hid_lo[:, KD * s + k, :]),
                            residual(core), subs=(KD, KD), after=True))
        linear(core, jobs, lambda gemm: norm_stage(core, "rms", core.x, KD, g=core.v["norm2"], eps=1e-6, gemm=gemm))
        norm_stage(core, "rms", core.x, KD, out32=core.x, g=core.v["final"], eps=1e-6, parts=False)


def swiglu_stage(core, A, layer):
    half_tiles = FFN2 // P // 2
    with ExitStack() as c:
        hid_hi = core.sb(c, "hid_hi", [P, half_tiles, T], F32R)
        hid_lo = core.sb(c, "hid_lo", [P, half_tiles, T], F32R)
        w_up, w_down = A["ffn_w_gate_up_2"][layer], A["ffn_w_down_2"][layer]
        jobs = []
        for half in range(2):
            first = half * half_tiles * P
            jobs.append(Job(half_tiles, columns(w_up, first, tile_step=FFN2, unit_step=P), act_tiles(core),
                            silu_times(core, hid_hi, hid_lo)))
            jobs.append(Job(4, columns(w_down[first:first + half_tiles * P], 0),
                            lambda s, t, k: (hid_hi[:, KD * s + k, :], hid_lo[:, KD * s + k, :]),
                            residual(core, DN_ALPHA if half == 0 else 1.0), subs=(KD, half_tiles - KD), after=True))
        linear(core, jobs, lambda gemm: post_norm(core, layer, 0, True, gemm))


def post_norm(core, layer, half, parts, gemm=None):
    norm_stage(core, "ln", core.x, KD, out32=core.x, g=core.v[f"ln_g{layer}{half}"], b=core.v[f"ln_b{layer}{half}"],
               eps=1e-5, parts=parts, gemm=gemm)


def mix_out_and_ffn(core, A, layer, o, w_out):
    with ExitStack() as c:
        activations(core, c)
        linear(core, [Job(4, columns(w_out, 0), act_tiles(core), residual(core, DN_ALPHA))],
               lambda gemm: norm_stage(core, "split", o, KD, gemm=gemm))
        swiglu_stage(core, A, layer)
        post_norm(core, layer, 1, False)


def even_layer(core, A, stop=None):
    w_in = A["even_w_in_2"][0]
    with ExitStack() as c:
        o = core.sb(c, "o", [P, KD, T])
        with ExitStack() as r:
            gla = core.sb(r, "gla", [P, 12, T])
            glr = core.sb(r, "glr", [P, 1, T])
            with ExitStack() as g:
                activations(core, g)
                linear(core, [Job(6, columns(w_in, 0), act_tiles(core), keep(gla)),
                              Job(1, columns(w_in, 12 * P), act_tiles(core), keep(glr, 1), tiles=1)],
                       lambda gemm: norm_stage(core, "split", core.x, KD, gemm=gemm))
            gla_stage(core, A, gla, glr[:, 0, :], o)
        with ExitStack() as r:
            rw = core.sb(r, "rw", [P, 15, T])
            decay, rate, gate = (core.sb(r, f"rw_{s}", [P, 4, T]) for s in ("decay", "rate", "gate"))
            with ExitStack() as g:
                activations(core, g)
                linear(core, [Job(7, columns(w_in, GLA_IN), act_tiles(core), keep(rw)),
                                  Job(1, columns(w_in, GLA_IN + RW_IN - P), act_tiles(core), keep(rw[:, 14:15, :], 1),
                                      tiles=1)],
                       lambda gemm: norm_stage(core, "split", core.x, KD, gemm=gemm))
            rwkv_prepare_stage(core, A, rw, decay, rate, gate)
            G = [rw[:, 8:12, :], core.sb(r, "rw_G_second", [P, 4, T])]
            F = [rw[:, 4:8, :], rate]
            rwkv_chunks_stage(core, rw, decay, rate, o, 4, G, F)
            rwkv_states_stage(core, rw[:, 0:4, :], decay, o[:, 4:8, :], gate, G, F, core.v["rln_g"], core.v["rln_b"])
        if stop == "even_o":
            with ExitStack() as r:
                output_stage(core, o, core.out)
            return
        mix_out_and_ffn(core, A, 0, o, A["even_w_out_2"][0])


MLA_H, MLA_Q, MLA_KV, ROPE = 16, 768, 256, 32
TWO_PI = (6.28125, 8117 / 4194304, 6.283185307179586 - 6.28125 - 8117 / 4194304)
ROUND = 1.5 * 2 ** 23
PI_IN = 3.1415925


def rope_stage(core, A, qr, k_pe):
    nc = core.nc
    tiles = [qr[:, n, :] for n in range(4)] + [k_pe]
    dve_names = (["pos", "ang", "n", "n2", "r1", "r2", "r3", "c", "over", "c2", "sin_in", "cos_in"] +
                 [f"{s}{n}" for n in range(5) for s in ("sin", "cos", "sum")])
    with ExitStack() as c:
        pos_i = core.sb(c, "pos_i", [P, T], I32)
        freq = core.sb(c, "freq", [P, 1])
        ang, turns, cosine, over, sine = (core.sb(c, f"rope_{s}", [P, T]) for s in ("ang", "n", "cos", "over", "sin"))
        parts = core.sb(c, "rope_parts", [P, 2, T])
        swap = core.sb(c, "rope_swap", [P, P])
        bank = [core.ps(c, f"rope_bank{n}", [P, T]) for n in range(5)]
        loaded, swapped, built, table = (core.sig(f"rope_{s}") for s in ("loaded", "swapped", "built", "table"))
        dve = Results(core.sig("rope_dve"), dve_names)
        block = c.enter_context(nc.Block())

        @block.sync
        def _(e):
            e.dma_start(pos_i[:, :], A["positions_2"][0].partition_broadcast(P)).then_inc(loaded.sem, 16)
            e.dma_start(freq[:, :], A["rope_freq"]).then_inc(loaded.sem, 16)

        @block.gpsimd
        def _(e):
            chain = Chain(e, built)
            chain.link(e.memset(swap[:, :], 0.0))
            pairs = swap[:, :].rearrange("p (i two) -> p two i", two=2)
            for two, value in ((1, 1.0), (0, -1.0)):
                chain.link(e.affine_select(out=pairs[:, two, :], in_=pairs[:, two, :], compare_op=ALU.not_equal,
                                           fill=value, base=two - 1, pattern=[[-2, P // 2]], channel_multiplier=1))

        @block.tensor
        def _(e):
            e.wait_ge(*built.at(3))
            for n, x in enumerate(tiles):
                e.matmul(bank[n][:, :], swap[:, :], x, start=True, stop=True).then_inc(swapped.sem, 1)

        @block.scalar
        def _(e):
            e.wait_ge(*dve.at("cos_in"))
            e.activation(sine[:, :], ang[:, :], ACT.Sin).then_inc(table.sem, 1)
            e.activation(cosine[:, :], cosine[:, :], ACT.Sin).then_inc(table.sem, 1)

        @block.vector
        def _(e):
            def do(name, instruction):
                dve.mark(instruction, name)
                e.wait_ge(*dve.at(name))
            ts, tt, stt = e.tensor_scalar, e.tensor_tensor, e.scalar_tensor_tensor
            e.wait_ge(*loaded.at(32))
            do("pos", e.tensor_copy(ang[:, :], pos_i[:, :]))
            do("ang", ts(ang[:, :], ang[:, :], freq[:, 0:1], None, ALU.mult))
            do("n", ts(turns[:, :], ang[:, :], 1.0 / (2 * np.pi), ROUND, ALU.mult, ALU.add))
            do("n2", ts(turns[:, :], turns[:, :], -ROUND, None, ALU.add))
            for n in range(3):
                do(f"r{n + 1}", stt(out=ang[:, :], in0=turns[:, :], scalar=-TWO_PI[n], in1=ang[:, :], op0=ALU.mult,
                                    op1=ALU.add))
            do("c", ts(cosine[:, :], ang[:, :], np.pi / 2, None, ALU.add))
            do("over", ts(over[:, :], cosine[:, :], np.pi, None, ALU.is_gt))
            do("c2", stt(out=cosine[:, :], in0=over[:, :], scalar=-2 * np.pi, in1=cosine[:, :], op0=ALU.mult, op1=ALU.add))
            do("sin_in", ts(ang[:, :], ang[:, :], PI_IN, -PI_IN, ALU.min, ALU.max))
            do("cos_in", ts(cosine[:, :], cosine[:, :], PI_IN, -PI_IN, ALU.min, ALU.max))
            e.wait_ge(*table.at(2))
            for n, x in enumerate(tiles):
                e.wait_ge(*swapped.at(n + 1))
                do(f"sin{n}", tt(parts[:, 0, :], bank[n][:, :], sine[:, :], ALU.mult))
                do(f"cos{n}", tt(parts[:, 1, :], x, cosine[:, :], ALU.mult))
                do(f"sum{n}", tt(x, parts[:, 0, :], parts[:, 1, :], ALU.add))
    core.ended(rope_loaded=32, rope_built=3, rope_swapped=5, rope_table=2, rope_dve=len(dve_names))


def head_columns(w, first, width):
    heads = P // width
    return lambda u, s, t, i: w[:, :, bass.ds(u * 2 * heads + (t * heads + i), 1), first:first + width]\
        .rearrange("p k o n -> p k (o n)")


def odd_layer(core, A):
    w_in = A["mla_w_in_2"][0].rearrange("(k p) n -> p k n", p=P)
    q_b = A["mla_w_q_b_2"][0].rearrange("(k p) (h n) -> p k h n", p=P, h=MLA_H)
    kv_b = A["mla_w_kv_b_2"][0].rearrange("(k p) (h n) -> p k h n", p=P, h=MLA_H)
    with ExitStack() as c:
        o = core.sb(c, "o", [P, KD, T])
        with ExitStack() as r:
            qn, kn, v = (core.sb(r, f"mla_{s}", [P, KD, T]) for s in ("qn", "kn", "v"))
            qr = core.sb(r, "mla_qr", [P, 4, T])
            k_pe = core.sb(r, "mla_k_pe", [P, 1, T])
            with ExitStack() as g:
                activations(core, g)
                linear(core, [Job(4, columns(A["mla_w_in_2"][0], 0), act_tiles(core), keep(o)),
                                  Job(1, lambda u, s, t, i: w_in[:, :, MLA_Q + MLA_KV:], act_tiles(core),
                                      keep(k_pe, 1), tiles=1, pieces=4)],
                       lambda gemm: norm_stage(core, "split", core.x, KD, gemm=gemm))
                norm_stage(core, "rms", o[:, 6:8, :], 2, at=6, g=core.v["kv_g"], eps=1e-6, features=MLA_KV)
                linear(core, [
                    Job(4, head_columns(q_b, 0, HD), act_tiles(core), keep(qn), subs=(6,), pieces=2),
                    Job(2, head_columns(q_b, HD, ROPE), act_tiles(core), keep(qr), subs=(6,), pieces=4),
                    Job(4, head_columns(kv_b, 0, HD), act_tiles(core, 6), keep(kn), subs=(2,), pieces=2),
                    Job(4, head_columns(kv_b, HD, HD), act_tiles(core, 6), keep(v), subs=(2,), pieces=2)],
                    lambda gemm: norm_stage(core, "rms", o[:, 0:6, :], 6, g=core.v["q_g"], eps=1e-6, features=MLA_Q,
                                            gemm=gemm))
            rope_stage(core, A, qr, k_pe[:, 0, :])

            attention_stage(core, 2, two_tiles(qn), two_tiles(kn), two_tiles(v), one_tile(o), (HD + ROPE) ** -0.5,
                            core.chunk_mask, rope=(one_tile(qr), k_pe[HD:HD + ROPE, 0, :]))
        mix_out_and_ffn(core, A, 1, o, A["mla_w_out_2"][0])


def one_tile(x, at=0):
    return lambda n: x[:, bass.ds(n + at, 1), :].rearrange("p o t -> p (o t)")


def two_tiles(x, at=0):
    return lambda n: x[:, bass.ds(n * 2 + at, 2), :]


def attention(core, iterations, qkv, o, o_at, mask, bias):
    attention_stage(core, iterations, two_tiles(qkv), two_tiles(qkv, 4), two_tiles(qkv, 8), one_tile(o, o_at),
                    HD ** -0.5, mask, bias)



def kernel(**inputs):
    import numpy as _np
    import concourse.bacc as _bacc
    from concourse import mybir as _mybir
    from concourse.bass_utils import run_bass_kernel_spmd as _run

    nc = _bacc.Bacc("TRN2", target_bir_lowering=False, num_devices=1)
    arrays, aps = {}, {}
    for name in inputs:
        a = _np.ascontiguousarray(inputs[name])
        arrays[f"in_{name}"] = a
        aps[name] = nc.dram_tensor(f"in_{name}", a.shape, _mybir.dt.from_np(a.dtype), kind="ExternalInput").ap()
    arrays["in_rope_freq"] = _np.array([[10000.0 ** -(p % ROPE // 2 * 2 / ROPE)] for p in range(P)], _np.float32)
    aps["rope_freq"] = nc.dram_tensor("in_rope_freq", (P, 1), F32, kind="ExternalInput").ap()
    out = nc.dram_tensor("out_x", (1, T, D), F32, kind="ExternalOutput").ap()
    transformer_program(nc, aps, out)
    return _run(nc, [arrays], core_ids=[0]).results[0]["out_x"]
```

```python
from contextlib import ExitStack

import numpy as np

import concourse.bass as bass
from concourse import mybir

F32 = mybir.dt.float32
F32R = mybir.dt.float32r
BF16 = mybir.dt.bfloat16
I32 = mybir.dt.int32
ACT = mybir.ActivationFunctionType
ALU = mybir.AluOpType
AX = mybir.AxisListType

P = 128
T = 512
D = 1024
KD = D // P
NT = T // P
HD = 64
C32 = 32
NCH = T // C32
CPT = P // C32
MASKED = -1e30
FFN1 = 4096
FFN2 = 2816
DN_ALPHA = 4.0 ** 0.25
GLA_IN, RW_IN = 1552, 1824
MAX_REL = 128


class Signal:

    def __init__(self, sem):
        self.sem, self.base = sem, 0

    def at(self, n):
        return self.sem, n + self.base


class Chain:

    def __init__(self, eng, signal, before=0):
        self.eng, self.counter, self.before, self.n = eng, signal, before, 0

    def link(self, instruction):
        self.n += 1
        instruction.then_inc(self.counter.sem, 1)
        self.eng.wait_ge(*self.counter.at(self.n + self.before))


class Core:

    def __init__(self, nc, ctx):
        self.nc, self.ctx, self.counters, self.stage_no = nc, ctx, {}, 0

    def sb(self, ctx, name, shape, dtype=F32):
        return ctx.enter_context(self.nc.sbuf_tensor(f"{name}_{self.stage_no}", shape, dtype))

    def ps(self, ctx, name, shape):
        return ctx.enter_context(self.nc.psum_tensor(f"{name}_{self.stage_no}", shape, F32))

    def sig(self, name):
        if name not in self.counters:
            self.counters[name] = Signal(self.ctx.enter_context(self.nc.semaphore(name)))
        return self.counters[name]

    def ended(self, **counts):
        for name, n in counts.items():
            self.counters[name].base += n
        self.stage_no += 1


def spread(ap, count, axis=1):
    shape = list(ap.shape)
    shape.insert(axis, count)
    return ap.unsqueeze(axis).broadcast_to(shape)



COUNT_FROM = {"at_scored": 33, "at_maxed": 33, "at_exped": 33, "at_p_turned": 33, "at_p_ready": 33, "at_pv_done": 33,
              "at_v_turned": 5, "at_v_ready": 5, "at_o_scaled": 5, "at_o_turned": 5, "at_o_kept": 5,
              "rw_pe": 1, "rw_dve": 1, "rw_act": 1}


def constants_stage(core, A):
    nc, ctx = core.nc, core.ctx
    core.x = core.sb(ctx, "x", [P, KD, T])
    core.ident = core.sb(ctx, "ident", [P, P])
    core.ident16 = core.sb(ctx, "ident16", [P, P], BF16)
    core.ones = core.sb(ctx, "ones", [P, P])
    core.head_ones = core.sb(ctx, "head_ones", [P, P])
    core.head_ident = core.sb(ctx, "head_ident", [P, HD])
    core.causal_mask = core.sb(ctx, "causal_mask", [P, P], BF16)
    core.chunk_mask = core.sb(ctx, "chunk_mask", [P, P], BF16)
    core.tri = core.sb(ctx, "tri", [P, 3, P])
    core.in_chunk = core.sb(ctx, "in_chunk", [P, CPT, HD])
    core.scan_keep = core.sb(ctx, "scan_keep", [P, T])
    core.pick_pair_head = core.sb(ctx, "pick_pair_head", [P, 4, P])

    vectors = [("norm1", A["norm1"][0]), ("norm2", A["norm2"][0]), ("final", A["final_norm"]),
               ("gla_b", A["gla_gate_b_2"][0]), ("gla_g", A["gla_norm_g_2"][0]),
               ("w0", A["rwkv_w0_2"][0]), ("a0", A["rwkv_a0_2"][0]), ("k_k", A["rwkv_k_k_2"][0]),
               ("k_a", A["rwkv_k_a_2"][0]), ("r_k", A["rwkv_r_k_2"][0].rearrange("h n -> (h n)")),
               ("rln_g", A["rwkv_ln_g_2"][0]), ("rln_b", A["rwkv_ln_b_2"][0]),
               ("mu", A["rwkv_mu_2"][0][0:14 * P]), ("mu_tail", A["rwkv_mu_2"][0][RW_IN - P:RW_IN]),
               ("q_g", A["mla_q_norm_g_2"][0]), ("kv_g", A["mla_kv_norm_g_2"][0])]
    for layer in range(2):
        for half in range(2):
            vectors += [(f"ln_g{layer}{half}", A["ln_g_2"][layer, half]),
                        (f"ln_b{layer}{half}", A["ln_b_2"][layer, half])]
    places, at = [], 0
    for name, src in vectors:
        n = src.shape[0] // P
        if at % P + n > P:
            at = -(-at // P) * P
        places.append((name, src, at, n))
        at += n
    row_tiles = -(-at // P)
    core.vec = core.sb(ctx, "vec", [P, row_tiles * P])
    core.v = {name: core.vec[:, at:at + n] for name, _, at, n in places}

    with ExitStack() as c:
        x_tok = core.sb(c, "x_tok", [P, NT, D])
        rows = core.sb(c, "rows", [P, row_tiles, P])
        bank = [core.ps(c, f"bank{b}", [P, T]) for b in range(2)]
        loaded_x, loaded_rows = core.sig("loaded_x"), core.sig("loaded_rows")
        masks, rows_zero = core.sig("masks"), core.sig("rows_zero")
        turned, copied = core.sig("turned"), core.sig("copied")
        block = c.enter_context(nc.Block())

        @block.sync
        def _(e):
            e.dma_start(x_tok[:, :, :], A["x"][0].rearrange("(t p) d -> p t d", p=P)).then_inc(loaded_x.sem, 16)
            e.wait_ge(*rows_zero.at(1))
            for _, src, at, n in places:
                e.dma_start(rows[at % P:at % P + n, at // P, :], src.rearrange("(k p) -> k p", p=P))\
                 .then_inc(loaded_rows.sem, 16)

        @block.gpsimd
        def _(e):
            for name, n in COUNT_FROM.items():
                e.sem_inc(core.sig(name).sem, n)
            chain = Chain(e, masks)
            e.memset(rows[:, :, :], 0.0).then_inc(rows_zero.sem, 1)
            chain.link(e.memset(core.ident[:, :], 0.0))
            chain.link(e.affine_select(out=core.ident[:, :], in_=core.ident[:, :], compare_op=ALU.not_equal,
                                       fill=1.0, base=0, pattern=[[-1, P]], channel_multiplier=1))
            chain.link(e.tensor_copy(core.ident16[:, :], core.ident[:, :]))
            chain.link(e.memset(core.ones[:, :], 1.0))
            chain.link(e.memset(core.head_ones[:, :], 0.0))
            for h in range(2):
                part = core.head_ones[HD * h:HD * h + HD, HD * h:HD * h + HD]
                chain.link(e.memset(part, 1.0))
            chain.link(e.tensor_tensor(core.head_ident[:, :], core.ident[:, 0:HD], core.ident[:, HD:P], ALU.add))
            chain.link(e.memset(core.causal_mask[:, :], 0.0))
            chain.link(e.affine_select(out=core.causal_mask[:, :], in_=core.causal_mask[:, :],
                                       compare_op=ALU.is_ge, fill=MASKED, base=0,
                                       pattern=[[-1, P]], channel_multiplier=1))
            chain.link(e.memset(core.chunk_mask[:, :], 0.0))
            chain.link(e.memset(core.chunk_mask[0:HD, HD:P], MASKED))
            chain.link(e.memset(core.scan_keep[:, :], 1.0))
            chain.link(e.memset(core.scan_keep[:, 0:T:C32], 0.0))
            chain.link(e.memset(core.in_chunk[:, :, :], 1.0))
            chain.link(e.affine_select(out=core.in_chunk[:, :, :], in_=core.in_chunk[:, :, :],
                                       compare_op=ALU.is_ge, fill=0.0, base=0,
                                       pattern=[[-C32, CPT], [0, HD]], channel_multiplier=1))
            chain.link(e.affine_select(out=core.in_chunk[:, :, :], in_=core.in_chunk[:, :, :],
                                       compare_op=ALU.is_ge, fill=0.0, base=C32 - 1,
                                       pattern=[[C32, CPT], [0, HD]], channel_multiplier=-1))
            chain.link(e.memset(core.pick_pair_head[:, :, :], 0.0))
            pick = core.pick_pair_head[:, :, :].rearrange("p n (j f) -> p n j f", j=2)
            chain.link(e.affine_select(out=pick, in_=pick, compare_op=ALU.not_equal, fill=1.0, base=0,
                                       pattern=[[-32, 4], [-16, 2], [0, HD]], channel_multiplier=1))
            for n, (base, step) in enumerate([(-1, 1), (0, 1), (-1, -1)]):
                tri = core.tri[:, n, :].rearrange("p (c f) -> p c f", f=C32)
                chain.link(e.tensor_copy(tri, core.in_chunk[:, :, 0:C32]))
                chain.link(e.affine_select(out=core.tri[:, n, :], in_=core.tri[:, n, :], compare_op=ALU.is_ge,
                                           fill=0.0, base=base, pattern=[[step, P]], channel_multiplier=-step))
            core.n_masks = chain.n

        @block.vector
        def _(e):
            e.sem_inc(core.sig("w_lo_ready").sem, 2)
            e.sem_inc(core.sig("epi_dve_done").sem, 2)

        @block.tensor
        def _(e):
            e.sem_inc(core.sig("w_used").sem, 2)
            e.wait_ge(*masks.at(core.n_masks))
            e.wait_ge(*loaded_rows.at(16 * len(places)))
            for r in range(row_tiles):
                last = e.transpose(bank[0][:, r * P:(r + 1) * P], rows[:, r, :], core.ident[:, :])
            last.then_inc(turned.sem, 1)
            e.wait_ge(*loaded_x.at(16))
            for k in range(KD):
                if k >= 1:
                    e.wait_ge(*copied.at(k))
                for t in range(NT):
                    last = e.transpose(bank[(k + 1) % 2][:, t * P:(t + 1) * P], x_tok[:, t, k * P:(k + 1) * P],
                                       core.ident[:, :])
                last.then_inc(turned.sem, 1)

        @block.scalar
        def _(e):
            e.sem_inc(core.sig("w_hi_ready").sem, 2)
            e.sem_inc(core.sig("epi_act_done").sem, 2)
            e.wait_ge(*turned.at(1))
            e.activation(core.vec[:, :], bank[0][:, 0:row_tiles * P], ACT.Copy).then_inc(copied.sem, 1)
            for k in range(KD):
                e.wait_ge(*turned.at(k + 2))
                e.activation(core.x[:, k, :], bank[(k + 1) % 2][:, :], ACT.Copy).then_inc(copied.sem, 1)
    core.ended(**COUNT_FROM)
    core.ended(loaded_x=16, loaded_rows=16 * len(places), masks=core.n_masks, rows_zero=1,
               turned=KD + 1, copied=KD + 1)



def activations(core, ctx):
    core.AH = core.sb(ctx, "act_hi", [P, KD, T], F32R)
    core.AL = core.sb(ctx, "act_lo", [P, KD, T], F32R)


def norm_stage(core, kind, src, n, out32=None, at=0, g=None, b=None, eps=0.0, features=D, parts=True,
               gemm=None):
    nc = core.nc
    with ExitStack() as c:
        if out32 is not None:
            y = out32
        else:
            y = core.sb(gemm.ctx if gemm else c, "norm_y", [P, 2 if gemm else n, T])
        squares = core.sb(c, "squares", [P, 2, T])
        average = core.sb(c, "average", [P, T])
        stat = core.sb(c, "stat", [P, 3, P])
        root = core.ps(gemm.ctx if gemm else c, "root", [P, T])
        sums = core.ps(c, "sums", [P, T])
        mean = core.ps(c, "mean", [P, T])
        squared, summed = core.sig("norm_squared"), core.sig("norm_summed")
        centred, var_ready = core.sig("norm_centred"), core.sig("norm_var")
        rooted, scaled, hi_ready = core.sig("norm_rooted"), core.sig("norm_scaled"), core.sig("norm_hi")
        own, levelled, placed = core.sig("norm_chain"), core.sig("norm_levelled"), core.sig("norm_placed")
        block = c.enter_context(nc.Block())
        taken = y if kind == "ln" else src

        if gemm:
            @block.sync
            def _(e):
                gemm.first_loads(e)

        @block.tensor
        def _(e):
            if kind == "ln":
                for k in range(n):
                    last = e.matmul(mean[:, :], core.ones[:, :], src[:, k, :], start=(k == 0), stop=(k == n - 1))
                last.then_inc(summed.sem, n)
            for k in range(n):
                e.wait_ge(*squared.at(k + 1))
                for t in range(NT):
                    last = e.matmul(sums[32 * t:32 * t + 32, 0:P], core.ones[:, 0:32], squares[:, k % 2, t * P:(t + 1) * P],
                                    start=(k == 0), stop=(k == n - 1))
                last.then_inc(summed.sem, 1)
            e.wait_ge(*rooted.at(1))
            for t in range(NT):
                last = e.matmul(root[:, t * P:(t + 1) * P], core.pick_pair_head[:, t, :], stat[:, 2, :],
                                start=True, stop=True)
            last.then_inc(levelled.sem, 1)

        offset = n if kind == "ln" else 0

        @block.scalar
        def _(e):
            for k in range(n):
                if kind == "ln":
                    e.wait_ge(*centred.at(k + 1))
                if k >= 2:
                    e.wait_ge(*summed.at(offset + k - 1))
                e.activation(squares[:, k % 2, :], taken[:, k, :], ACT.Square).then_inc(squared.sem, 1)
            e.wait_ge(*var_ready.at(1))
            e.activation(stat[:, 2, :], stat[:, 1, :], ACT.Sqrt).then_inc(rooted.sem, 1)
            for k in range(n if not gemm and (parts or b is not None) else 0):
                e.wait_ge(*scaled.at(k + 1))
                if b is not None:
                    e.activation(y[:, k, :], y[:, k, :], ACT.Identity, scale=g[:, k:k + 1], bias=b[:, k:k + 1])\
                     .then_inc(placed.sem, 1)
                    if not parts:
                        continue
                    e.wait_ge(*placed.at(k + 1))
                e.activation(core.AH[:, at + k, :], y[:, k, :], ACT.Copy).then_inc(hi_ready.sem, 1)
            if gemm:
                gemm.first_hi(e)

        @block.vector
        def _(e):
            chain = Chain(e, own)
            if kind == "ln":
                e.wait_ge(*summed.at(n))
                chain.link(e.tensor_scalar(average[:, :], mean[:, :], 1.0 / features, None, ALU.mult))
                for k in range(n):
                    e.tensor_tensor(y[:, k, :], src[:, k, :], average[:, :], ALU.subtract).then_inc(centred.sem, 1)
            e.wait_ge(*summed.at(offset + n))
            chain.link(e.tensor_scalar(stat[:, 0, :], sums[:, 0:P], 1.0 / features, eps, ALU.mult, ALU.add))
            e.reciprocal(stat[:, 1, :], stat[:, 0, :]).then_inc(var_ready.sem, 1)
            e.wait_ge(*levelled.at(1))
            for k in range(0 if gemm else n):
                if b is not None:
                    ins = e.tensor_tensor(y[:, k, :], taken[:, k, :], root[:, :], ALU.mult)
                else:
                    ins = e.scalar_tensor_tensor(out=y[:, k, :], in0=taken[:, k, :], scalar=g[:, k:k + 1],
                                                 in1=root[:, :], op0=ALU.mult, op1=ALU.mult)
                ins.then_inc(scaled.sem, 1)
            for k in range(n if parts and not gemm else 0):
                e.wait_ge(*hi_ready.at(k + 1))
                e.tensor_tensor(core.AL[:, at + k, :], y[:, k, :], core.AH[:, at + k, :].bitcast(F32), ALU.subtract)
            if gemm:
                gemm.first_lo(e)
            core.n_chain = chain.n

    here = gemm is None
    core.ended(norm_squared=n, norm_summed=n + offset, norm_centred=offset, norm_var=1, norm_rooted=1,
               norm_scaled=n * here, norm_hi=n * parts * here, norm_chain=core.n_chain, norm_levelled=1,
               norm_placed=n * (b is not None) * here)
    if gemm:
        def scale(e, k):
            if b is not None:
                return e.tensor_tensor(y[:, k, :], taken[:, k, :], root[:, :], ALU.mult)
            return e.scalar_tensor_tensor(out=y[:, k % 2, :], in0=taken[:, k, :], scalar=g[:, k:k + 1],
                                          in1=root[:, :], op0=ALU.mult, op1=ALU.mult)

        def place(e, k):
            return e.activation(y[:, k, :], y[:, k, :], ACT.Identity, scale=g[:, k:k + 1], bias=b[:, k:k + 1])

        gemm.lead = Lead(core, n, lambda k: y[:, k if b is not None else k % 2, :], scale, place if b is not None else None)



UN = 2 * P


class Job:

    def __init__(self, units, load, act, epilogue, subs=(KD,), tiles=2, pieces=1, after=0):
        self.units, self.load, self.act, self.tiles, self.pieces, self.after = units, load, act, tiles, pieces, after
        self.epi_act, self.epi_dve, self.links = epilogue
        self.subs, self.S = list(subs), len(subs)


def signal_after(e, instruction, signal):
    if instruction is None:
        e.sem_inc(signal.sem, 1)
    else:
        instruction.then_inc(signal.sem, 1)


def columns(w, first=0, tile_step=P, unit_step=UN):
    view = w.rearrange("(k p) n -> p k n", p=P)

    def load(u, s, t):
        n = min(KD, w.shape[0] // P - KD * s)
        return view[:, KD * s:KD * s + n, bass.ds(u * unit_step + (first + t * tile_step), P)]
    return load


def act_tiles(core, at=0):
    return lambda s, t, k: (core.AH[:, at + k, :], core.AL[:, at + k, :])



def keep(dst, tiles=2, scale=1.0):
    def act(e, u, acc, slot):
        return e.activation(dst[:, bass.ds(u * tiles, tiles), 0:T // 2], acc[:, 0:tiles, 0:T // 2], ACT.Copy)

    def dve(e, chain, u, acc, slot):
        return e.tensor_copy(dst[:, bass.ds(u * tiles, tiles), T // 2:T], acc[:, 0:tiles, T // 2:T])
    return act, dve, 0


def keep_shifted(core, dst, share, tiles=2):
    def act(e, u, acc, slot):
        return e.activation(dst[:, bass.ds(u * tiles, tiles), :], acc[:, 0:tiles, :], ACT.Copy)

    def dve(e, chain, u, acc, slot):
        x, diff = dst[:, bass.ds(u * tiles, tiles), :], core.tmp_dve[:, 0:tiles, :]
        e.tensor_scalar(diff[:, :, 0:1], x[:, :, 0:1], -1.0, None, ALU.mult)
        chain.link(e.tensor_tensor(diff[:, :, 1:T], x[:, :, 0:T - 1], x[:, :, 1:T], ALU.subtract))
        chain.link(e.tensor_tensor(diff, diff, share[:, bass.ds(u * tiles, tiles)].unsqueeze(2).broadcast_to([P, tiles, T]),
                                   ALU.mult))
        return e.tensor_tensor(x, x, diff, ALU.add)
    return act, dve, 2


def keep_sigmoid(dst):
    def act(e, u, acc, slot):
        return e.activation(dst[:, bass.ds(u * 2, 2), :], acc[:, :, :], ACT.Sigmoid)
    return act, lambda e, chain, u, acc, slot: None, 0


def residual(core, alpha=1.0):
    def dve(e, chain, u, acc, slot):
        x = core.x[:, bass.ds(u * 2, 2), :]
        return e.scalar_tensor_tensor(out=x, in0=x, scalar=alpha, in1=acc[:, :, :], op0=ALU.mult, op1=ALU.add)
    return lambda e, u, acc, slot: None, dve, 0


def relu_squared(core, hid_hi, hid_lo):
    def act(e, u, acc, slot):
        return e.activation(core.tmp_act[:, slot, :, :], acc[:, :, :], ACT.Relu)

    def dve(e, chain, u, acc, slot):
        r, y = core.tmp_act[:, slot, :, :], core.tmp_dve[:, :, :]
        hi, lo = hid_hi[:, bass.ds(u * 2, 2), :], hid_lo[:, bass.ds(u * 2, 2), :]
        chain.link(e.tensor_tensor(y, r, r, ALU.mult))
        chain.link(e.tensor_copy(hi, y))
        return e.tensor_tensor(lo, y, hi.bitcast(F32), ALU.subtract)
    return act, dve, 2


def silu_times(core, hid_hi, hid_lo):
    def act(e, u, acc, slot):
        return e.activation(core.tmp_act[:, slot, 0, :], acc[:, 0, :], ACT.Silu)

    def dve(e, chain, u, acc, slot):
        y = core.tmp_dve[:, 0, :]
        hi, lo = hid_hi[:, bass.ds(u, 1), :], hid_lo[:, bass.ds(u, 1), :]
        chain.link(e.tensor_tensor(y, core.tmp_act[:, slot, 0, :], acc[:, 1, :], ALU.mult))
        chain.link(e.tensor_copy(hi, core.tmp_dve[:, 0:1, :]))
        return e.tensor_tensor(lo, core.tmp_dve[:, 0:1, :], hi.bitcast(F32), ALU.subtract)
    return act, dve, 2


def gated_sum(core, gates):
    def dve(e, chain, u, acc, slot):
        g_a, g_b = gates[:, bass.ds(u, 1), :], gates[:, bass.ds(u + KD, 1), :]
        chain.link(e.tensor_tensor(core.tmp_dve[:, 0:1, :], g_b, acc[:, 1:2, :], ALU.mult))
        chain.link(e.tensor_tensor(g_a, g_a, acc[:, 0:1, :], ALU.mult))
        return e.tensor_tensor(g_a, g_a, core.tmp_dve[:, 0:1, :], ALU.add)
    return lambda e, u, acc, slot: None, dve, 2


class Lead:

    def __init__(self, core, n, tile, scale=None, place=None):
        self.core, self.n, self.tile, self.scale, self.place = core, n, tile, scale, place
        self.scaled, self.placed = core.sig("lead_scaled"), core.sig("lead_placed")
        self.hi, self.lo = core.sig("lead_hi"), core.sig("lead_lo")

    def high_parts(self, e):
        for k in range(self.n):
            if self.scale:
                e.wait_ge(*self.scaled.at(k + 1))
            if self.place:
                self.place(e, k).then_inc(self.placed.sem, 1)
                e.wait_ge(*self.placed.at(k + 1))
            e.activation(self.core.AH[:, k, :], self.tile(k), ACT.Copy).then_inc(self.hi.sem, 1)

    def low_parts(self, e):
        for k in range(self.n + 1):
            if k < self.n and self.scale:
                if k >= 2 and not self.place:
                    e.wait_ge(*self.lo.at(k - 1))
                self.scale(e, k).then_inc(self.scaled.sem, 1)
            if k >= 1:
                e.wait_ge(*self.hi.at(k))
                e.tensor_tensor(self.core.AL[:, k - 1, :], self.tile(k - 1), self.core.AH[:, k - 1, :].bitcast(F32),
                                ALU.subtract).then_inc(self.lo.sem, 1)

    def ended(self):
        for signal, used in ((self.scaled, self.scale), (self.placed, self.place), (self.hi, True), (self.lo, True)):
            if used:
                signal.base += self.n


class Gemm:
    RING = 2

    def __init__(self, core, ctx, jobs):
        R = self.RING
        self.nc, self.ctx, self.jobs, self.ahead, self.lead = core.nc, ctx, jobs, False, None
        self.w32 = core.sb(ctx, "w32", [P, R, KD, UN])
        self.w_hi = [core.sb(ctx, f"w_hi{r}", [P, KD, UN], F32R) for r in range(R)]
        self.w_lo = [core.sb(ctx, f"w_lo{r}", [P, KD, UN], F32R) for r in range(R)]
        self.landed = [core.sig(f"w_landed{r}") for r in range(R)]
        self.hi, self.lo = core.sig("w_hi_ready"), core.sig("w_lo_ready")
        self.used = core.sig("w_used")
        U = G = links = 0
        loads = [0] * R
        for j in jobs:
            j.U0, j.G0 = U, G
            j.base = list(loads)
            j.C0 = links
            links += j.units * j.links
            for n in range(j.units * j.S):
                loads[(G + n) % R] += 16 * j.tiles * j.pieces
            U += j.units
            G += j.units * j.S
        self.all_units, self.all_parts, self.all_links, self.loads = U, G, links, loads

    def landed_at(self, j, it, part):
        slot = (j.G0 + part) % self.RING
        first = (slot - j.G0) % self.RING
        each = 16 * j.tiles * j.pieces
        return slot, it * (j.S * each) + (j.base[slot] + ((part - first) // self.RING + 1) * each)

    def upcoming(self, n, k):
        while n < len(self.jobs):
            j = self.jobs[n]
            if k < j.units * j.S:
                return j, k // j.S, k % j.S
            n, k = n + 1, k - j.units * j.S
        return None

    def load(self, e, j, u, s, slot):
        wide = P // j.pieces
        for t in range(j.tiles):
            for i in range(j.pieces):
                src = j.load(u, s, t) if j.pieces == 1 else j.load(u, s, t, i)
                e.dma_start(self.w32[:, slot, 0:j.subs[s], t * P + i * wide:t * P + (i + 1) * wide], src)\
                 .then_inc(self.landed[slot].sem, 16)

    def split_hi(self, e, j, it, part, s):
        slot, count = self.landed_at(j, it, part)
        kt, cols = j.subs[s], j.tiles * P
        e.wait_ge(*self.landed[slot].at(count))
        e.wait_ge(*self.used.at(it * (2 * j.S) + (j.G0 + part + 1)))
        e.activation(self.w_hi[slot][:, 0:kt, 0:cols], self.w32[:, slot, 0:kt, 0:cols], ACT.Copy)\
         .then_inc(self.hi.sem, 1)

    def split_lo(self, e, j, it, part, s):
        slot, _ = self.landed_at(j, it, part)
        kt, cols = j.subs[s], j.tiles * P
        e.wait_ge(*self.hi.at(it * (2 * j.S) + (j.G0 + part + 3)))
        e.tensor_tensor(self.w_lo[slot][:, 0:kt, 0:cols], self.w32[:, slot, 0:kt, 0:cols],
                        self.w_hi[slot][:, 0:kt, 0:cols].bitcast(F32), ALU.subtract).then_inc(self.lo.sem, 1)

    def first_loads(self, e):
        for k in range(self.RING):
            part = self.upcoming(0, k)
            if part:
                self.load(e, *part, k)

    def first_hi(self, e):
        self.split_hi(e, self.jobs[0], 0, 0, 0)

    def first_lo(self, e):
        self.split_lo(e, self.jobs[0], 0, 0, 0)


def gemm_stage(core, gemm):
    nc, jobs, RING = core.nc, gemm.jobs, gemm.RING
    hi, lo, used, w_hi, w_lo = gemm.hi, gemm.lo, gemm.used, gemm.w_hi, gemm.w_lo
    with ExitStack() as c:
        core.tmp_act = core.sb(c, "tmp_act", [P, 2, 2, T])
        core.tmp_dve = core.sb(c, "tmp_dve", [P, 2, T])
        acc = [core.ps(c, f"acc{r}", [P, 2, T]) for r in range(2)]
        act_done, dve_done = core.sig("epi_act_done"), core.sig("epi_dve_done")
        chained = core.sig("epi_chain")
        block = c.enter_context(nc.Block())

        def walk(e, body, peel=1):
            for n, j in enumerate(jobs):
                rounds = (j.units - peel) // 2
                if rounds >= 2:
                    with e.Fori(0, rounds) as it:
                        for r in range(2):
                            body(n, j, it * 2 + r, it, r, False)
                else:
                    rounds = 0
                for u in range(2 * rounds, j.units):
                    body(n, j, u, 0, u, u == j.units - 1)

        @block.sync
        def _(e):
            def body(n, j, u, it, r, last):
                for s in range(j.S):
                    part = r * j.S + s
                    units_on, s_next = divmod(s + RING, j.S)
                    if isinstance(u, int):
                        target = gemm.upcoming(n, part + RING)
                    else:
                        target = j, it * 2 + (r + units_on), s_next
                    if target:
                        e.wait_ge(*lo.at(it * (2 * j.S) + (j.G0 + part + 3)))
                        gemm.load(e, *target, (j.G0 + part) % RING)
            if not gemm.ahead:
                gemm.first_loads(e)
            walk(e, body, peel=2)

        @block.tensor
        def _(e):
            def body(n, j, u, it, r, last):
                e.wait_ge(*act_done.at(it * 2 + (j.U0 + r + 1)))
                e.wait_ge(*dve_done.at(it * 2 + (j.U0 + r + 1)))
                for s, kt in enumerate(j.subs):
                    part = r * j.S + s
                    slot = (j.G0 + part) % RING
                    e.wait_ge(*hi.at(it * (2 * j.S) + (j.G0 + part + 3)))
                    e.wait_ge(*lo.at(it * (2 * j.S) + (j.G0 + part + 3)))
                    if j.after:
                        before = jobs[n - 1]
                        needed = min(-(-KD * (s + 1) // j.after), before.units)
                        e.wait_ge(*act_done.at(before.U0 + needed + 2))
                        e.wait_ge(*dve_done.at(before.U0 + needed + 2))
                    for t in range(j.tiles):
                        cols = slice(t * P, (t + 1) * P)
                        out = acc[(j.U0 + r) % 2][:, t, :]
                        for k in range(kt):
                            tile = t * kt + k if gemm.lead and kt < gemm.lead.n else k
                            if gemm.lead and n == r == s == 0 and (t == 0 or tile > k):
                                e.wait_ge(*gemm.lead.lo.at(tile + 1))
                            a_hi, a_lo = j.act(s, t, k)
                            ends = s == j.S - 1 and k == kt - 1
                            e.matmul(out, w_hi[slot][:, k, cols], a_hi, start=(s == 0 and k == 0), stop=False)
                            e.matmul(out, w_hi[slot][:, k, cols], a_lo, start=False, stop=False)
                            mm = e.matmul(out, w_lo[slot][:, k, cols], a_hi, start=False, stop=ends)
                    mm.then_inc(used.sem, 1)
            walk(e, body)

        def splitter(e, first, one):
            def body(n, j, u, it, r, last):
                for s in range(j.S):
                    part = r * j.S + s + 1
                    ends = s == j.S - 1
                    if not (last and ends):
                        one(j, it, part, (s + 1) % j.S)
                    elif n + 1 < len(jobs):
                        one(jobs[n + 1], 0, 0, 0)
                    if ends:
                        first(j, u, it, r)
            if not gemm.ahead:
                one(jobs[0], 0, 0, 0)
            walk(e, body)

        @block.scalar
        def _(e):
            if gemm.lead:
                gemm.lead.high_parts(e)

            def one(j, it, part, s):
                gemm.split_hi(e, j, it, part, s)

            def epilogue(j, u, it, r):
                e.wait_ge(*used.at(it * (2 * j.S) + (j.G0 + (r + 1) * j.S + 2)))
                e.wait_ge(*dve_done.at(it * 2 + (j.U0 + r + 1)))
                signal_after(e, j.epi_act(e, u, acc[(j.U0 + r) % 2], (j.U0 + r) % 2), act_done)
            splitter(e, epilogue, one)

        @block.vector
        def _(e):
            if gemm.lead:
                gemm.lead.low_parts(e)

            def one(j, it, part, s):
                gemm.split_lo(e, j, it, part, s)

            def epilogue(j, u, it, r):
                chain = Chain(e, chained, it * (2 * j.links) + (j.C0 + r * j.links))
                e.wait_ge(*act_done.at(it * 2 + (j.U0 + r + 3)))
                e.wait_ge(*dve_done.at(it * 2 + (j.U0 + r + 2)))
                last = j.epi_dve(e, chain, u, acc[(j.U0 + r) % 2], (j.U0 + r) % 2)
                assert chain.n == j.links
                signal_after(e, last, dve_done)
            splitter(e, epilogue, one)

    core.ended(w_hi_ready=gemm.all_parts, w_lo_ready=gemm.all_parts, w_used=gemm.all_parts,
               epi_act_done=gemm.all_units, epi_dve_done=gemm.all_units, epi_chain=gemm.all_links,
               **{f"w_landed{r}": gemm.loads[r] for r in range(RING)})


def linear(core, jobs, prepare=None, split=None):
    with ExitStack() as c:
        gemm = Gemm(core, c, jobs)
        if prepare:
            gemm.ahead = True
            prepare(gemm)
        if split is not None:
            gemm.lead = Lead(core, KD, lambda k: split[:, k, :])
        gemm_stage(core, gemm)
        if gemm.lead:
            gemm.lead.ended()


QUAD = 4
OCT = 2 * QUAD
UNITS = OCT * NT
PAIRS = OCT // 2
S_SLOTS, P_SLOTS = 3, 4
WINDOW = 2 * P


def wide_operands(core, ctx):
    return [core.sb(ctx, s, [P, 2, QUAD, T]) for s in ("q_now", "k_now")]


def attention_stage(core, iterations, q, k, v, out, scale, mask=None, near=None, rope=None, placed=None):
    nc = core.nc
    all_links = PAIRS
    wide = rope or placed
    with ExitStack() as c:
        if wide:
            qs, ks = placed or wide_operands(core, c)
        else:
            qs, ks = (core.sb(c, s, [P, 2, 2, T]) for s in ("q_now", "k_now"))
        v_raw = core.sb(c, "v_raw", [P, 2, 2, T])
        v_tok = core.sb(c, "v_tok", [P, 2, 2, NT, P])
        probs = core.sb(c, "probs", [P, P_SLOTS, T])
        probs_T = core.sb(c, "probs_T", [P, 2, NT, P])
        o_tok = core.sb(c, "o_tok", [P, 2, NT, P])
        neg_max = core.sb(c, "neg_max", [P, 4])
        sums = core.sb(c, "exp_sums", [P, 2, 8])
        inverse = core.sb(c, "inverse_sums", [P, 2, 8])
        score = [core.ps(c, f"score{s}", [P, T]) for s in range(S_SLOTS)]
        turned = [core.ps(c, f"turned{s}", [P, NT, P]) for s in range(2)]
        flip = core.ps(c, "flip", [P, NT, P])
        o_bank = [core.ps(c, f"o_bank{s}", [P, T]) for s in range(2)]
        q_staged, k_staged, v_staged = core.sig("at_q_staged"), core.sig("at_k_staged"), core.sig("at_v_staged")
        v_turned, v_ready = core.sig("at_v_turned"), core.sig("at_v_ready")
        scored, maxed, exped = core.sig("at_scored"), core.sig("at_maxed"), core.sig("at_exped")
        p_turned, p_ready, pv_done = core.sig("at_p_turned"), core.sig("at_p_ready"), core.sig("at_pv_done")
        o_scaled, o_turned, o_kept = core.sig("at_o_scaled"), core.sig("at_o_turned"), core.sig("at_o_kept")
        rope_placed, chained = core.sig("at_rope_placed"), core.sig("at_chain")
        block = c.enter_context(nc.Block())

        def over(e, body):
            if iterations == 1:
                body(0)
            else:
                with e.Fori(0, iterations) as it:
                    body(it)

        def unit(n):
            return n // 16, n // 8 % 2, n // 4 % 2, n % 4, (n % 4 + 1) * P

        def operands(n):
            quad, a, j, _, _ = unit(n)
            return (slice(0, HD + 32), 2 * a + j) if wide else (slice(HD * j, HD * j + HD), a)

        @block.gpsimd
        def _(e):
            def iteration(it):
                for quad in range(2):
                    e.wait_ge(*v_turned.at(it * PAIRS + (2 * quad - 2)))
                    e.tensor_copy(v_raw[:, quad, :, :], v(it * 2 + quad)).then_inc(v_staged.sem, 1)
                    if not wide:
                        e.wait_ge(*scored.at(it * UNITS + (16 * quad - 16)))
                        e.tensor_copy(ks[:, quad, :, :], k(it * 2 + quad)).then_inc(k_staged.sem, 1)
            over(e, iteration)

        @block.tensor
        def _(e):
            def turn_v(it, r):
                quad, a = r // 2, r % 2
                e.wait_ge(*v_staged.at(it * 2 + (quad + 1)))
                if r == 0:
                    e.wait_ge(*o_kept.at(it * PAIRS))
                else:
                    e.wait_ge(*v_ready.at(it * PAIRS + r))
                for kt in range(NT):
                    last = e.transpose(flip[:, kt, :], v_raw[:, quad, a, kt * P:(kt + 1) * P], core.ident[:, :])
                last.then_inc(v_turned.sem, 1)

            def turn_o(it, r):
                e.wait_ge(*o_scaled.at(it * PAIRS + (r + 1)))
                if r == 0:
                    e.wait_ge(*v_ready.at(it * PAIRS + PAIRS))
                else:
                    e.wait_ge(*o_kept.at(it * PAIRS + r))
                for i in range(NT):
                    last = e.transpose(flip[:, i, :], o_tok[:, r % 2, i, :], core.ident[:, :])
                last.then_inc(o_turned.sem, 1)

            def scores(it, n):
                quad, a, j, i, keys = unit(n)
                rows, tile = operands(n)
                cols = slice(P * i, P * i + P)
                if n == 0 and rope:
                    e.wait_ge(*rope_placed.at(1))
                if n % 16 == 0:
                    e.wait_ge(*q_staged.at(it * 2 + (quad + 1)))
                    e.wait_ge(*k_staged.at(it * 2 + (quad + 1)))
                e.wait_ge(*exped.at(it * UNITS + (n - S_SLOTS + 1)))
                s = score[n % S_SLOTS]
                e.matmul(s[:, 0:keys], qs[rows, quad, tile, cols], ks[rows, quad, tile, 0:keys], start=True, stop=False)
                if near is None:
                    last = e.matmul(s[:, cols], core.ident16[:, :], mask[:, :], start=False, stop=True)
                else:
                    window = min(keys, WINDOW)
                    last = e.matmul(s[:, keys - window:keys], core.ident[:, :], near[:, n // 4, WINDOW - window:WINDOW],
                                    start=False, stop=True)
                last.then_inc(scored.sem, 1)

            def turn(it, n):
                i = unit(n)[3]
                e.wait_ge(*exped.at(it * UNITS + (n + 1)))
                e.wait_ge(*p_ready.at(it * UNITS + (n - 1)))
                for kt in range(i + 1):
                    last = e.transpose(turned[n % 2][:, kt, :], probs[:, n % P_SLOTS, kt * P:(kt + 1) * P],
                                       core.ident[:, :])
                last.then_inc(p_turned.sem, 1)

            def values(it, n):
                quad, a, j, i, _ = unit(n)
                r = n // 8
                e.wait_ge(*p_ready.at(it * UNITS + (n + 1)))
                if n % 8 == 0:
                    e.wait_ge(*v_ready.at(it * PAIRS + (r + 1)))
                    e.wait_ge(*o_scaled.at(it * PAIRS + (r - 1)))
                for kt in range(i + 1):
                    last = e.matmul(o_bank[r % 2][:, (n % 8) * HD:(n % 8 + 1) * HD], probs_T[:, n % 2, kt, :],
                                    v_tok[:, quad, a, kt, HD * j:HD * j + HD], start=(kt == 0), stop=(kt == i))
                last.then_inc(pv_done.sem, 1)

            def iteration(it):
                turn_v(it, 0)
                scores(it, 0)
                turn_v(it, 1)
                for n in range(1, UNITS + 4):
                    if n < UNITS:
                        scores(it, n)
                    if n in (8, 10):
                        turn_v(it, 2 if n == 8 else 3)
                    if 3 <= n < UNITS + 3:
                        turn(it, n - 3)
                    if n >= 4:
                        values(it, n - 4)
                    if n % 8 == 6 and n > 8:
                        turn_o(it, n // 8 - 1)
                turn_o(it, PAIRS - 1)
            over(e, iteration)

        @block.vector
        def _(e):
            if rope:
                for quad in range(2):
                    last = e.tensor_copy(ks[HD:HD + 32, quad, :, :], spread(rope[1], QUAD))
                last.then_inc(rope_placed.sem, 1)

            def stage_k(it, quad):
                e.wait_ge(*scored.at(it * UNITS + (16 * quad - 16)))
                for j in range(2):
                    last = e.tensor_copy(ks[0:HD, quad, j:QUAD:2, :], k(it * 2 + quad)[HD * j:HD * j + HD])
                last.then_inc(k_staged.sem, 1)

            def maximum(it, n):
                keys = unit(n)[4]
                e.wait_ge(*scored.at(it * UNITS + (n + 1)))
                e.tensor_reduce(neg_max[:, n % 4:n % 4 + 1], score[n % S_SLOTS][:, 0:keys], AX.X, ALU.max, negate=True)\
                 .then_inc(maxed.sem, 1)

            def divide(it, r, chain):
                e.wait_ge(*pv_done.at(it * UNITS + 8 * (r + 1)))
                e.wait_ge(*o_turned.at(it * PAIRS + (r - 1)))
                chain.link(e.reciprocal(inverse[:, r % 2, :], sums[:, r % 2, :]))
                e.tensor_tensor(o_tok[:, r % 2, :, :].rearrange("p i (j d) -> p j i d", j=2),
                                o_bank[r % 2][:, :].rearrange("p (j i d) -> p j i d", j=2, i=NT),
                                spread(inverse[:, r % 2, :], HD, 2).rearrange("p (j i) d -> p j i d", j=2),
                                ALU.mult).then_inc(o_scaled.sem, 1)

            def keep_o(it, r):
                e.wait_ge(*o_turned.at(it * PAIRS + (r + 1)))
                e.tensor_copy(out(it * PAIRS + r), flip[:, :, :].rearrange("p i f -> p (i f)")).then_inc(o_kept.sem, 1)

            def iteration(it):
                chain = Chain(e, chained, it * all_links)
                if wide:
                    stage_k(it, 0)
                for n in range(UNITS + 1):
                    if n < UNITS:
                        maximum(it, n)
                    if n == 4 and wide:
                        stage_k(it, 1)
                    if n % 8 == 4 and n > 8:
                        divide(it, n // 8 - 1, chain)
                    if n % 8 == 7 and n > 8:
                        keep_o(it, n // 8 - 1)
                divide(it, PAIRS - 1, chain)
                keep_o(it, PAIRS - 1)
                core.n_chain = chain.n
            over(e, iteration)

        @block.scalar
        def _(e):
            def stage_q(it, quad):
                e.wait_ge(*scored.at(it * UNITS + (16 * quad - 16)))
                if wide:
                    for j in range(2):
                        last = e.activation(qs[0:HD, quad, j:QUAD:2, :], q(it * 2 + quad)[HD * j:HD * j + HD], ACT.Copy,
                                            scale=scale)
                    for h in range(QUAD if rope else 0):
                        last = e.activation(qs[HD:HD + 32, quad, h, :], rope[0](it * 2 + quad)[32 * h:32 * h + 32],
                                            ACT.Copy, scale=scale)
                else:
                    last = e.activation(qs[:, quad, :, :], q(it * 2 + quad), ACT.Copy, scale=scale)
                last.then_inc(q_staged.sem, 1)

            def exponentials(it, n):
                keys = unit(n)[4]
                e.wait_ge(*maxed.at(it * UNITS + (n + 1)))
                e.wait_ge(*p_turned.at(it * UNITS + (n - P_SLOTS + 1)))
                if n % 8 == 0:
                    e.wait_ge(*o_scaled.at(it * PAIRS + (n // 8 - 1)))
                e.activation(probs[:, n % P_SLOTS, 0:keys], score[n % S_SLOTS][:, 0:keys], ACT.Exp, bias=neg_max[:, n % 4:n % 4 + 1],
                             accum_out=sums[:, n // 8 % 2, n % 8:n % 8 + 1]).then_inc(exped.sem, 1)

            def copy_turned(it, n):
                i = unit(n)[3]
                e.wait_ge(*p_turned.at(it * UNITS + (n + 1)))
                e.wait_ge(*pv_done.at(it * UNITS + (n - 1)))
                e.activation(probs_T[:, n % 2, 0:i + 1, :], turned[n % 2][:, 0:i + 1, :], ACT.Copy)\
                 .then_inc(p_ready.sem, 1)

            def copy_v(it, r):
                e.wait_ge(*v_turned.at(it * PAIRS + (r + 1)))
                e.activation(v_tok[:, r // 2, r % 2, :, :], flip[:, :, :], ACT.Copy).then_inc(v_ready.sem, 1)

            def iteration(it):
                stage_q(it, 0)
                copy_v(it, 0)
                copy_v(it, 1)
                for n in range(UNITS + 3):
                    if n < UNITS:
                        exponentials(it, n)
                    if n == 4:
                        stage_q(it, 1)
                    if n in (8, 10):
                        copy_v(it, 2 if n == 8 else 3)
                    if n >= 3:
                        copy_turned(it, n - 3)
            over(e, iteration)

    assert core.n_chain == all_links, (core.n_chain, all_links)
    per_iteration = dict.fromkeys(("at_scored", "at_maxed", "at_exped", "at_p_turned", "at_p_ready",
                                   "at_pv_done"), UNITS)
    per_iteration |= dict.fromkeys(("at_q_staged", "at_k_staged", "at_v_staged"), 2)
    per_iteration |= dict.fromkeys(("at_v_turned", "at_v_ready", "at_o_scaled", "at_o_turned", "at_o_kept"), PAIRS)
    per_iteration["at_chain"] = all_links
    core.ended(**{name: n * iterations for name, n in per_iteration.items()})
    if rope:
        core.counters["at_rope_placed"].base += 1


def forget_stage(core, fa, forget_bias, qs, ks):
    nc, H = core.nc, 8
    with ExitStack() as c:
        fb = core.sb(c, "forget_bias", [H, 1])
        z, mag, soft, log_f, cum, one = (core.sb(c, s, [H, T]) for s in
                                         ("f_z", "f_abs", "f_soft", "f_log", "f_cum", "f_one"))
        wide = HD + 32
        pick = core.sb(c, "pick_head", [H, H, wide])
        bank = [core.ps(c, f"f_bank{s}", [P, T]) for s in range(2)]
        loaded, picked, soft_ready = core.sig("f_loaded"), core.sig("f_picked"), core.sig("f_soft_ready")
        mag_ready, cum_ready = core.sig("f_abs_ready"), core.sig("f_cum_ready")
        spread, kept, own, act_own = core.sig("f_spread"), core.sig("f_kept"), core.sig("f_chain"), core.sig("f_act_chain")
        block = c.enter_context(nc.Block())

        @block.sync
        def _(e):
            e.dma_start(fb[:, :], forget_bias[0].rearrange("(h o) -> h o", o=1)).then_inc(loaded.sem, 16)

        @block.gpsimd
        def _(e):
            e.memset(one[:, :], 1.0).then_inc(picked.sem, 1)
            e.memset(pick[:, :, :], 0.0).then_inc(picked.sem, 1)
            e.wait_ge(*picked.at(2))
            e.affine_select(out=pick[:, :, HD], in_=pick[:, :, HD], compare_op=ALU.not_equal, fill=1.0, base=0,
                            pattern=[[-1, H]], channel_multiplier=1).then_inc(picked.sem, 1)
            e.memset(qs[HD:wide, :, :, :], 0.0).then_inc(picked.sem, 1)
            e.wait_ge(*picked.at(4))
            e.memset(qs[HD:HD + 1, :, :, :], 1.0)

        @block.vector
        def _(e):
            chain = Chain(e, own)
            e.wait_ge(*loaded.at(16))
            chain.link(e.tensor_scalar(z[:, :], fa[0:H, :], fb[:, 0:1], None, ALU.add))
            e.scalar_tensor_tensor(out=mag[:, :], in0=z[:, :], scalar=-1.0, in1=z[:, :], op0=ALU.mult, op1=ALU.max)\
             .then_inc(mag_ready.sem, 1)
            e.wait_ge(*soft_ready.at(1))
            chain.link(e.scalar_tensor_tensor(out=log_f[:, :], in0=z[:, :], scalar=0.0, in1=soft[:, :],
                                              op0=ALU.min, op1=ALU.subtract))
            e.wait_ge(*picked.at(1))
            chain.link(e.tensor_tensor_scan(cum[:, :], one[:, :], log_f[:, :], 0.0, ALU.mult, ALU.add))
            e.tensor_scalar(cum[:, :], cum[:, :], -1.0, None, ALU.mult).then_inc(cum_ready.sem, 1)
            core.n_chain = chain.n

        @block.scalar
        def _(e):
            e.wait_ge(*mag_ready.at(1))
            Chain(e, act_own).link(e.activation(mag[:, :], mag[:, :], ACT.Exp, scale=-1.0))
            e.activation(soft[:, :], mag[:, :], ACT.Ln, bias=1.0).then_inc(soft_ready.sem, 1)
            for h in range(H):
                e.wait_ge(*spread.at(h + 1))
                e.activation(ks[HD:wide, h // QUAD, h % QUAD, :], bank[h % 2][HD:wide, :], ACT.Copy).then_inc(kept.sem, 1)

        @block.tensor
        def _(e):
            e.wait_ge(*picked.at(3))
            e.wait_ge(*cum_ready.at(1))
            for h in range(H):
                if h >= 2:
                    e.wait_ge(*kept.at(h - 1))
                e.matmul(bank[h % 2][0:wide, :], pick[:, h, :], cum[:, :], start=True, stop=True).then_inc(spread.sem, 1)
    core.ended(f_loaded=16, f_picked=4, f_soft_ready=1, f_abs_ready=1, f_cum_ready=1, f_spread=H, f_kept=H,
               f_chain=core.n_chain, f_act_chain=1)


EXTENDED = MAX_REL * 2 + 1 + P - 1


def relative_stage(core, rel_bias, scratch, mask, near, qs, ks):
    nc, H, last = core.nc, 8, 2 * MAX_REL
    with ExitStack() as c:
        ext = core.sb(c, "rel_extended", [H, EXTENDED])
        window = core.sb(c, "rel_window", [P, H, WINDOW])
        far = core.sb(c, "rel_far", [P, H])
        loaded, extended = core.sig("rel_loaded"), core.sig("rel_extended")
        stored, windows = core.sig("rel_stored"), core.sig("rel_windows")
        differences = core.sig("rel_differences")
        block = c.enter_context(nc.Block())

        @block.sync
        def _(e):
            e.dma_start(ext[:, 0:last + 1], rel_bias[0]).then_inc(loaded.sem, 16)
            e.wait_ge(*extended.at(1))
            e.dma_start(scratch, ext[:, :]).then_inc(stored.sem, 16)
            e.wait_ge(*stored.at(16))
            e.dma_start(window[:, :, :], bass.AP(scratch.tensor, 1, [[1, P], [EXTENDED, H], [1, WINDOW]]))\
             .then_inc(windows.sem, 16)
            e.dma_start(far[:, :], bass.AP(scratch.tensor, last, [[0, P], [EXTENDED, H]]),
                        allow_slow_non_contiguous=True).then_inc(windows.sem, 16)
            e.wait_ge(*windows.at(32))

        @block.gpsimd
        def _(e):
            for place in (qs, ks):
                e.memset(place[HD:HD + 32, :, :, :], 0.0)

        @block.vector
        def _(e):
            e.wait_ge(*loaded.at(16))
            e.tensor_copy(ext[:, last + 1:EXTENDED],
                          ext[:, last:last + 1].broadcast_to([H, EXTENDED - last - 1])).then_inc(extended.sem, 1)
            e.wait_ge(*windows.at(32))
            e.tensor_tensor(near[:, :, :], window[:, :, ::-1], spread(far[:, :], WINDOW, 2), ALU.subtract)\
             .then_inc(differences.sem, 1)
            e.wait_ge(*differences.at(1))
            e.tensor_tensor(near[:, :, WINDOW - P:WINDOW], near[:, :, WINDOW - P:WINDOW], spread(mask[:, :], H), ALU.add)
    core.ended(rel_loaded=16, rel_extended=1, rel_stored=16, rel_windows=32, rel_differences=1)

class Results:

    def __init__(self, signal, names):
        self.counter, self.names = signal, list(names)
        self.index = {name: n + 1 for n, name in enumerate(self.names)}
        assert len(self.index) == len(self.names)
        self.marked = 0

    def mark(self, instruction, name):
        assert self.names[self.marked] == name, (self.names[self.marked], name)
        self.marked += 1
        instruction.then_inc(self.counter.sem, 1)

    def at(self, name, it=0, ahead=0):
        return self.counter.at(it * len(self.names) + (ahead * len(self.names) + self.index[name]))

    def before(self, it):
        return self.counter.at(it * len(self.names))


GLA_HEADS, GLA_RANK, GLA_EXP = 4, 16, 40.0


def gla_stage(core, A, gla, glr, o):
    nc = core.nc
    H, pairs = range(GLA_HEADS), range(2)
    dve_names = ([f"{s}{p}" for p in pairs for s in ("z", "mag")] +
                 [f"{s}{p}" for p in pairs for s in ("la", "scan", "b", "d", "c1", "c2", "d4")] +
                 [f"{s}{p}" for p in pairs for s in ("qg", "kg", "qx", "kx")] +
                 [f"AT{h}" for h in H] + ["S_zero0", "S_zero1"] +
                 [f"S{p}_{c}" for p in pairs for c in range(1, NCH)] +
                 ["var", "inverse"] + [f"{s}{h}" for h in H for s in ("y", "out")])
    act_names = ([f"{s}{p}" for p in pairs for s in ("e", "l")] + [f"v{h}" for h in H] +
                 [f"{s}{p}" for p in pairs for s in ("E1", "E2", "E3", "E4")] + ["kt0", "kt1"] +
                 [f"{s}{h}" for h in H for s in ("o", "sq")] + ["root"] + [f"silu{h}" for h in H])
    pe_names = (["Z0", "Z1"] + [f"V{h}" for h in H] + ["KX0", "KX1"] + [f"A{h}" for h in H] +
                [f"U0{t}" for t in range(NT)] + ["O0", "O1"] + [f"U1{t}" for t in range(NT)] + ["O2", "O3"] +
                ["sums"] + [f"R{h}" for h in H])
    pool_names = [f"kxm{p}{t}" for p in pairs for t in range(NT)]
    with ExitStack() as c:
        w2 = core.sb(c, "gla_w2", [GLA_RANK, 2 * P])
        z, mag, b, d, c1, c2, d4 = (core.sb(c, f"gla_{s}", [P, 2, T]) for s in ("z", "mag", "b", "d", "c1", "c2", "d4"))
        E1, E2, E3, E4 = c1, c2, core.sb(c, "gla_E3", [P, 2, T]), d4
        qg, kg, qx, kx = (core.sb(c, f"gla_{s}", [P, 2, T]) for s in ("qg", "kg", "qx", "kx"))
        v_tok = core.sb(c, "gla_v_tok", [P, GLA_HEADS, NT, P])
        kx_tok = core.sb(c, "gla_kx_tok", [P, 2, NT, P])
        kxm = core.sb(c, "gla_kx_masked", [P, NT, CPT, P])
        AT = core.sb(c, "gla_AT", [P, GLA_HEADS, NT, P])
        S = [core.sb(c, f"gla_S{p}", [P, NCH, P]) for p in pairs]
        raw = qg, kg
        sq = core.sb(c, "gla_sq", [P, GLA_HEADS, T])
        bank = [core.ps(c, f"gla_bank{n}", [P, T]) for n in range(8)]
        loaded = core.sig("gla_loaded")
        dve, act = Results(core.sig("gla_dve"), dve_names), Results(core.sig("gla_act"), act_names)
        pe, pool = Results(core.sig("gla_pe"), pe_names), Results(core.sig("gla_pool"), pool_names)
        block = c.enter_context(nc.Block())

        def chunks(ap):
            return ap.rearrange("p (c t) -> p c t", t=C32)

        def of_chunk(ap, t):
            return chunks(ap)[:, :, t:t + 1].broadcast_to([P, NCH, C32])

        def stat(h):
            return (z, d)[h // 2][:, h % 2, :]

        def raw_o(h):
            return raw[h // 2][:, h % 2, :]

        @block.sync
        def _(e):
            e.dma_start(w2[:, :], A["gla_gate_w2_2"][0]).then_inc(loaded.sem, 16)

        @block.tensor
        def _(e):
            e.wait_ge(*loaded.at(16))
            for p in pairs:
                pe.mark(e.matmul(bank[6 + p][:, :], w2[:, p * P:(p + 1) * P], glr[0:GLA_RANK, :],
                                 start=True, stop=True), f"Z{p}")
            turned = ([(f"V{h}", gla[:, 4 + h, :], f"v{h}") for h in H] + [(f"KX{p}", kx[:, p, :], f"kt{p}") for p in pairs])
            for n, (name, src, _) in enumerate(turned):
                if n >= 2:
                    e.wait_ge(*act.at(turned[n - 2][2]))
                if name[0] == "K":
                    e.wait_ge(*dve.at(f"kx{name[2]}"))
                for t in range(NT):
                    last = e.transpose(bank[4 + n % 2][:, t * P:(t + 1) * P], src[:, t * P:(t + 1) * P], core.ident[:, :])
                pe.mark(last, name)
            for h in H:
                p, rows = h // 2, slice(HD * (h % 2), HD * (h % 2) + HD)
                e.wait_ge(*dve.at(f"kg{p}"))
                if h >= 2:
                    e.wait_ge(*dve.at(f"AT{h - 2}"))
                for t in range(NT):
                    cols = slice(t * P, (t + 1) * P)
                    last = e.matmul(bank[6 + h % 2][:, cols], kg[rows, p, cols], qg[rows, p, cols], start=True, stop=True)
                pe.mark(last, f"A{h}")
            for p in pairs:
                for t in range(NT):
                    e.wait_ge(*pool.at(f"kxm{p}{t}"))
                    if p:
                        e.wait_ge(*dve.at(f"S0_{min(4 * t + 4, NCH - 1)}"))
                    for j in range(2):
                        for ch in range(CPT):
                            last = e.matmul(bank[t][HD * j:HD * j + HD, ch * P:(ch + 1) * P],
                                            kxm[:, t, ch, HD * j:HD * j + HD], v_tok[:, 2 * p + j, t, :],
                                            start=True, stop=True)
                    pe.mark(last, f"U{p}{t}")
                for h in (2 * p, 2 * p + 1):
                    rows = slice(HD * (h % 2), HD * (h % 2) + HD)
                    e.wait_ge(*act.at("kt1" if p == 0 else f"o{h - 2}"))
                    e.wait_ge(*dve.at(f"AT{h}"))
                    e.wait_ge(*dve.at(f"S{p}_{NCH - 1}"))
                    for t in range(NT):
                        e.matmul(bank[4 + h % 2][:, t * P:(t + 1) * P], v_tok[:, h, t, :], AT[:, h, t, :],
                                 start=True, stop=False)
                        for ch in range(CPT):
                            n = t * CPT + ch
                            cols = slice(n * C32, (n + 1) * C32)
                            last = e.matmul(bank[4 + h % 2][:, cols], S[p][rows, n, :], qx[rows, p, cols],
                                            start=False, stop=(ch == CPT - 1))
                    pe.mark(last, f"O{h}")
            e.wait_ge(*dve.at("AT3"))
            for h in H:
                e.wait_ge(*act.at(f"sq{h}"))
                last = e.matmul(bank[6][32 * h:32 * h + 32, :], core.ones[:, 0:32], sq[:, h, :], start=True, stop=True)
            pe.mark(last, "sums")
            e.wait_ge(*act.at("root"))
            for h in H:
                pe.mark(e.matmul(bank[h][:, :], core.pick_pair_head[:, h, :], b[:, 0, :], start=True, stop=True), f"R{h}")

        @block.gpsimd
        def _(e):
            for p in pairs:
                e.wait_ge(*act.at(f"kt{p}"))
                for t in range(NT):
                    if p:
                        e.wait_ge(*pe.at(f"U0{t}"))
                    src = kx_tok[:, p, t, :].rearrange("p (j k) -> p j k", j=2)
                    for ch in range(CPT):
                        last = e.tensor_tensor(kxm[:, t, ch, :].rearrange("p (j k) -> p j k", j=2), src,
                                               spread(core.in_chunk[:, ch, :], 2), ALU.mult)
                    pool.mark(last, f"kxm{p}{t}")

        @block.vector
        def _(e):
            gb = core.v["gla_b"]
            for p in pairs:
                e.wait_ge(*pe.at(f"Z{p}"))
                dve.mark(e.tensor_scalar(z[:, p, :], bank[6 + p][:, :], gb[:, p:p + 1], None, ALU.add), f"z{p}")
                e.wait_ge(*dve.at(f"z{p}"))
                dve.mark(e.scalar_tensor_tensor(out=mag[:, p, :], in0=z[:, p, :], scalar=-1.0, in1=z[:, p, :],
                                                op0=ALU.mult, op1=ALU.max), f"mag{p}")
            for p in pairs:
                zp, bp, dp = z[:, p, :], b[:, p, :], d[:, p, :]
                e.wait_ge(*act.at(f"l{p}"))
                dve.mark(e.scalar_tensor_tensor(out=zp, in0=zp, scalar=0.0, in1=mag[:, p, :], op0=ALU.min,
                                                op1=ALU.subtract), f"la{p}")
                e.wait_ge(*dve.at(f"la{p}"))
                dve.mark(e.tensor_tensor_scan(dp, core.scan_keep[:, :], zp, 0.0, ALU.mult, ALU.add), f"scan{p}")
                e.wait_ge(*dve.at(f"scan{p}"))
                dve.mark(e.tensor_scalar(bp, dp, 1.0 / 16.0, None, ALU.mult), f"b{p}")
                e.wait_ge(*dve.at(f"b{p}"))
                dve.mark(e.tensor_tensor(chunks(dp), chunks(bp), of_chunk(bp, C32 // 2 - 1), ALU.subtract), f"d{p}")
                e.wait_ge(*dve.at(f"d{p}"))
                dve.mark(e.tensor_scalar(c1[:, p, :], dp, GLA_EXP, None, ALU.min), f"c1{p}")
                dve.mark(e.tensor_scalar(c2[:, p, :], dp, -1.0, GLA_EXP, ALU.mult, ALU.min), f"c2{p}")
                dve.mark(e.tensor_tensor(chunks(d4[:, p, :]), of_chunk(bp, C32 - 1), chunks(bp), ALU.subtract), f"d4{p}")
            for p in pairs:
                e.wait_ge(*act.at(f"E4{p}"))
                q, k = gla[:, p, :], gla[:, 2 + p, :]
                dve.mark(e.scalar_tensor_tensor(out=qg[:, p, :], in0=q, scalar=HD ** -0.5, in1=E1[:, p, :],
                                                op0=ALU.mult, op1=ALU.mult), f"qg{p}")
                dve.mark(e.tensor_tensor(kg[:, p, :], k, E2[:, p, :], ALU.mult), f"kg{p}")
                dve.mark(e.scalar_tensor_tensor(out=qx[:, p, :], in0=q, scalar=HD ** -0.5, in1=E3[:, p, :],
                                                op0=ALU.mult, op1=ALU.mult), f"qx{p}")
                dve.mark(e.tensor_tensor(kx[:, p, :], k, E4[:, p, :], ALU.mult), f"kx{p}")
            for h in H:
                e.wait_ge(*pe.at(f"A{h}"))
                src = bank[6 + h % 2][:, :].rearrange("p (t f) -> p t f", t=NT)
                dve.mark(e.tensor_tensor(AT[:, h, :, :], src, spread(core.tri[:, 1, :], NT), ALU.mult), f"AT{h}")
            for p in pairs:
                dve.mark(e.memset(S[p][:, 0, :], 0.0), f"S_zero{p}")
            for p in pairs:
                for ch in range(1, NCH):
                    n = ch - 1
                    e.wait_ge(*pe.at(f"U{p}{n // CPT}"))
                    e.wait_ge(*dve.at(f"S{p}_{n}" if n else f"S_zero{p}"))
                    u = bank[n // CPT][:, (n % CPT) * P:(n % CPT + 1) * P]
                    dve.mark(e.scalar_tensor_tensor(out=S[p][:, ch, :], in0=S[p][:, n, :],
                                                    scalar=E3[:, p, n * C32 + C32 - 1:n * C32 + C32], in1=u,
                                                    op0=ALU.mult, op1=ALU.add), f"S{p}_{ch}")
            e.wait_ge(*pe.at("sums"))
            dve.mark(e.tensor_scalar(mag[:, 0, :], bank[6][:, :], 1.0 / P, 1e-6, ALU.mult, ALU.add), "var")
            e.wait_ge(*dve.at("var"))
            dve.mark(e.reciprocal(mag[:, 1, :], mag[:, 0, :]), "inverse")
            for h in H:
                e.wait_ge(*pe.at(f"R{h}"))
                dve.mark(e.scalar_tensor_tensor(out=stat(h), in0=raw_o(h), scalar=core.v["gla_g"][:, 0:1], in1=bank[h][:, :],
                                                op0=ALU.mult, op1=ALU.mult), f"y{h}")
                e.wait_ge(*dve.at(f"y{h}"))
                e.wait_ge(*act.at(f"silu{h}"))
                dve.mark(e.tensor_tensor(o[:, h, :], stat(h), sq[:, h, :], ALU.mult), f"out{h}")

        @block.scalar
        def _(e):
            for p in pairs:
                e.wait_ge(*dve.at(f"mag{p}"))
                act.mark(e.activation(mag[:, p, :], mag[:, p, :], ACT.Exp, scale=-1.0), f"e{p}")
                e.wait_ge(*act.at(f"e{p}"))
                act.mark(e.activation(mag[:, p, :], mag[:, p, :], ACT.Ln, bias=1.0), f"l{p}")
            for h in H:
                e.wait_ge(*pe.at(f"V{h}"))
                act.mark(e.activation(v_tok[:, h, :, :], bank[4 + h % 2][:, :].rearrange("p (t f) -> p t f", t=NT),
                                      ACT.Copy), f"v{h}")
            for p in pairs:
                e.wait_ge(*dve.at(f"d4{p}"))
                act.mark(e.activation(E1[:, p, :], c1[:, p, :], ACT.Exp), f"E1{p}")
                act.mark(e.activation(E2[:, p, :], c2[:, p, :], ACT.Exp), f"E2{p}")
                act.mark(e.activation(E3[:, p, :], b[:, p, :], ACT.Exp), f"E3{p}")
                act.mark(e.activation(E4[:, p, :], d4[:, p, :], ACT.Exp), f"E4{p}")
            for p in pairs:
                e.wait_ge(*pe.at(f"KX{p}"))
                act.mark(e.activation(kx_tok[:, p, :, :], bank[4 + p][:, :].rearrange("p (t f) -> p t f", t=NT),
                                      ACT.Copy), f"kt{p}")
            for h in H:
                e.wait_ge(*pe.at(f"O{h}"))
                act.mark(e.activation(raw_o(h), bank[4 + h % 2][:, :], ACT.Copy), f"o{h}")
                e.wait_ge(*act.at(f"o{h}"))
                act.mark(e.activation(sq[:, h, :], raw_o(h), ACT.Square), f"sq{h}")
            e.wait_ge(*dve.at("inverse"))
            act.mark(e.activation(b[:, 0, :], mag[:, 1, :], ACT.Sqrt), "root")
            for h in H:
                act.mark(e.activation(sq[:, h, :], gla[:, 8 + h, :], ACT.Silu), f"silu{h}")
    core.ended(gla_loaded=16, gla_dve=len(dve_names), gla_act=len(act_names), gla_pe=len(pe_names),
               gla_pool=len(pool_names))


RW_DECAY, RW_GN_EPS = 0.6065306597126334, 64e-5


def rwkv_prepare_stage(core, A, rw, decay, rate, gate):
    nc = core.nc
    pairs = range(4)
    dve_names = [f"decay{p}" for p in pairs]
    act_names = ["tanh", "low_a", "sig13", "sig14"] + [f"{s}{p}" for p in pairs for s in ("w", "a", "g")]
    pe_names = [f"{s}{p}" for p in pairs for s in ("W", "A", "G")]
    with ExitStack() as c:
        w2, a2 = (core.sb(c, s, [P, T]) for s in ("w2", "a2"))
        g2 = core.sb(c, "g2", [P, 2, T])
        zeroed = core.sig("rwp_zeroed")
        low = core.sb(c, "low_rank", [P, 3, T])
        bank = [core.ps(c, f"rwp_bank{n}", [P, T]) for n in range(6)]
        loaded = core.sig("rwp_loaded")
        dve, act, pe = (Results(core.sig(f"rwp_{s}"), n) for s, n in
                        (("dve", dve_names), ("act", act_names), ("pe", pe_names)))
        block = c.enter_context(nc.Block())

        @block.sync
        def _(e):
            e.wait_ge(*zeroed.at(4))
            for dst, src in ((w2[0:HD, :], A["rwkv_w2_2"][0]), (a2[HD:P, :], A["rwkv_a2_2"][0]),
                             (g2[:, 0, :], A["rwkv_g2_2"][0][0:P]), (g2[96:P, 1, :], A["rwkv_g2_2"][0][P:P + 32])):
                e.dma_start(dst, src).then_inc(loaded.sem, 16)

        @block.gpsimd
        def _(e):
            for part in (w2[:, :], a2[:, :], g2[:, 1, :], low[:, 2, :]):
                e.memset(part, 0.0).then_inc(zeroed.sem, 1)

        @block.vector
        def _(e):
            for p in pairs:
                e.wait_ge(*act.at(f"w{p}"))
                dve.mark(e.tensor_scalar(decay[:, p, :], decay[:, p, :], -RW_DECAY, None, ALU.mult), f"decay{p}")

        @block.scalar
        def _(e):
            act.mark(e.activation(low[0:HD, 0, :], rw[0:HD, 12, :], ACT.Tanh), "tanh")
            act.mark(e.activation(low[HD:P, 0, :], rw[HD:P, 12, :], ACT.Copy), "low_a")
            e.wait_ge(*zeroed.at(4))
            act.mark(e.activation(low[:, 1, :], rw[:, 13, :], ACT.Sigmoid), "sig13")
            act.mark(e.activation(low[96:P, 2, :], rw[96:P, 14, :], ACT.Sigmoid), "sig14")
            for p in pairs:
                b = 3 * (p % 2)
                e.wait_ge(*pe.at(f"W{p}"))
                act.mark(e.activation(decay[:, p, :], bank[b][:, :], ACT.Sigmoid, bias=core.v["w0"][:, p:p + 1]), f"w{p}")
                e.wait_ge(*pe.at(f"A{p}"))
                act.mark(e.activation(rate[:, p, :], bank[b + 1][:, :], ACT.Sigmoid, bias=core.v["a0"][:, p:p + 1]), f"a{p}")
                e.wait_ge(*pe.at(f"G{p}"))
                act.mark(e.activation(gate[:, p, :], bank[b + 2][:, :], ACT.Copy), f"g{p}")

        @block.tensor
        def _(e):
            e.wait_ge(*loaded.at(64))
            e.wait_ge(*act.at("sig14"))
            for p in pairs:
                cols, b = slice(p * P, (p + 1) * P), 3 * (p % 2)
                if p >= 2:
                    e.wait_ge(*act.at(f"g{p - 2}"))
                pe.mark(e.matmul(bank[b][:, :], w2[:, cols], low[:, 0, :], start=True, stop=True), f"W{p}")
                pe.mark(e.matmul(bank[b + 1][:, :], a2[:, cols], low[:, 0, :], start=True, stop=True), f"A{p}")
                e.matmul(bank[b + 2][:, :], g2[:, 0, cols], low[:, 1, :], start=True, stop=False)
                pe.mark(e.matmul(bank[b + 2][:, :], g2[:, 1, cols], low[:, 2, :], start=False, stop=True), f"G{p}")
    core.ended(rwp_loaded=64, rwp_zeroed=4, rwp_dve=len(dve_names), rwp_act=len(act_names), rwp_pe=len(pe_names))


def rwkv_chunks_stage(core, rw, decay, rate, o, o_at, G, F):
    nc = core.nc
    J, PAIRS4 = range(2), 4
    both = lambda s: [f"{s}{j}" for j in J]
    fills = ([("TA", "A"), ("TB", "A"), ("TK", "A"), ("TV", "A")] +
             [(f"{s}{j}", eng) for j in J for s, eng in (("BAa", "D"), ("BAb", "D"), ("M", "D"), ("KAa", "D"), ("KAb", "D"))] +
             [(f"{s}{j}", eng) for j in J for s, eng in (("M2", "A"), ("T2", "D"), ("AV", "A"))] +
             [(f"{s}{j}", eng) for j in J for s, eng in (("M4", "A"), ("T4", "A"), ("X2", "D"))] +
             [(f"{s}{j}", eng) for j in J for s, eng in (("M8", "A"), ("T8", "A"), ("X4", "D"))] +
             [(f"{s}{j}", eng) for j in J for s, eng in (("M16", "A"), ("X8", "D"))] +
             [(f"X16{j}", "D") for j in J] + [(f"P{j}", "A") for j in J] + [("Q", "D")] +
             [("Ga", "D"), ("Gb", "D"), ("Fa", "A"), ("Fb", "A"), ("Y", "A")])
    number = {name: n for n, (name, _) in enumerate(fills)}
    taken_by = dict(fills)
    BANKS = 7
    dve_names = ([f"{s}{j}" for j in J for s in ("BAa", "BAb", "M", "X1", "KAa", "KAb")] +
                 both("T2") + both("X2") + both("X4") + both("X8") + both("X16") + ["Q", "Ga", "Gb"])
    act_names = (["TA", "TB", "TK", "TV"] +
                 [f"{s}{j}" for j in J for s in ("M2", "AV")] + [f"{s}{j}" for j in J for s in ("M4", "T4")] +
                 [f"{s}{j}" for j in J for s in ("M8", "T8")] + both("M16") + both("P") + ["Fa", "Fb", "Y"])
    pool_names = [f"{s}{j}" for s in ("Bm", "Km") for j in J] + ["q_decayed", "G_decayed"]
    pe_names = [name for name, _ in fills]
    ready_dve = ["kk0", "t", "kx", "scan", "cx", "last", "NORM", "rn_a", "rn_b", "kk", "ah", "bb", "bh", "kh", "rk", "rh", "BONUS"]
    ready_act = ["sq", "Ew", "En", "Ex", "root"]
    with ExitStack() as c:
        f = {s: core.sb(c, f"rw_{s}", [P, T]) for s in ("cw", "cx", "En", "Ew", "s1", "s2", "bh", "kh")}
        f |= {"kk": rw[:, 12, :], "k2": rw[:, 13, :], "v": rw[:, 14, :], "t": f["s1"], "bb": rw[:, 12, :]}
        ar = core.sb(c, "rw_ar", [P, 2, T])
        last_w = core.sb(c, "rw_last_w", [P, PAIRS4, NCH])
        tok_b, tok_k, tok_v = (core.sb(c, f"rw_tok_{s}", [P, NT, P]) for s in "bkv")
        av = [core.sb(c, f"rw_av{j}", [P, NT, P]) for j in J]
        ba = [core.sb(c, f"rw_ba{j}", [P, NT, 2, P]) for j in J]
        ka = [core.sb(c, f"rw_ka{j}", [P, NT, 2, P]) for j in J]
        Ms = [[core.sb(c, f"rw_M{j}{s}", [P, NT, P]) for s in range(2)] for j in J]
        Ts = [[core.sb(c, f"rw_T{j}{s}", [P, NT, P]) for s in range(2)] for j in J]
        XT = [core.sb(c, f"rw_XT{j}", [P, NT, P]) for j in J]
        PP = av
        bm = [core.sb(c, f"rw_bm{j}", [P, NT, CPT, HD]) for j in J]
        km = [core.sb(c, f"rw_km{j}", [P, NT, CPT, HD]) for j in J]
        bank = [core.ps(c, f"rw_bank{n}", [P, T]) for n in range(BANKS)]
        ready_bank = core.ps(c, "rw_ready_bank", [P, T])
        dve, act = Results(core.sig("rw_dve"), dve_names), Results(core.sig("rw_act"), act_names)
        pe, pool = Results(core.sig("rw_pe"), pe_names), Results(core.sig("rw_pool"), pool_names)
        made_dve, made_act = Results(core.sig("rw_made_dve"), ready_dve), Results(core.sig("rw_made_act"), ready_act)
        made_pe = Results(core.sig("rw_made_pe"), ["NORM", "BONUS"])
        made_v = core.sig("rw_made_v")
        block = c.enter_context(nc.Block())

        def taken(name, it):
            return (dve if taken_by[name] == "D" else act).at(name, it)

        def bank_of(name):
            return bank[number[name] % BANKS]

        def tiles4(name):
            return bank_of(name)[:, :].rearrange("p (t f) -> p t f", t=NT)

        def row(tensor, tile):
            return tensor[:, bass.ds(tile, 1), :].rearrange("p o t -> p (o t)")

        def over_pairs(e, body):
            with e.Fori(0, PAIRS4 - 1) as it:
                body(it, True)
            body(PAIRS4 - 1, False)

        @block.gpsimd
        def _(e):
            def copy_v(it):
                e.tensor_copy(f["v"][:, :], row(rw, it + 8)).then_inc(made_v.sem, 1)

            def pair(it, more):
                pool.marked = 0
                for s, src, dst in (("Bm", tok_b, bm), ("Km", tok_k, km)):
                    e.wait_ge(*act.at("T" + s[0], it))
                    for j in J:
                        for t in range(NT):
                            last = e.tensor_tensor(dst[j][:, t, :, :], spread(src[:, t, HD * j:HD * j + HD], CPT),
                                                   core.in_chunk[:, :, :], ALU.mult)
                        pool.mark(last, f"{s}{j}")
                if more:
                    e.wait_ge(*pe.at("TV", it))
                    e.wait_ge(*made_dve.at("BONUS", it))
                    copy_v(it + 1)
                e.wait_ge(*dve.at("Q", it))
                q = row(decay, it)[:, C32:T].rearrange("p (c t) -> p c t", t=C32)
                decays = last_w[:, bass.ds(it, 1), 0:NCH - 1].rearrange("p o c -> p (o c)").unsqueeze(2)
                pool.mark(e.tensor_tensor(q, q, decays.broadcast_to([P, NCH - 1, C32]), ALU.mult), "q_decayed")
                e.wait_ge(*dve.at("Gb", it))
                for half, first in ((0, 1), (1, 0)):
                    g = row(G[half], it).rearrange("p (c k) -> p c k", k=HD)[:, first:, :]
                    before = last_w[:, bass.ds(it, 1), 8 * half + first - 1:8 * half + 7].rearrange("p o c -> p (o c)")
                    last = e.tensor_tensor(g, g, spread(before, HD, 2), ALU.mult)
                pool.mark(last, "G_decayed")

            copy_v(0)
            over_pairs(e, pair)

        @block.tensor
        def _(e):
            def fill(name, it, emit, *needs):
                n = number[name]
                if n >= BANKS:
                    e.wait_ge(*taken(fills[n - BANKS][0], it))
                for need in needs:
                    e.wait_ge(*need)
                pe.mark(emit(bank_of(name)), name)

            def over_tiles(out_cols, operands):
                def emit(b):
                    for t in range(NT):
                        lhsT, rhs = operands(t)
                        last = e.matmul(b[:, t * out_cols:(t + 1) * out_cols], lhsT, rhs, start=True, stop=True)
                    return last
                return emit

            def turn(src):
                def emit(b):
                    for t in range(NT):
                        last = e.transpose(b[:, t * P:(t + 1) * P], src[:, t * P:(t + 1) * P], core.ident[:, :])
                    return last
                return emit

            def head_sums(name, it, ahead, src, need):
                e.wait_ge(*need)
                made_pe.mark(e.matmul(ready_bank[:, :], core.head_ones[:, :], f[src][:, :], start=True, stop=True), name)

            def norm_sums(it, ahead):
                made_pe.marked = 0
                head_sums("NORM", it, ahead, "s1", made_act.at("sq", it, ahead))

            def bonus_sums(it, ahead):
                head_sums("BONUS", it, ahead, "t", made_dve.at("rk", it, ahead))

            def pair(it, more):
                pe.marked = 0
                e.wait_ge(*dve.before(it))
                e.wait_ge(*act.before(it))
                fill("TA", it, turn(ar[:, 0, :]), made_dve.at("ah", it))
                fill("TB", it, turn(f["bh"]), made_dve.at("bh", it))
                fill("TK", it, turn(f["kh"]), made_dve.at("kh", it))
                fill("TV", it, turn(f["v"]), made_v.at(it + 1))
                for j in J:
                    rows = slice(HD * j, HD * j + HD)
                    for s, lhs in (("BA", "bh"), ("M", None), ("KA", "kh")):
                        if s == "M":
                            fill(f"M{j}", it, over_tiles(P, lambda t: (ar[rows, 0, t * P:(t + 1) * P],
                                                                       f["bh"][rows, t * P:(t + 1) * P])))
                            continue
                        for half in range(2):
                            def emit(b):
                                for t in (2 * half, 2 * half + 1):
                                    cols = slice(t * P, (t + 1) * P)
                                    last = e.matmul(b[:, (t % 2) * 2 * P:(t % 2 + 1) * 2 * P].rearrange("p (a f) -> p a f", a=2),
                                                    f[lhs][rows, cols], ar[rows, :, cols], start=True, stop=True)
                                return last
                            fill(f"{s}{'ab'[half]}{j}", it, emit, made_dve.at("rh", it))
                for j in J:
                    fill(f"M2{j}", it, over_tiles(P, lambda t: (ba[j][:, t, 0, :], Ms[j][0][:, t, :])), dve.at(f"M{j}", it))
                    fill(f"T2{j}", it, over_tiles(P, lambda t: (Ms[j][0][:, t, :], ba[j][:, t, 0, :])))
                    fill(f"AV{j}", it, over_tiles(HD, lambda t: (ka[j][:, t, 0, :], tok_v[:, t, HD * j:HD * j + HD])),
                         dve.at(f"KAb{j}", it), act.at("TV", it))
                if more:
                    norm_sums(it, 1)
                for n, power in enumerate((2, 4, 8)):
                    for j in J:
                        now, nxt = Ms[j][(n + 1) % 2], power * 2
                        tn = Ts[j][(n + 1) % 2]
                        t_ready = (dve if power == 2 else act).at(f"T{power}{j}", it)
                        fill(f"M{nxt}{j}", it, over_tiles(P, lambda t: (tn[:, t, :], now[:, t, :])),
                             act.at(f"M{power}{j}", it), t_ready)
                        if nxt < 16:
                            fill(f"T{nxt}{j}", it, over_tiles(P, lambda t: (now[:, t, :], tn[:, t, :])))
                        x_ready = dve.at(f"X{power // 2}{j}" , it)
                        fill(f"X{power}{j}", it, over_tiles(P, lambda t: (now[:, t, :], XT[j][:, t, :])), x_ready)
                for j in J:
                    fill(f"X16{j}", it, over_tiles(P, lambda t: (Ms[j][0][:, t, :], XT[j][:, t, :])),
                         act.at(f"M16{j}", it), dve.at(f"X8{j}", it))
                for j in J:
                    fill(f"P{j}", it, over_tiles(P, lambda t: (XT[j][:, t, :], av[j][:, t, :])),
                         dve.at(f"X16{j}", it), act.at(f"AV{j}", it))

                def q_products(b):
                    for j in J:
                        for t in range(NT):
                            last = e.matmul(b[HD * j:HD * j + HD, t * P:(t + 1) * P], PP[j][:, t, 0:HD], ba[j][:, t, 1, :],
                                            start=True, stop=True)
                    return last
                fill("Q", it, q_products, act.at("P1", it))
                for half in range(2):
                    def emit(b):
                        for j in J:
                            for t in (2 * half, 2 * half + 1):
                                last = e.matmul(b[HD * j:HD * j + HD, (t % 2) * 2 * P:(t % 2 + 1) * 2 * P],
                                                PP[j][:, t, 0:HD], bm[j][:, t, :, :].rearrange("p c k -> p (c k)"),
                                                start=True, stop=True)
                        return last
                    fill(f"G{'ab'[half]}", it, emit, pool.at("Bm1", it))
                for half in range(2):
                    def emit(b):
                        for j in J:
                            for n in range(8 * half, 8 * half + 8):
                                t, ch = n // CPT, n % CPT
                                out = b[HD * j:HD * j + HD, (n % 8) * HD:(n % 8 + 1) * HD]
                                e.matmul(out, bm[j][:, t, ch, :], PP[j][:, t, HD:P], start=True, stop=False)
                                last = e.matmul(out, km[j][:, t, ch, :], tok_v[:, t, HD * j:HD * j + HD],
                                                start=False, stop=True)
                        return last
                    fill(f"F{'ab'[half]}", it, emit, pool.at("Km1", it))

                def outputs(b):
                    for j in J:
                        rows = slice(HD * j, HD * j + HD)
                        for t in range(NT):
                            out = b[rows, t * P:(t + 1) * P]
                            e.matmul(out, PP[j][:, t, HD:P], ba[j][:, t, 1, :], start=True, stop=False)
                            last = e.matmul(out, tok_v[:, t, HD * j:HD * j + HD], ka[j][:, t, 1, :], start=False, stop=True)
                    return last
                fill("Y", it, outputs)
                if more:
                    bonus_sums(it, 1)

            norm_sums(0, 0)
            bonus_sums(0, 0)
            over_pairs(e, pair)

        @block.vector
        def _(e):
            tt, ts, stt = e.tensor_tensor, e.tensor_scalar, e.scalar_tensor_tensor

            def make(name, instruction, *needs):
                for need in needs:
                    e.wait_ge(*need)
                made_dve.mark(instruction(), name)

            def decays(it, ahead):
                n = it + ahead
                made_dve.marked = 0
                k, lw, a = row(rw, n + 4), row(decay, n), row(rate, n)
                make("kk0", lambda: ts(f["kk"][:, :], k, core.v["k_k"][:, bass.ds(n, 1)], None, ALU.mult))
                make("t", lambda: ts(f["k2"][:, :], a, -1.0, core.v["k_a"][:, bass.ds(n, 1)], ALU.add, ALU.mult))
                make("kx", lambda: stt(out=f["k2"][:, :], in0=f["k2"][:, :], scalar=1.0, in1=k, op0=ALU.add, op1=ALU.mult),
                     made_dve.at("t", it, ahead))
                make("scan", lambda: e.tensor_tensor_scan(f["cw"][:, :], core.scan_keep[:, :], lw, 0.0, ALU.mult, ALU.add))
                make("cx", lambda: tt(f["cx"][:, :], f["cw"][:, :], lw, ALU.subtract), made_dve.at("scan", it, ahead))

            def key_norm(it, ahead, step):
                if step == 0:
                    make("last", lambda: e.tensor_copy(last_w[:, bass.ds(it + ahead, 1), :].rearrange("p o c -> p (o c)"),
                                                       f["Ew"][:, C32 - 1:T:C32]), made_act.at("Ew", it, ahead))
                    make("NORM", lambda: ts(f["s2"][:, :], ready_bank[:, :], 1e-24, None, ALU.max),
                         made_pe.at("NORM", it, ahead))
                    e.wait_ge(*made_dve.at("NORM", it, ahead))
                half, name = ((slice(0, T // 2), "rn_a"), (slice(T // 2, T), "rn_b"))[step]
                make(name, lambda: e.reciprocal(f["s2"][:, half], f["s2"][:, half]))

            def key_operands(it, ahead):
                n = it + ahead
                at = lambda s: made_dve.at(s, it, ahead)
                make("kk", lambda: tt(f["kk"][:, :], f["kk"][:, :], f["s2"][:, :], ALU.mult), made_act.at("root", it, ahead))
                if ahead:
                    e.wait_ge(*pe.at("KAb1", it))
                make("ah", lambda: stt(out=ar[:, 0, :], in0=f["kk"][:, :], scalar=-1.0, in1=f["cx"][:, :], op0=ALU.mult,
                                       op1=ALU.mult), made_act.at("Ex", it, ahead), at("kk"))
                make("bb", lambda: tt(f["bb"][:, :], f["kk"][:, :], row(rate, n), ALU.mult), at("kk"))

            def other_operands(it, ahead):
                n = it + ahead
                at = lambda s: made_dve.at(s, it, ahead)
                make("bh", lambda: tt(f["bh"][:, :], f["bb"][:, :], f["En"][:, :], ALU.mult), at("bb"))
                make("kh", lambda: tt(f["kh"][:, :], f["k2"][:, :], f["En"][:, :], ALU.mult), at("kx"))
                make("rk", lambda: stt(out=f["t"][:, :], in0=row(rw, n), scalar=core.v["r_k"][:, bass.ds(n, 1)],
                                       in1=f["k2"][:, :], op0=ALU.mult, op1=ALU.mult))

            def queries(it, ahead):
                if ahead:
                    e.wait_ge(*dve.at("Q", it))
                make("rh", lambda: tt(ar[:, 1, :], row(rw, it + ahead), f["Ew"][:, :], ALU.mult))

            def bonus(it, ahead):
                make("BONUS", lambda: tt(row(o, it + (ahead + o_at)), ready_bank[:, :], f["v"][:, :], ALU.mult),
                     made_pe.at("BONUS", it, ahead), made_v.at(it + (ahead + 1)))

            def pair(it, more):
                dve.marked = 0

                def do(name, instruction, *needs):
                    for need in needs:
                        e.wait_ge(*need)
                    dve.mark(instruction(), name)

                D_, P_ = (lambda s: dve.at(s, it)), (lambda s: pe.at(s, it))
                upper = core.tri[:, 0:2, :]
                for j in J:
                    for s, dst in (("BA", ba), ("M", None), ("KA", ka)):
                        if s == "M":
                            do(f"M{j}", lambda: tt(Ms[j][0][:, :, :], tiles4(f"M{j}"), spread(core.tri[:, 2, :], NT), ALU.mult),
                               P_(f"M{j}"))
                            do(f"X1{j}", lambda: tt(XT[j][:, :, :], ba[j][:, :, 0, :], spread(core.ident[:, :], NT), ALU.add),
                               D_(f"BAb{j}"))
                            continue
                        for half in range(2):
                            name = f"{s}{'ab'[half]}{j}"
                            src = bank_of(name)[:, :].rearrange("p (t f) -> p t f", t=2)
                            do(name, lambda: tt(dst[j][:, 2 * half:2 * half + 2, :, :].rearrange("p t a f -> p t (a f)"), src,
                                                spread(upper.rearrange("p a f -> p (a f)"), 2), ALU.mult), P_(name))
                if more:
                    decays(it, 1)
                for j in J:
                    do(f"T2{j}", lambda: e.tensor_copy(Ts[j][1][:, :, :], tiles4(f"T2{j}")), P_(f"T2{j}"))
                for power in (2, 4, 8, 16):
                    for j in J:
                        do(f"X{power}{j}", lambda: tt(XT[j][:, :, :], XT[j][:, :, :], tiles4(f"X{power}{j}"), ALU.add),
                           P_(f"X{power}{j}"), D_(f"X{power // 2}{j}"))
                    if more and power == 2:
                        key_norm(it, 1, 0)
                        key_norm(it, 1, 1)
                    if more and power == 4:
                        key_operands(it, 1)
                    if more and power == 16:
                        other_operands(it, 1)
                do("Q", lambda: tt(row(decay, it), bank_of("Q")[:, :], ar[:, 1, :], ALU.add), P_("Q"))
                if more:
                    queries(it, 1)
                for half in range(2):
                    name = f"G{'ab'[half]}"
                    do(name, lambda: tt(row(G[half], it).rearrange("p (c k) -> p c k", c=8), bank_of(name)[:, :].rearrange("p (c k) -> p c k", c=8),
                                        spread(core.head_ident[:, :], 8), ALU.add), P_(name))
                if more:
                    bonus(it, 1)

            decays(0, 0)
            key_norm(0, 0, 0)
            key_norm(0, 0, 1)
            key_operands(0, 0)
            other_operands(0, 0)
            queries(0, 0)
            bonus(0, 0)
            over_pairs(e, pair)

        @block.scalar
        def _(e):
            def make(name, instruction, *needs):
                for need in needs:
                    e.wait_ge(*need)
                made_act.mark(instruction(), name)

            def exponentials(it, ahead):
                made_act.marked = 0
                at = lambda s: made_dve.at(s, it, ahead)
                make("sq", lambda: e.activation(f["s1"][:, :], f["kk"][:, :], ACT.Square), at("kk0"))
                make("Ew", lambda: e.activation(f["Ew"][:, :], f["cw"][:, :], ACT.Exp), at("scan"))
                make("En", lambda: e.activation(f["En"][:, :], f["cw"][:, :], ACT.Exp, scale=-1.0))
                make("Ex", lambda: e.activation(f["cx"][:, :], f["cx"][:, :], ACT.Exp), at("cx"))

            def root(it, ahead):
                make("root", lambda: e.activation(f["s2"][:, :], f["s2"][:, :], ACT.Sqrt), made_dve.at("rn_b", it, ahead))

            def pair(it, more):
                act.marked = 0

                def do(name, instruction, *needs):
                    for need in needs:
                        e.wait_ge(*need)
                    act.mark(instruction(), name)

                def copy_tiles(name, dst, *needs):
                    do(name, lambda: e.activation(dst, tiles4(name), ACT.Copy), pe.at(name, it), *needs)

                for j in J:
                    src = tiles4("TA")[:, :, HD * j:HD * j + HD]
                    if j == 0:
                        e.wait_ge(*pe.at("TA", it))
                        e.activation(av[j][:, :, 0:HD], src, ACT.Copy)
                    else:
                        do("TA", lambda: e.activation(av[j][:, :, 0:HD], src, ACT.Copy))
                copy_tiles("TB", tok_b[:, :, :])
                copy_tiles("TK", tok_k[:, :, :])
                copy_tiles("TV", tok_v[:, :, :])
                for j in J:
                    copy_tiles(f"M2{j}", Ms[j][1][:, :, :])
                    do(f"AV{j}", lambda: e.activation(av[j][:, :, HD:P], bank_of(f"AV{j}")[:, 0:NT * HD].rearrange(
                        "p (t f) -> p t f", t=NT), ACT.Copy), pe.at(f"AV{j}", it))
                if more:
                    exponentials(it, 1)
                for n, power in enumerate((4, 8)):
                    for j in J:
                        copy_tiles(f"M{power}{j}", Ms[j][n % 2][:, :, :])
                        copy_tiles(f"T{power}{j}", Ts[j][n % 2][:, :, :])
                    if more and power == 4:
                        root(it, 1)
                for j in J:
                    copy_tiles(f"M16{j}", Ms[j][0][:, :, :])
                for j in J:
                    copy_tiles(f"P{j}", PP[j][:, :, :])
                for half in range(2):
                    name = f"F{'ab'[half]}"
                    do(name, lambda: e.activation(row(F[half], it), bank_of(name)[:, :], ACT.Copy), pe.at(name, it))
                do("Y", lambda: e.activation(row(rw, it), bank_of("Y")[:, :], ACT.Copy), pe.at("Y", it))

            exponentials(0, 0)
            root(0, 0)
            over_pairs(e, pair)
    for name, r in (("rw_dve", dve), ("rw_act", act), ("rw_pe", pe), ("rw_pool", pool), ("rw_made_dve", made_dve),
                    ("rw_made_act", made_act), ("rw_made_pe", made_pe)):
        assert r.marked == len(r.names)
        core.ended(**{name: PAIRS4 * len(r.names)})
    core.ended(rw_made_v=PAIRS4)


def rwkv_states_stage(core, y, q, bonus, gate, G, S, g, b):
    nc = core.nc
    J, PAIRS4, HALVES = range(2), 4, range(2)
    pairs = range(PAIRS4)
    dve_names = ([f"S{h}_{n}" for n in range(1, NCH - 1) for h in HALVES] + [f"y{p}" for p in pairs] +
                 [f"yc{p}" for p in pairs] + ["var", "inverse"] + [f"{s}{p}" for p in pairs for s in ("yg", "yb")] +
                 [f"out{p}" for p in pairs])
    pe_names = ([f"S{h}_{n}" for n in range(1, NCH - 1) for h in HALVES] + ["Y"] + [f"mu{p}" for p in pairs] +
                ["var"] + [f"root{p}" for p in pairs])
    with ExitStack() as c:
        squares = core.sb(c, "rws_squares", [P, PAIRS4, T])
        stat = core.sb(c, "rws_stat", [P, 3, T])
        step_bank = [core.ps(c, f"rws_step{n}", [P, 2, 2, HD]) for n in HALVES]
        y_bank = [core.ps(c, f"rws_y{p}", [P, T]) for p in pairs]
        stat_bank = core.ps(c, "rws_stat_bank", [P, T])
        dve, pe = Results(core.sig("rws_dve"), dve_names), Results(core.sig("rws_pe"), pe_names)
        act = Results(core.sig("rws_act"), [f"sq{p}" for p in pairs] + ["root"])
        block = c.enter_context(nc.Block())

        def of_chunk(parts, rows, pair, n):
            return parts[n // 8][rows, pair, n % 8 * HD:(n % 8 + 1) * HD]

        @block.tensor
        def _(e):
            for n in range(1, NCH):
                for half in HALVES:
                    if n > 1:
                        e.wait_ge(*dve.at(f"S{half}_{n - 1}"))
                    if n < NCH - 1:
                        for i in range(2):
                            for j in J:
                                rows = slice(HD * j, HD * j + HD)
                                last = e.matmul(step_bank[half][rows, n % 2, i, :], of_chunk(G, rows, 2 * half + i, n),
                                                of_chunk(S, rows, 2 * half + i, n - 1), start=True, stop=True)
                        pe.mark(last, f"S{half}_{n}")
                    cols = slice(n * C32, (n + 1) * C32)
                    for i in range(2):
                        for j in J:
                            rows = slice(HD * j, HD * j + HD)
                            p = 2 * half + i
                            last = e.matmul(y_bank[p][rows, cols], of_chunk(S, rows, p, n - 1), q[rows, p, cols],
                                            start=True, stop=True)
            pe.mark(last, "Y")
            for p in pairs:
                e.wait_ge(*dve.at(f"y{p}"))
                pe.mark(e.matmul(y_bank[p][:, :], core.head_ones[:, :], y[:, p, :], start=True, stop=True), f"mu{p}")
            for p in pairs:
                e.wait_ge(*act.at(f"sq{p}"))
                last = e.matmul(stat_bank[32 * p:32 * p + 32, :], core.head_ones[:, 3 * HD // 4:5 * HD // 4],
                                squares[:, p, :], start=True, stop=True)
            pe.mark(last, "var")
            e.wait_ge(*act.at("root"))
            for p in pairs:
                pe.mark(e.matmul(y_bank[p][:, :], core.pick_pair_head[:, p, :], stat[:, 2, :], start=True, stop=True), f"root{p}")

        @block.vector
        def _(e):
            for n in range(1, NCH - 1):
                for half in HALVES:
                    e.wait_ge(*pe.at(f"S{half}_{n}"))
                    s = of_chunk(S, slice(0, P), slice(2 * half, 2 * half + 2), n)
                    dve.mark(e.tensor_tensor(s, s, step_bank[half][:, n % 2, :, :], ALU.add), f"S{half}_{n}")
            e.wait_ge(*pe.at("Y"))
            for p in pairs:
                dve.mark(e.tensor_tensor(y[:, p, C32:T], y[:, p, C32:T], y_bank[p][:, C32:T], ALU.add), f"y{p}")
            for p in pairs:
                e.wait_ge(*pe.at(f"mu{p}"))
                dve.mark(e.scalar_tensor_tensor(out=y[:, p, :], in0=y_bank[p][:, :], scalar=-1.0 / HD, in1=y[:, p, :],
                                                op0=ALU.mult, op1=ALU.add), f"yc{p}")
            e.wait_ge(*pe.at("var"))
            dve.mark(e.tensor_scalar(stat[:, 0, :], stat_bank[:, :], 1.0 / HD, RW_GN_EPS, ALU.mult, ALU.add), "var")
            e.wait_ge(*dve.at("var"))
            dve.mark(e.reciprocal(stat[:, 1, :], stat[:, 0, :]), "inverse")
            for p in pairs:
                e.wait_ge(*pe.at(f"root{p}"))
                dve.mark(e.scalar_tensor_tensor(out=y[:, p, :], in0=y[:, p, :], scalar=g[:, p:p + 1], in1=y_bank[p][:, :],
                                                op0=ALU.mult, op1=ALU.mult), f"yg{p}")
                e.wait_ge(*dve.at(f"yg{p}"))
                dve.mark(e.scalar_tensor_tensor(out=y[:, p, :], in0=y[:, p, :], scalar=b[:, p:p + 1], in1=bonus[:, p, :],
                                                op0=ALU.add, op1=ALU.add), f"yb{p}")
            for p in pairs:
                e.wait_ge(*dve.at(f"yb{p}"))
                dve.mark(e.tensor_tensor(bonus[:, p, :], y[:, p, :], gate[:, p, :], ALU.mult), f"out{p}")

        @block.scalar
        def _(e):
            for p in pairs:
                e.wait_ge(*dve.at(f"yc{p}"))
                act.mark(e.activation(squares[:, p, :], y[:, p, :], ACT.Square), f"sq{p}")
            e.wait_ge(*dve.at("inverse"))
            act.mark(e.activation(stat[:, 2, :], stat[:, 1, :], ACT.Sqrt), "root")
    core.ended(rws_dve=len(dve_names), rws_pe=len(pe_names), rws_act=PAIRS4 + 1)

def transformer_program(nc, A, out):
    with ExitStack() as ctx:
        core = Core(nc, ctx)
        scratch = nc.dram_tensor("rel_scratch", (8, EXTENDED), F32, kind="Internal").ap()
        constants_stage(core, A)
        first_block(core, A, scratch)
        even_layer(core, A)
        odd_layer(core, A)
        output_stage(core, core.x, out)


def output_stage(core, src, out):
    nc = core.nc
    with ExitStack() as c:
        rows = core.sb(c, "out_rows", [P, 2, D])
        bank = [core.ps(c, f"out_bank{b}", [P, T]) for b in range(4)]
        turned, copied, stored = core.sig("out_turned"), core.sig("out_copied"), core.sig("out_stored")
        block = c.enter_context(nc.Block())
        out_v = out[0].rearrange("(t p) d -> t p d", p=P)
        halves = [(t, h) for t in range(NT) for h in range(2)]

        @block.tensor
        def _(e):
            for n, (t, h) in enumerate(halves):
                if n >= 4:
                    e.wait_ge(*copied.at(n - 3))
                for k in range(4):
                    last = e.transpose(bank[n % 4][:, k * P:(k + 1) * P], src[:, 4 * h + k, t * P:(t + 1) * P],
                                       core.ident[:, :])
                last.then_inc(turned.sem, 1)

        @block.scalar
        def _(e):
            for n, (t, h) in enumerate(halves):
                e.wait_ge(*turned.at(n + 1))
                if t >= 2:
                    e.wait_ge(*stored.at(16 * (t - 1)))
                e.activation(rows[:, t % 2, h * T:(h + 1) * T], bank[n % 4][:, :], ACT.Copy).then_inc(copied.sem, 1)

        @block.sync
        def _(e):
            for t in range(NT):
                e.wait_ge(*copied.at(2 * t + 2))
                if t >= 1:
                    e.wait_ge(*stored.at(16 * t))
                e.dma_start(out_v[t], rows[:, t % 2, :]).then_inc(stored.sem, 16)
            e.wait_ge(*stored.at(16 * NT))
    core.ended(out_turned=2 * NT, out_copied=2 * NT, out_stored=16 * NT)


def first_block(core, A, scratch):
    w_in = A["w_in"][0]
    fox, width = 0, 4 * P
    chk = 3 * width + 8
    gate = chk + 3 * width
    with ExitStack() as c:
        o = core.sb(c, "o", [P, 2 * 4, T])
        activations(core, c)
        with ExitStack() as a:
            qkv, qkv_chk = (core.sb(a, s, [P, 12, T]) for s in ("qkv", "qkv_chk"))
            with ExitStack() as f:
                fa = core.sb(f, "fa", [P, 1, T])
                linear(core, [
                    Job(6, columns(w_in, fox), act_tiles(core), keep(qkv)),
                    Job(1, columns(w_in, 3 * width), act_tiles(core), keep(fa, 1), tiles=1),
                    Job(6, columns(w_in, chk), act_tiles(core), keep(qkv_chk))],
                    lambda gemm: norm_stage(core, "rms", core.x, KD, g=core.v["norm1"], eps=1e-6, gemm=gemm))
                qs, ks = wide_operands(core, f)
                forget_stage(core, fa[:, 0, :], A["forget_bias"], qs, ks)
                attention(core, qkv, o, 0, mask=core.causal_mask, placed=(qs, ks))
            with ExitStack() as f:
                near = core.sb(f, "near", [P, 8, WINDOW])
                qs, ks = wide_operands(core, f)
                relative_stage(core, A["rel_bias"], scratch, core.chunk_mask, near, qs, ks)
                attention(core, qkv_chk, o, 4, near=near, placed=(qs, ks))
        gates = core.sb(c, "gates", [P, 2 * KD, T])
        linear(core, [Job(KD, columns(w_in, gate), act_tiles(core), keep_sigmoid(gates))])
        views = [A[n][0].rearrange("(k p) n -> p k n", p=P) for n in ("w_branch_a", "w_branch_b")]
        linear(core, [Job(KD, lambda u, s, t: views[t][:, :, bass.ds(u * P, P)],
                              lambda s, t, k: (core.AH[:, 4 * t + k, :], core.AL[:, 4 * t + k, :]),
                              gated_sum(core, gates), subs=(4,))],
               split=o)
        linear(core, [Job(4, columns(A["w_out"][0], 0), act_tiles(core), residual(core))],
               split=gates)
    with ExitStack() as c:
        activations(core, c)
        tiles = FFN1 // P // 2
        hid_hi = core.sb(c, "hid_hi", [P, tiles, T], F32R)
        hid_lo = core.sb(c, "hid_lo", [P, tiles, T], F32R)
        w_up, w_down = A["w_up"][0], A["w_down"][0]
        jobs = []
        for half in range(2):
            jobs.append(Job(tiles // 2, columns(w_up, half * tiles * P), act_tiles(core),
                            relu_squared(core, hid_hi, hid_lo)))
            jobs.append(Job(4, columns(w_down[half * tiles * P:(half + 1) * tiles * P], 0),
                            lambda s, t, k: (hid_hi[:, KD * s + k, :], hid_lo[:, KD * s + k, :]),
                            residual(core), subs=(KD, KD), after=2))
        linear(core, jobs, lambda gemm: norm_stage(core, "rms", core.x, KD, g=core.v["norm2"], eps=1e-6, gemm=gemm))
        norm_stage(core, "rms", core.x, KD, out32=core.x, g=core.v["final"], eps=1e-6, parts=False)


def swiglu_stage(core, A, layer):
    half_tiles = FFN2 // P // 2
    with ExitStack() as c:
        hid_hi = core.sb(c, "hid_hi", [P, half_tiles, T], F32R)
        hid_lo = core.sb(c, "hid_lo", [P, half_tiles, T], F32R)
        w_up, w_down = A["ffn_w_gate_up_2"][layer], A["ffn_w_down_2"][layer]
        jobs = []
        for half in range(2):
            first = half * half_tiles * P
            jobs.append(Job(half_tiles, columns(w_up, first, tile_step=FFN2, unit_step=P), act_tiles(core),
                            silu_times(core, hid_hi, hid_lo)))
            jobs.append(Job(4, columns(w_down[first:first + half_tiles * P], 0),
                            lambda s, t, k: (hid_hi[:, KD * s + k, :], hid_lo[:, KD * s + k, :]),
                            residual(core, DN_ALPHA if half == 0 else 1.0), subs=(KD, half_tiles - KD), after=1))
        linear(core, jobs, lambda gemm: post_norm(core, layer, 0, True, gemm))


def post_norm(core, layer, half, parts, gemm=None):
    norm_stage(core, "ln", core.x, KD, out32=core.x, g=core.v[f"ln_g{layer}{half}"], b=core.v[f"ln_b{layer}{half}"],
               eps=1e-5, parts=parts, gemm=gemm)


def mix_out_and_ffn(core, A, layer, o, w_out):
    with ExitStack() as c:
        activations(core, c)
        linear(core, [Job(4, columns(w_out, 0), act_tiles(core), residual(core, DN_ALPHA))],
               split=o)
        swiglu_stage(core, A, layer)
        post_norm(core, layer, 1, False)


def even_layer(core, A):
    w_in = A["even_w_in_2"][0]
    with ExitStack() as c:
        o = core.sb(c, "o", [P, KD, T])
        with ExitStack() as r:
            gla = core.sb(r, "gla", [P, 12, T])
            glr = core.sb(r, "glr", [P, 1, T])
            with ExitStack() as g:
                activations(core, g)
                linear(core, [Job(6, columns(w_in, 0), act_tiles(core), keep(gla)),
                              Job(1, columns(w_in, 12 * P), act_tiles(core), keep(glr, 1), tiles=1)],
                       split=core.x)
            gla_stage(core, A, gla, glr[:, 0, :], o)
        with ExitStack() as r:
            rw = core.sb(r, "rw", [P, 15, T])
            decay, rate, gate = (core.sb(r, f"rw_{s}", [P, 4, T]) for s in ("decay", "rate", "gate"))
            with ExitStack() as g:
                activations(core, g)
                linear(core, [Job(7, columns(w_in, GLA_IN), act_tiles(core),
                                  keep_shifted(core, rw, core.v["mu"])),
                                  Job(1, columns(w_in, GLA_IN + RW_IN - P), act_tiles(core), 
                                  keep_shifted(core, rw[:, 14:15, :], core.v["mu_tail"], 1),
                                      tiles=1)],
                       split=core.x)
            rwkv_prepare_stage(core, A, rw, decay, rate, gate)
            G = [rw[:, 8:12, :], core.sb(r, "rw_G_second", [P, 4, T])]
            F = [rw[:, 4:8, :], rate]
            rwkv_chunks_stage(core, rw, decay, rate, o, 4, G, F)
            rwkv_states_stage(core, rw[:, 0:4, :], decay, o[:, 4:8, :], gate, G, F, core.v["rln_g"], core.v["rln_b"])
        mix_out_and_ffn(core, A, 0, o, A["even_w_out_2"][0])


MLA_H, MLA_Q, MLA_KV, ROPE = 16, 768, 256, 32
TWO_PI = (6.28125, 8117 / 4194304, 6.283185307179586 - 6.28125 - 8117 / 4194304)
ROUND = 1.5 * 2 ** 23
PI_IN = 3.1415925


def rope_stage(core, A, qr, k_pe):
    nc = core.nc
    tiles = [qr[:, n, :] for n in range(4)] + [k_pe]
    dve_names = (["pos", "ang", "n", "n2", "r1", "r2", "r3", "c", "over", "c2", "sin_in", "cos_in"] +
                 [f"{s}{n}" for n in range(5) for s in ("sin", "cos", "sum")])
    with ExitStack() as c:
        pos_i = core.sb(c, "pos_i", [P, T], I32)
        freq = core.sb(c, "freq", [P, 1])
        ang, turns, cosine, over, sine = (core.sb(c, f"rope_{s}", [P, T]) for s in ("ang", "n", "cos", "over", "sin"))
        parts = core.sb(c, "rope_parts", [P, 2, T])
        swap = core.sb(c, "rope_swap", [P, P])
        bank = [core.ps(c, f"rope_bank{n}", [P, T]) for n in range(5)]
        loaded, swapped, built, table = (core.sig(f"rope_{s}") for s in ("loaded", "swapped", "built", "table"))
        dve = Results(core.sig("rope_dve"), dve_names)
        block = c.enter_context(nc.Block())

        @block.sync
        def _(e):
            e.dma_start(pos_i[:, :], A["positions_2"][0].partition_broadcast(P)).then_inc(loaded.sem, 16)
            e.dma_start(freq[:, :], A["rope_freq"]).then_inc(loaded.sem, 16)

        @block.gpsimd
        def _(e):
            chain = Chain(e, built)
            chain.link(e.memset(swap[:, :], 0.0))
            pairs = swap[:, :].rearrange("p (i two) -> p two i", two=2)
            for two, value in ((1, 1.0), (0, -1.0)):
                chain.link(e.affine_select(out=pairs[:, two, :], in_=pairs[:, two, :], compare_op=ALU.not_equal,
                                           fill=value, base=two - 1, pattern=[[-2, P // 2]], channel_multiplier=1))

        @block.tensor
        def _(e):
            e.wait_ge(*built.at(3))
            for n, x in enumerate(tiles):
                e.matmul(bank[n][:, :], swap[:, :], x, start=True, stop=True).then_inc(swapped.sem, 1)

        @block.scalar
        def _(e):
            e.wait_ge(*dve.at("cos_in"))
            e.activation(sine[:, :], ang[:, :], ACT.Sin).then_inc(table.sem, 1)
            e.activation(cosine[:, :], cosine[:, :], ACT.Sin).then_inc(table.sem, 1)

        @block.vector
        def _(e):
            def do(name, instruction):
                dve.mark(instruction, name)
                e.wait_ge(*dve.at(name))
            ts, tt, stt = e.tensor_scalar, e.tensor_tensor, e.scalar_tensor_tensor
            e.wait_ge(*loaded.at(32))
            do("pos", e.tensor_copy(ang[:, :], pos_i[:, :]))
            do("ang", ts(ang[:, :], ang[:, :], freq[:, 0:1], None, ALU.mult))
            do("n", ts(turns[:, :], ang[:, :], 1.0 / (2 * np.pi), ROUND, ALU.mult, ALU.add))
            do("n2", ts(turns[:, :], turns[:, :], -ROUND, None, ALU.add))
            for n in range(3):
                do(f"r{n + 1}", stt(out=ang[:, :], in0=turns[:, :], scalar=-TWO_PI[n], in1=ang[:, :], op0=ALU.mult,
                                    op1=ALU.add))
            do("c", ts(cosine[:, :], ang[:, :], np.pi / 2, None, ALU.add))
            do("over", ts(over[:, :], cosine[:, :], np.pi, None, ALU.is_gt))
            do("c2", stt(out=cosine[:, :], in0=over[:, :], scalar=-2 * np.pi, in1=cosine[:, :], op0=ALU.mult, op1=ALU.add))
            do("sin_in", ts(ang[:, :], ang[:, :], PI_IN, -PI_IN, ALU.min, ALU.max))
            do("cos_in", ts(cosine[:, :], cosine[:, :], PI_IN, -PI_IN, ALU.min, ALU.max))
            e.wait_ge(*table.at(2))
            for n, x in enumerate(tiles):
                e.wait_ge(*swapped.at(n + 1))
                do(f"sin{n}", tt(parts[:, 0, :], bank[n][:, :], sine[:, :], ALU.mult))
                do(f"cos{n}", tt(parts[:, 1, :], x, cosine[:, :], ALU.mult))
                do(f"sum{n}", tt(x, parts[:, 0, :], parts[:, 1, :], ALU.add))
    core.ended(rope_loaded=32, rope_built=3, rope_swapped=5, rope_table=2, rope_dve=len(dve_names))


def head_columns(w, first, width):
    heads = P // width
    return lambda u, s, t, i: w[:, :, bass.ds(u * 2 * heads + (t * heads + i), 1), first:first + width]\
        .rearrange("p k o n -> p k (o n)")


def odd_layer(core, A):
    w_in = A["mla_w_in_2"][0].rearrange("(k p) n -> p k n", p=P)
    q_b = A["mla_w_q_b_2"][0].rearrange("(k p) (h n) -> p k h n", p=P, h=MLA_H)
    kv_b = A["mla_w_kv_b_2"][0].rearrange("(k p) (h n) -> p k h n", p=P, h=MLA_H)
    with ExitStack() as c:
        o = core.sb(c, "o", [P, KD, T])
        with ExitStack() as r:
            qn, kn, v = (core.sb(r, f"mla_{s}", [P, KD, T]) for s in ("qn", "kn", "v"))
            qr = core.sb(r, "mla_qr", [P, 4, T])
            k_pe = core.sb(r, "mla_k_pe", [P, 1, T])
            with ExitStack() as g:
                activations(core, g)
                linear(core, [Job(4, columns(A["mla_w_in_2"][0], 0), act_tiles(core), keep(o)),
                                  Job(1, lambda u, s, t, i: w_in[:, :, MLA_Q + MLA_KV:], act_tiles(core),
                                      keep(k_pe, 1), tiles=1, pieces=4)],
                       split=core.x)
                norm_stage(core, "rms", o[:, 6:8, :], 2, at=6, g=core.v["kv_g"], eps=1e-6, features=MLA_KV)
                linear(core, [
                    Job(4, head_columns(q_b, 0, HD), act_tiles(core), keep(qn), subs=(6,), pieces=2),
                    Job(2, head_columns(q_b, HD, ROPE), act_tiles(core), keep(qr), subs=(6,), pieces=4),
                    Job(4, head_columns(kv_b, 0, HD), act_tiles(core, 6), keep(kn), subs=(2,), pieces=2),
                    Job(4, head_columns(kv_b, HD, HD), act_tiles(core, 6), keep(v), subs=(2,), pieces=2)],
                    lambda gemm: norm_stage(core, "rms", o[:, 0:6, :], 6, g=core.v["q_g"], eps=1e-6, features=MLA_Q,
                                            gemm=gemm))
            rope_stage(core, A, qr, k_pe[:, 0, :])

            attention_stage(core, 2, two_tiles(qn), two_tiles(kn), two_tiles(v), one_tile(o), (HD + ROPE) ** -0.5,
                            core.chunk_mask, rope=(one_tile(qr), k_pe[HD:HD + ROPE, 0, :]))
        mix_out_and_ffn(core, A, 1, o, A["mla_w_out_2"][0])


def one_tile(x, at=0):
    return lambda n: x[:, bass.ds(n + at, 1), :].rearrange("p o t -> p (o t)")


def two_tiles(x, at=0):
    return lambda n: x[:, bass.ds(n * 2 + at, 2), :]


def attention(core, qkv, o, o_at, **kinds):
    attention_stage(core, 1, two_tiles(qkv), two_tiles(qkv, 4), two_tiles(qkv, 8), one_tile(o, o_at), HD ** -0.5, **kinds)



def kernel(**inputs):
    import numpy as _np
    import concourse.bacc as _bacc
    from concourse import mybir as _mybir
    from concourse.bass_utils import run_bass_kernel_spmd as _run

    nc = _bacc.Bacc("TRN2", target_bir_lowering=False, num_devices=1)
    arrays, aps = {}, {}
    for name in inputs:
        a = _np.ascontiguousarray(inputs[name])
        arrays[f"in_{name}"] = a
        aps[name] = nc.dram_tensor(f"in_{name}", a.shape, _mybir.dt.from_np(a.dtype), kind="ExternalInput").ap()
    arrays["in_rope_freq"] = _np.array([[10000.0 ** -(p % ROPE // 2 * 2 / ROPE)] for p in range(P)], _np.float32)
    aps["rope_freq"] = nc.dram_tensor("in_rope_freq", (P, 1), F32, kind="ExternalInput").ap()
    out = nc.dram_tensor("out_x", (1, T, D), F32, kind="ExternalOutput").ap()
    transformer_program(nc, aps, out)
    return _run(nc, [arrays], core_ids=[0]).results[0]["out_x"]
```
